# Optimizing a Trainium2 kernel written in Bass

```python
import math
import jax, jax.numpy as jnp
from jax import lax
import numpy as np
import jax
import jax.numpy as jnp

D_MODEL = 1024
BATCH = 1
SEQ = 512
DEPTH = 1

CHUNK = 64
N_META = 16
Q_BLOCK = 128
HEAD_DIM = 64
ROPE_DIM = HEAD_DIM // 4
ROPE_THETA = 500000.0
SB_HEADS = 8
DSA_HEADS = 8
KV_LATENT = 128
NOPE_DIM = HEAD_DIM - ROPE_DIM
IDX_HEADS = 8
IDX_DIM = 64
TOPK_MAX = 256
N_GROUPS = 4
EXP_PER_GROUP = 8
N_EXPERTS = N_GROUPS * EXP_PER_GROUP
TOP_E = 2
D_EXPERT = 512
EXPERT_BLOCK = 128
NORM_EPS = 1e-6
SB_W = SB_HEADS * HEAD_DIM
DSA_W = DSA_HEADS * HEAD_DIM
SPLITS = (SB_W, SB_W, SB_W, DSA_W, KV_LATENT, ROPE_DIM, IDX_HEADS * IDX_DIM, IDX_DIM, IDX_HEADS, D_MODEL, D_MODEL)
IN_WIDTH = 3 * SB_W + DSA_W + KV_LATENT + ROPE_DIM + IDX_HEADS * IDX_DIM + IDX_DIM + IDX_HEADS + 2 * D_MODEL


def rmsnorm(x, g):
    xf = x.astype(jnp.float32)
    y = xf * lax.rsqrt(jnp.mean(xf * xf, axis=-1, keepdims=True) + NORM_EPS)
    return (y * g.astype(jnp.float32)).astype(x.dtype)

def partial_rope(x, pos):
    half = ROPE_DIM // 2
    inv = ROPE_THETA ** (-jnp.arange(half, dtype=jnp.float32) / half)
    ang = pos.astype(jnp.float32)[:, None] * inv[None, :]
    cos = jnp.cos(ang)[None, :, None, :]
    sin = jnp.sin(ang)[None, :, None, :]
    x1 = x[..., :half].astype(jnp.float32)
    x2 = x[..., half:ROPE_DIM].astype(jnp.float32)
    rot = jnp.concatenate([x1 * cos - x2 * sin, x2 * cos + x1 * sin], axis=-1).astype(x.dtype)
    return jnp.concatenate([rot, x[..., ROPE_DIM:]], axis=-1)

def chunk_ids(pos):
    return jnp.where(pos < N_META, 0, 1 + (pos - N_META) // CHUNK)

def to_blocks(a, t_pad):
    b, t = a.shape[0], a.shape[1]
    pad = [(0, 0), (0, t_pad - t)] + [(0, 0)] * (a.ndim - 2)
    a = jnp.pad(a, pad).reshape((b, t_pad // Q_BLOCK, Q_BLOCK) + a.shape[2:])
    return jnp.moveaxis(a, 1, 0)

def from_blocks(a, t):
    a = jnp.moveaxis(a, 0, 1)
    return a.reshape((a.shape[0], a.shape[1] * a.shape[2]) + a.shape[3:])[:, :t]

def stick_breaking(q, k, v, pos):
    t = q.shape[1]
    t_pad = -(-t // Q_BLOCK) * Q_BLOCK
    scale = 1.0 / math.sqrt(HEAD_DIM)
    qpos = jnp.arange(t_pad).reshape(t_pad // Q_BLOCK, Q_BLOCK)

    def block(args):
        qb, qp = args
        z = jnp.einsum('bqhd,bkhd->bhqk', qb, k).astype(jnp.float32) * scale
        strict = pos[None, :] < qp[:, None]
        log_keep = jnp.where(strict, jax.nn.log_sigmoid(-z), 0.0)
        later = lax.cumsum(log_keep, axis=3, reverse=True) - log_keep
        a = jnp.where(strict, jnp.exp(jax.nn.log_sigmoid(z) + later), 0.0)
        return jnp.einsum('bhqk,bkhd->bqhd', a.astype(v.dtype), v)

    out = lax.map(block, (to_blocks(q, t_pad), qpos))
    return from_blocks(out, t)

def dsa_attention(q_full, kv_all, q_idx, w_idx, k_idx, pos, topk):
    t = q_full.shape[1]
    t_pad = -(-t // Q_BLOCK) * Q_BLOCK
    scale = 1.0 / math.sqrt(HEAD_DIM)
    cid = chunk_ids(pos)
    qcid = chunk_ids(jnp.arange(t_pad)).reshape(t_pad // Q_BLOCK, Q_BLOCK)

    def block(args):
        qf, qi, wi, qc = args
        s_idx = jax.nn.relu(jnp.einsum('bqhd,bkd->bqhk', qi, k_idx))
        score = jnp.einsum('bqh,bqhk->bqk', wi, s_idx).astype(jnp.float32)
        adm = cid[None, :] <= qc[:, None]
        score = jnp.where(adm[None], score, -jnp.inf)
        _, sel = lax.top_k(score, topk)
        valid = cid[sel] <= qc[None, :, None]
        kv_sel = jax.vmap(lambda kv, i: kv[i])(kv_all, sel)
        logits = jnp.einsum('bqhc,bqkc->bqhk', qf, kv_sel).astype(jnp.float32) * scale
        logits = jnp.where(valid[:, :, None, :], logits, -1e30)
        p = jax.nn.softmax(logits, axis=-1)
        return jnp.einsum('bqhk,bqkc->bqhc', p.astype(kv_sel.dtype), kv_sel[..., ROPE_DIM:])

    out = lax.map(block, (to_blocks(q_full, t_pad), to_blocks(q_idx, t_pad), to_blocks(w_idx, t_pad), qcid))
    return from_blocks(out, t)

def mixer(u, w_in, w_uk, w_uv, w_up_a, w_up_b, w_o, pos, topk):
    b, t, _ = u.shape
    proj = u @ w_in
    qa, ka, va, qb, ckv, krope, qi, ki, wi, ga, gb = jnp.split(proj, list(np.cumsum(SPLITS)[:-1]), axis=-1)
    y_a = stick_breaking(qa.reshape(b, t, SB_HEADS, HEAD_DIM), ka.reshape(b, t, SB_HEADS, HEAD_DIM),
                         va.reshape(b, t, SB_HEADS, HEAD_DIM), pos).reshape(b, t, SB_W)
    qb = partial_rope(qb.reshape(b, t, DSA_HEADS, HEAD_DIM), pos)
    q_lat = jnp.einsum('bthn,hcn->bthc', qb[..., ROPE_DIM:], w_uk)
    q_full = jnp.concatenate([qb[..., :ROPE_DIM], q_lat], axis=-1)
    krope = partial_rope(krope[:, :, None, :], pos)[:, :, 0]
    kv_all = jnp.concatenate([krope, ckv], axis=-1)
    qi = partial_rope(qi.reshape(b, t, IDX_HEADS, IDX_DIM), pos)
    ki = partial_rope(ki[:, :, None, :], pos)[:, :, 0]
    o_lat = dsa_attention(q_full, kv_all, qi, wi, ki, pos, topk)
    y_b = jnp.einsum('bthc,hcd->bthd', o_lat, w_uv).reshape(b, t, DSA_W)
    z = jax.nn.sigmoid(ga) * (y_a @ w_up_a) + jax.nn.sigmoid(gb) * (y_b @ w_up_b)
    return z @ w_o

def hier_moe(u, w_group, b_group, w_router, b_router, w1, w3, w2):
    n, d = u.shape
    g_logits = (u @ w_group).astype(jnp.float32) + b_group.astype(jnp.float32)
    g_prob = jax.nn.softmax(g_logits, axis=-1)
    p_grp, g_sel = lax.top_k(g_prob, 1)
    e_logits = ((u @ w_router).astype(jnp.float32) + b_router.astype(jnp.float32)).reshape(n, N_GROUPS, EXP_PER_GROUP)
    gidx = jnp.broadcast_to(g_sel[:, :, None], (n, 1, EXP_PER_GROUP))
    in_grp = jnp.take_along_axis(e_logits, gidx, axis=1)[:, 0]
    e_prob = jax.nn.softmax(in_grp, axis=-1)
    p_exp, e_sel = lax.top_k(e_prob, TOP_E)
    gate = p_grp * p_exp / jnp.sum(p_exp, axis=-1, keepdims=True)
    expert = g_sel * EXP_PER_GROUP + e_sel
    m = n * TOP_E
    e_flat = expert.reshape(m).astype(jnp.int32)
    tok = jnp.repeat(jnp.arange(n, dtype=jnp.int32), TOP_E)
    w_flat = gate.reshape(m)
    order = jnp.argsort(e_flat)
    e_s = e_flat[order]
    counts = jnp.zeros((N_EXPERTS,), jnp.int32).at[e_flat].add(1)
    padded = (counts + EXPERT_BLOCK - 1) // EXPERT_BLOCK * EXPERT_BLOCK
    p_end = jnp.cumsum(padded)
    p_start = p_end - padded
    start = jnp.cumsum(counts) - counts
    dest = p_start[e_s] + jnp.arange(m, dtype=jnp.int32) - start[e_s]
    n_blk = -(-m // EXPERT_BLOCK) + N_EXPERTS
    p_tot = n_blk * EXPERT_BLOCK
    buf_tok = jnp.full((p_tot,), n, jnp.int32).at[dest].set(tok[order])
    buf_w = jnp.zeros((p_tot,), jnp.float32).at[dest].set(w_flat[order])
    blk_e = jnp.minimum(jnp.searchsorted(p_end, jnp.arange(n_blk, dtype=jnp.int32) * EXPERT_BLOCK, side='right'), N_EXPERTS - 1)
    u_pad = jnp.concatenate([u, jnp.zeros((1, d), u.dtype)], axis=0)
    xb = u_pad[buf_tok].reshape(n_blk, EXPERT_BLOCK, d)

    def expert_block(args):
        xe, e = args
        hid = jax.nn.silu(xe @ w1[e]) * (xe @ w3[e])
        return hid @ w2[e]

    yb = lax.map(expert_block, (xb, blk_e)).reshape(p_tot, d)
    out = jnp.zeros((n + 1, d), u.dtype).at[buf_tok].add(yb * buf_w[:, None].astype(yb.dtype))
    return out[:n]

def first_inputs(seed: int = 0) -> dict:
    key = jax.random.key(seed)
    ks = jax.random.split(key, 20)
    f32 = jnp.float32
    nrm = lambda k, shape, s: jax.random.normal(k, shape, f32) * s
    return {
        "x": nrm(ks[0], (BATCH, SEQ, D_MODEL), 1.0),
        "meta_tokens": nrm(ks[1], (N_META, D_MODEL), 1.0),
        "norm_mix_g": 1.0 + nrm(ks[2], (DEPTH, D_MODEL), 0.02),
        "w_in": nrm(ks[3], (DEPTH, D_MODEL, IN_WIDTH), D_MODEL ** -0.5),
        "w_uk": nrm(ks[4], (DEPTH, DSA_HEADS, KV_LATENT, NOPE_DIM), KV_LATENT ** -0.5),
        "w_uv": nrm(ks[5], (DEPTH, DSA_HEADS, KV_LATENT, HEAD_DIM), KV_LATENT ** -0.5),
        "w_up_a": nrm(ks[6], (DEPTH, SB_W, D_MODEL), SB_W ** -0.5),
        "w_up_b": nrm(ks[7], (DEPTH, DSA_W, D_MODEL), DSA_W ** -0.5),
        "w_o": nrm(ks[8], (DEPTH, D_MODEL, D_MODEL), D_MODEL ** -0.5),
        "norm_ffn_g": 1.0 + nrm(ks[9], (DEPTH, D_MODEL), 0.02),
        "w_group": nrm(ks[10], (DEPTH, D_MODEL, N_GROUPS), D_MODEL ** -0.5),
        "b_group": nrm(ks[11], (DEPTH, N_GROUPS), 0.01),
        "w_router": nrm(ks[12], (DEPTH, D_MODEL, N_EXPERTS), D_MODEL ** -0.5),
        "b_router": nrm(ks[13], (DEPTH, N_EXPERTS), 0.01),
        "w1": nrm(ks[14], (DEPTH, N_EXPERTS, D_MODEL, D_EXPERT), D_MODEL ** -0.5),
        "w3": nrm(ks[15], (DEPTH, N_EXPERTS, D_MODEL, D_EXPERT), D_MODEL ** -0.5),
        "w2": nrm(ks[16], (DEPTH, N_EXPERTS, D_EXPERT, D_MODEL), D_EXPERT ** -0.5),
        "norm_final_g": 1.0 + nrm(ks[17], (D_MODEL,), 0.02),
    }

def first_block(x, meta_tokens, norm_mix_g, w_in, w_uk, w_uv, w_up_a, w_up_b, w_o, norm_ffn_g,
              w_group, b_group, w_router, b_router, w1, w3, w2, norm_final_g):
    b, s, d = x.shape
    topk = min(TOPK_MAX, s // 4)
    meta = jnp.broadcast_to(meta_tokens[None].astype(x.dtype), (b, N_META, d))
    h = jnp.concatenate([meta, x], axis=1)
    t = s + N_META
    pos = jnp.arange(t)
    for l in range(DEPTH):
        h = h + mixer(rmsnorm(h, norm_mix_g[l]), w_in[l], w_uk[l], w_uv[l], w_up_a[l], w_up_b[l], w_o[l], pos, topk)
        u = rmsnorm(h, norm_ffn_g[l]).reshape(b * t, d)
        h = h + hier_moe(u, w_group[l], b_group[l], w_router[l], b_router[l], w1[l], w3[l], w2[l]).reshape(b, t, d)
    return rmsnorm(h, norm_final_g)[:, N_META:]


D_MIX = D_MODEL
CONV_CH = D_MIX // 2
CONV_GROUPS = 8
CONV_K = 3
N_HEADS = 8
N_KV_HEADS = 2
ATTN_WIDTH = N_HEADS * HEAD_DIM
KV_WIDTH = N_KV_HEADS * HEAD_DIM
IN_WIDTH_2 = 3 * CONV_CH + ATTN_WIDTH + 2 * KV_WIDTH
WINDOW = 128
BLOCK = 128
N_BUCKETS = 32
MAX_DISTANCE = 128
PEER_HEADS = 8
PEER_NKEYS = 128
PEER_EXPERTS = PEER_NKEYS * PEER_NKEYS
PEER_DK = 128
PEER_TOPK = 16
PEER_CHUNK = 128
EPS = 1e-6


def rms_norm(x, g):
    xf = x.astype(jnp.float32)
    y = xf * lax.rsqrt(jnp.mean(xf * xf, axis=-1, keepdims=True) + EPS)
    return (y * g.astype(jnp.float32)).astype(x.dtype)

def group_rms_norm(y, g, n_groups):
    w = y.shape[-1]
    yg = y.reshape(y.shape[:-1] + (n_groups, w // n_groups))
    return rms_norm(yg, g.reshape(n_groups, w // n_groups)).reshape(y.shape)

def t5_bucket(dist):
    max_exact = N_BUCKETS // 2
    d = jnp.maximum(dist, 1).astype(jnp.float32)
    large = max_exact + (jnp.log(d / max_exact) / math.log(MAX_DISTANCE / max_exact)
                         * (N_BUCKETS - max_exact)).astype(jnp.int32)
    large = jnp.minimum(large, N_BUCKETS - 1)
    return jnp.where(dist < max_exact, dist, large)

def short_conv(b_gate, c_gate, h, conv_w):
    u = c_gate * h
    s = u.shape[1]
    up = jnp.pad(u, ((0, 0), (CONV_K - 1, 0), (0, 0)))
    y = conv_w[0] * up[:, 0:s]
    for j in range(1, CONV_K):
        y = y + conv_w[j] * up[:, j:j + s]
    return b_gate * y

def window_attention(q, k, v, rel_bias, sinks):
    bsz, s = q.shape[0], q.shape[1]
    nb = s // BLOCK
    grp = N_HEADS // N_KV_HEADS
    qb = q.reshape(bsz, nb, BLOCK, N_KV_HEADS, grp, HEAD_DIM)
    kb = k.reshape(bsz, nb, BLOCK, N_KV_HEADS, HEAD_DIM)
    vb = v.reshape(bsz, nb, BLOCK, N_KV_HEADS, HEAD_DIM)

    def with_prev(t):
        prev = jnp.concatenate([jnp.zeros_like(t[:, :1]), t[:, :-1]], axis=1)
        return jnp.concatenate([prev, t], axis=2)

    kw = with_prev(kb)
    vw = with_prev(vb)
    scores = jnp.einsum('bnqkgd,bnjkd->bnkgqj', qb, kw).astype(jnp.float32) * (HEAD_DIM ** -0.5)

    qi = jnp.arange(BLOCK)[:, None]
    kj = jnp.arange(2 * BLOCK)[None, :]
    dist = qi + BLOCK - kj
    bias = rel_bias.astype(jnp.float32)[t5_bucket(jnp.maximum(dist, 0))]
    bias = bias.transpose(2, 0, 1).reshape(N_KV_HEADS, grp, BLOCK, 2 * BLOCK)
    blk = jnp.arange(nb)[:, None, None]
    valid = (dist >= 0) & (dist < WINDOW) & (blk * BLOCK - BLOCK + kj >= 0)
    scores = jnp.where(valid[None, :, None, None], scores + bias, -jnp.inf)

    sink = sinks.astype(jnp.float32).reshape(N_KV_HEADS, grp)[None, None, :, :, None]
    m = jnp.maximum(scores.max(axis=-1), sink)
    p = jnp.exp(scores - m[..., None])
    denom = p.sum(axis=-1) + jnp.exp(sink - m)
    o = jnp.einsum('bnkgqj,bnjkd->bnkgqd', p, vw.astype(jnp.float32)) / denom[..., None]
    o = o.transpose(0, 1, 4, 2, 3, 5).reshape(bsz, s, ATTN_WIDTH)
    return o.astype(q.dtype)

def peer_ffn(h, wq, keys, u_tab, v_tab):
    bsz, s, d = h.shape

    def chunk(ht):
        t = ht.shape[0]
        q = (ht @ wq).reshape(t, PEER_HEADS, 2, PEER_DK)
        sa = jnp.einsum('thd,hnd->thn', q[:, :, 0], keys[0]).astype(jnp.float32)
        sb = jnp.einsum('thd,hnd->thn', q[:, :, 1], keys[1]).astype(jnp.float32)
        va, ia = lax.top_k(sa, PEER_TOPK)
        vb, ib = lax.top_k(sb, PEER_TOPK)
        cand = (va[..., :, None] + vb[..., None, :]).reshape(t, PEER_HEADS, PEER_TOPK * PEER_TOPK)
        cidx = (ia[..., :, None] * PEER_NKEYS + ib[..., None, :]).reshape(t, PEER_HEADS, PEER_TOPK * PEER_TOPK)
        top, pos = lax.top_k(cand, PEER_TOPK)
        eidx = jnp.take_along_axis(cidx, pos, axis=-1)
        g = jax.nn.softmax(top, axis=-1).astype(ht.dtype)
        u = u_tab[eidx]
        v = v_tab[eidx]
        a = jax.nn.gelu(jnp.einsum('thkd,td->thk', u, ht))
        return jnp.einsum('thk,thkd->td', g * a, v)

    out = lax.map(chunk, h.reshape(-1, PEER_CHUNK, d))
    return out.reshape(bsz, s, d)

def second_inputs(seed: int = 0) -> dict:
    key = jax.random.key(seed)
    ks = jax.random.split(key, 20)
    f32 = jnp.float32
    nrm = lambda k, shp, sc: jax.random.normal(k, shp, f32) * sc
    return {
        'x': nrm(ks[0], (BATCH, SEQ, D_MODEL), 1.0),
        'c': nrm(ks[1], (BATCH, D_MODEL), 1.0),
        'w_ada': nrm(ks[2], (DEPTH, D_MODEL, 6 * D_MODEL), 0.5 * D_MODEL ** -0.5),
        'b_ada': nrm(ks[3], (DEPTH, 6 * D_MODEL), 0.02),
        'norm1_g': 1.0 + nrm(ks[4], (DEPTH, D_MODEL), 0.1),
        'w_in': nrm(ks[5], (DEPTH, D_MODEL, IN_WIDTH_2), D_MODEL ** -0.5),
        'conv_w': nrm(ks[6], (DEPTH, CONV_K, CONV_CH), CONV_K ** -0.5),
        'q_norm_g': 1.0 + nrm(ks[7], (DEPTH, HEAD_DIM), 0.1),
        'k_norm_g': 1.0 + nrm(ks[8], (DEPTH, HEAD_DIM), 0.1),
        'sinks': nrm(ks[9], (DEPTH, N_HEADS), 0.5),
        'rel_bias': nrm(ks[10], (N_BUCKETS, N_HEADS), 0.5),
        'conv_out_g': 1.0 + nrm(ks[11], (DEPTH, CONV_CH), 0.1),
        'attn_out_g': 1.0 + nrm(ks[12], (DEPTH, ATTN_WIDTH), 0.1),
        'w_out': nrm(ks[13], (DEPTH, D_MIX, D_MODEL), D_MIX ** -0.5),
        'norm2_g': 1.0 + nrm(ks[14], (DEPTH, D_MODEL), 0.1),
        'peer_wq': nrm(ks[15], (DEPTH, D_MODEL, PEER_HEADS * 2 * PEER_DK), D_MODEL ** -0.5),
        'peer_keys': nrm(ks[16], (DEPTH, 2, PEER_HEADS, PEER_NKEYS, PEER_DK), PEER_DK ** -0.5),
        'peer_u': nrm(ks[17], (DEPTH, PEER_EXPERTS, D_MODEL), D_MODEL ** -0.5),
        'peer_v': nrm(ks[18], (DEPTH, PEER_EXPERTS, D_MODEL), 0.5),
    }

def second_block(x, c, w_ada, b_ada, norm1_g, w_in, conv_w, q_norm_g, k_norm_g, sinks, rel_bias,
              conv_out_g, attn_out_g, w_out, norm2_g, peer_wq, peer_keys, peer_u, peer_v):
    bsz, s, _ = x.shape
    cond = jax.nn.silu(c)
    splits = [CONV_CH, 2 * CONV_CH, 3 * CONV_CH, 3 * CONV_CH + ATTN_WIDTH,
              3 * CONV_CH + ATTN_WIDTH + KV_WIDTH]
    for l in range(DEPTH):
        mod = cond @ w_ada[l] + b_ada[l]
        sh1, sc1, g1, sh2, sc2, g2 = jnp.split(mod, 6, axis=-1)

        h = rms_norm(x, norm1_g[l]) * (1.0 + sc1[:, None]) + sh1[:, None]
        proj = h @ w_in[l]
        b_gate, c_gate, hc, q, k, v = jnp.split(proj, splits, axis=-1)
        y_conv = short_conv(b_gate, c_gate, hc, conv_w[l])
        q = rms_norm(q.reshape(bsz, s, N_HEADS, HEAD_DIM), q_norm_g[l])
        k = rms_norm(k.reshape(bsz, s, N_KV_HEADS, HEAD_DIM), k_norm_g[l])
        v = v.reshape(bsz, s, N_KV_HEADS, HEAD_DIM)
        y_attn = window_attention(q, k, v, rel_bias, sinks[l])
        mixed = jnp.concatenate([group_rms_norm(y_conv, conv_out_g[l], CONV_GROUPS),
                                 group_rms_norm(y_attn, attn_out_g[l], N_HEADS)], axis=-1)
        x = x + g1[:, None] * (mixed @ w_out[l])

        h2 = rms_norm(x, norm2_g[l]) * (1.0 + sc2[:, None]) + sh2[:, None]
        x = x + g2[:, None] * peer_ffn(h2, peer_wq[l], peer_keys[l], peer_u[l], peer_v[l])
    return x


def setup_inputs(seed=0):
    out = dict(first_inputs(seed))
    for name, value in second_inputs(seed + 1).items():
        if name != "x":
            out[name + "_2"] = value
    return out


def reference(
    x, meta_tokens, norm_mix_g, w_in, w_uk, w_uv, w_up_a, w_up_b, w_o, norm_ffn_g, w_group,
    b_group, w_router, b_router, w1, w3, w2, norm_final_g, c_2, w_ada_2, b_ada_2, norm1_g_2,
    w_in_2, conv_w_2, q_norm_g_2, k_norm_g_2, sinks_2, rel_bias_2, conv_out_g_2, attn_out_g_2,
    w_out_2, norm2_g_2, peer_wq_2, peer_keys_2, peer_u_2, peer_v_2,
):
    x = first_block(
        x, meta_tokens, norm_mix_g, w_in, w_uk, w_uv, w_up_a, w_up_b, w_o, norm_ffn_g, w_group,
        b_group, w_router, b_router, w1, w3, w2, norm_final_g,
    )
    return second_block(
        x, c_2, w_ada_2, b_ada_2, norm1_g_2, w_in_2, conv_w_2, q_norm_g_2, k_norm_g_2, sinks_2,
        rel_bias_2, conv_out_g_2, attn_out_g_2, w_out_2, norm2_g_2, peer_wq_2, peer_keys_2,
        peer_u_2, peer_v_2,
    )


_drawn_inputs = setup_inputs


def setup_inputs(seed=0):
    import zlib

    import numpy as np

    out = dict(_drawn_inputs(seed))
    spreads = {}
    factors = {'b_group': 2.943,
     'b_router': 2.982,
     'q_norm_g_2': 4.786,
     'k_norm_g_2': 4.656,
     'sinks_2': 200.0}
    for name, (base, spread) in spreads.items():
        noise = np.random.default_rng([zlib.crc32(name.encode()), seed]).standard_normal(out[name].shape)
        drawn = base * np.exp(spread * noise) if base else spread * noise
        out[name] = jnp.asarray(drawn.astype(out[name].dtype))
    for name, factor in factors.items():
        out[name] = (out[name] * factor).astype(out[name].dtype)
    return out
```

```python
import numpy as np

import concourse.bass as bass
from concourse import mybir
from concourse.alu_op_type import AluOpType as ALU
from contextlib import ExitStack

F32 = mybir.dt.float32
U32 = mybir.dt.uint32
ACT = mybir.ActivationFunctionType
AX = mybir.AxisListType.X

T = 512
META = 16
TK = T + META
EPS = 1e-6


class Queue:

    def __init__(self, sem):
        self.sem, self.n, self.items, self.seen = sem, 0, [], {}

    def wait(self, *marks):
        for sem, value in marks:
            if self.seen.get(id(sem), 0) < value:
                self.seen[id(sem)] = value
                self.items.append((None, sem, value, None))

    def run(self, method, *args, mark=True, **kw):
        if mark:
            self.n += 1
        self.items.append((method, args, kw, (self.sem, 1) if mark else None))
        return (self.sem, self.n)

    def dma(self, method, out, in_, slot, **kw):
        slot.n += 16
        kw["out"], kw["in_"] = out, in_
        self.items.append((method, (), kw, (slot.sem, 16)))
        return (slot.sem, slot.n)

    def now(self):
        return (self.sem, self.n)

    def flush(self, eng):
        for item in self.items:
            if item[0] is None:
                eng.wait_ge(item[1], item[2])
            elif item[0] == "call":
                item[1](eng)
            else:
                ins = item[0](*item[1], **item[2])
                if item[3] is not None:
                    ins.then_inc(*item[3])


class Slot:

    def __init__(self, sem):
        self.sem, self.n = sem, 0

    def now(self):
        return (self.sem, self.n)


ARENA = 53200
RING = 4096
O_TEMP = 16384
O_XT = 40960
O_CST = 45184
O_WORK = 47360

C_ID, C_ONE, C_NEG, C_TRI, C_UP, C_TRIM, C_SEL, C_M8, C_BLK, C_IOTA = (
    0, 128, 256, 384, 512, 640, 768, 1008, 1016, 1144)
C_N = 1272
V_MIX, V_FFN, V_FIN, V_N1, V_N2, V_BADA, V_COND, V_CONV, V_CG, V_AG, V_QG, V_KG = (
    0, 8, 16, 24, 32, 40, 88, 96, 108, 112, 116, 117)
V_N = 118


def program(nc, A):
    with ExitStack() as ctx:
        build(nc, A, ctx)


def build(nc, A, ctx):
    AR = ctx.enter_context(nc.sbuf_tensor("arena", [128, ARENA], F32))
    PS = ctx.enter_context(nc.psum_tensor("psum", [128, 8, 512], F32))

    def new_sem(name):
        return ctx.enter_context(nc.semaphore(name))

    pe, ac, dv, po, sp = (Queue(new_sem("s_" + n)) for n in ("pe", "act", "dve", "pool", "sp"))
    engines = (pe, ac, dv, po)
    te, se, ve, ge, sy = nc.tensor, nc.scalar, nc.vector, nc.gpsimd, nc.sync

    def slot(name):
        return Slot(new_sem("d_" + name))

    def at(off, n):
        return AR[:, off:off + n]

    def at3(off, a, b):
        return AR[:, off:off + a * b].rearrange("p (a b) -> p a b", a=a)

    def mm(out, l, r, start, stop, mark=False):
        return pe.run(te.matmul, out, l, r, start=start, stop=stop, mark=mark, skip_group_check=True)

    def turn(out, i, mark=False):
        k = i.shape[0]
        return pe.run(te.transpose, out, i, CST[0:k, C_ID:C_ID + k], mark=mark)

    def barrier(*extra):
        marks = [q.now() for q in engines] + list(extra)
        for q in engines + (sp,):
            q.wait(*marks)

    ring_sem = [slot(f"ring{i}") for i in range(6)]
    pieces = []
    loaded = {}
    free_marks = {}

    def ring_at(s, width):
        return at(s * RING, width)

    def piece(src, width, s):
        pieces.append((src, width, s))
        return len(pieces) - 1

    state = {"next": 0}

    def load_ready():
        while state["next"] < len(pieces):
            src, width, (sem, off) = pieces[state["next"]]
            if (sem, off) in state and state[(sem, off)] is None:
                return
            mark = state.get((sem, off))
            if mark is not None:
                sp.wait(*mark)
            loaded[state["next"]] = sp.dma(sy.dma_start, at(off, width), src, ring_sem[sem])
            state[(sem, off)] = None
            state["next"] += 1

    def use(i):
        if i not in loaded:
            load_ready()
        return loaded[i]

    def release(i, *marks):
        _, _, key = pieces[i]
        state[key] = marks
        load_ready()

    def pos(i, kk):
        src, width, (sem, off) = pieces[i]
        return at3(off, kk, width // kk)

    XT = at3(O_XT, 8, TK)
    CST = at(O_CST, C_N)
    VEC = at(O_CST + C_N, V_N)
    SMALL = O_CST + C_N + V_N
    assert SMALL <= O_WORK
    ONE = CST[:, C_ONE:C_ONE + 128]
    NEG = CST[:, C_NEG:C_NEG + 128]
    TRI = CST[:, C_TRI:C_TRI + 128]
    UP = CST[:, C_UP:C_UP + 128]

    s_in = slot("in")
    s_misc = [slot(f"misc{i}") for i in range(8)]
    t_in = sp.dma(sy.dma_start, XT[:, :, 0:META], A["metaT"].rearrange("(k p) t -> p k t", p=128), s_in)
    t_in = sp.dma(sy.dma_start, XT[:, :, META:TK], A["xT"].rearrange("(k p) t -> p k t", p=128), s_in)
    t_in = sp.dma(sy.dma_start, CST, A["cst"], s_in)
    t_in = sp.dma(sy.dma_start, VEC, A["vec"], s_in)
    for q in engines:
        q.wait(t_in)

    PROJ = [piece(A["wp1"][i], 4096, (i % 4, (i % 4) * RING)) for i in range(7)]
    PSM = piece(A["wp1s"], 320, (3, 3 * RING))
    PG = [piece(A["wp1"][7 + i], 4096, (i, i * RING)) for i in range(4)]

    o = O_TEMP
    UT = at3(o, 8, TK); o += 8 * TK
    KA = at3(o, 4, TK); o += 4 * TK
    QA = at3(o, 4, T); o += 4 * T
    VA = at3(o, 4, T); o += 4 * T
    QLAT = at3(o, 8, T); o_qlat = o; o += 8 * T
    QI = at3(o, 4, T); o_qi = o; o += 4 * T
    KI = at(o, TK); o += TK
    CKT = at(o, TK); o += TK
    CKV = at3(o, 5, 128); o += 640
    RB = at(o, T); o += T
    KR = at(o, TK); o += TK
    WI = at3(o, 4, 8); o += 32
    WUK = at3(o, 4, 128); o += 512
    WUV = at3(o, 8, 64); o += 512
    KMB = at3(o, 4, 128); o += 512
    VM2 = at(o, T); o += T
    PM = at(o, T); o += T
    YA = at3(o, 4, T); o += 4 * T
    assert o <= O_XT, o
    OW = O_WORK
    SQ = at3(o_qi, 4, TK)
    RN = at(OW, TK)
    COS = at(OW + TK, TK)
    SIN = at(OW + 2 * TK, TK)
    T1 = at(OW + 3 * TK, TK)
    T2 = at(OW + 4 * TK, TK)
    QBN = at3(o_qlat, 4, T)
    s_w = slot("w")
    t_tab = sp.dma(sy.dma_start, COS, A["cos"], s_w)
    t_tab = sp.dma(sy.dma_start, SIN, A["sin"], s_w)
    t_tab = sp.dma(sy.dma_start, WUK, A["wukT"], s_w)
    t_tab = sp.dma(sy.dma_start, WUV, A["wuv"], s_w)
    load_ready()

    def halves(n):
        return [(0, n)] if n <= 512 else [(0, n // 2), (n // 2, n - n // 2)]

    def norm(X, c0, n, U, gcol, squares, r, bank, cols=None):
        hs = halves(n)
        done = []
        sq_free = {}
        for k in range(8):
            b = k % squares.shape[1]
            s = squares[:, b, 0:n]
            x = X[:, k, c0:c0 + n]
            if k % 2 == 0:
                if b in sq_free:
                    ac.wait(sq_free[b])
                t = ac.run(se.activation, s, x, ACT.Square)
            else:
                if b in sq_free:
                    po.wait(sq_free[b])
                t = po.run(ge.tensor_tensor, s, x, x, ALU.mult)
            pe.wait(t)
            for i, (a, w) in enumerate(hs):
                t = mm(PS[:, bank + i, 0:w], ONE, s[:, a:a + w], k == 0, k == 7, mark=True)
            sq_free[b] = t
        dv.wait(t)
        for i, (a, w) in enumerate(hs):
            t = dv.run(ve.tensor_scalar, r[:, a:a + w], PS[:, bank + i, 0:w], 1.0 / 1024, EPS, ALU.mult, ALU.add)
        ac.wait(t)
        t = ac.run(se.activation, r[:, 0:n], r[:, 0:n], ACT.Sqrt)
        dv.wait(t)
        t = dv.run(ve.reciprocal, r[:, 0:n], r[:, 0:n])
        dv.wait(t)
        for k in range(8):
            t = dv.run(ve.scalar_tensor_tensor, U[:, k, 0:n], X[:, k, c0:c0 + n], (VEC[:, gcol + k:gcol + k + 1] if cols is None else cols[:, k:k + 1]),
                       r[:, 0:n], ALU.mult, ALU.mult)
        return t

    t_ut = norm(XT, 0, TK, UT, V_MIX, SQ, RN, 0)
    pe.wait(t_ut)

    def proj(W, c, m, b, p0, hs, X=None, base=0, kk=8):
        X = UT if X is None else X
        for i, (a, w) in enumerate(hs):
            for k in range(kk):
                t = mm(PS[p0:p0 + m, b + i, 0:w], W[:, k, c:c + m], X[:, k, base + a:base + a + w],
                       k == 0, k == kk - 1, mark=(k == kk - 1))
        return t

    FULL = halves(TK)
    XONLY = [(0, T)]
    bank_free = [None] * 8

    def claim(*banks):
        for b in banks:
            if bank_free[b] is not None:
                pe.wait(*bank_free[b])

    def evac(q, out, in_, b, t, scale=None):
        q.wait(t)
        if q is ac:
            t = ac.run(se.activation, out, in_, ACT.Copy, scale=1.0 if scale is None else scale)
        elif scale is None:
            t = dv.run(ve.tensor_copy, out, in_)
        else:
            t = dv.run(ve.tensor_scalar, out, in_, scale, None, ALU.mult)
        return t

    ZERO = at(O_XT - 512, 512)
    s_z = slot("z")
    CAP = 64
    NX = (1024 - 32) // CAP
    ROWS = 32 * CAP + NX * CAP
    xb = nc.dram_tensor("xb", [ROWS, 1024], F32, kind="Internal").ap()
    yb = nc.dram_tensor("yb", [ROWS, 1024], F32, kind="Internal").ap()
    t = dv.run(ve.memset, ZERO, 0.0)
    sp.wait(t)
    n0 = NX * CAP * 2 // 128
    ybt = yb.rearrange("r (a c) -> (r a) c", a=2)[64 * CAP:2 * ROWS, :]
    sp.dma(sy.dma_start, ybt[0:128 * n0, :].rearrange("(n p) c -> p n c", p=128), ZERO.unsqueeze(1).to_broadcast([128, n0, 512]), s_z)
    if NX * CAP * 2 > 128 * n0:
        sp.dma(sy.dma_start, ybt[128 * n0:, :], ZERO[0:NX * CAP * 2 - 128 * n0, :], s_z)
    nz = ROWS * 2 // 128
    sp.dma(sy.dma_start, xb.rearrange("r (a c) -> (r a) c", a=2)[0:128 * nz, :].rearrange("(n p) c -> p n c", p=128),
           ZERO.unsqueeze(1).to_broadcast([128, nz, 512]), s_z)
    if ROWS * 2 > 128 * nz:
        sp.dma(sy.dma_start, xb.rearrange("r (a c) -> (r a) c", a=2)[128 * nz:2 * ROWS, :], ZERO[0:2 * ROWS - 128 * nz, :], s_z)

    pe.wait(use(PROJ[0]))
    for j in range(4):
        b = 2 * j
        claim(b, b + 1)
        t = proj(pos(PROJ[0], 8), 128 * j, 128, b, 0, FULL)
        t = evac((ac, dv)[j % 2], KA[:, j, :].rearrange("p (a b) -> p a b", a=2), PS[:, b:b + 2, 0:264], b, t)
        bank_free[b] = bank_free[b + 1] = (t,)
    release(PROJ[0], pe.now())
    t_ka = (ac.now(), dv.now())
    pe.wait(use(PROJ[1]))
    for j in range(4):
        claim(j)
        t = proj(pos(PROJ[1], 8), 128 * j, 128, j, 0, XONLY, base=META)
        t = evac((ac, dv)[j % 2], QA[:, j, :], PS[:, j, :], j, t, scale=0.125)
        bank_free[j] = (t,)
    release(PROJ[1], pe.now())
    pe.wait(use(PROJ[2]))
    W = pos(PROJ[2], 8)
    for j in range(4):
        claim(4 + j)
        for k in range(8):
            t = mm(PS[:, 4 + j, :], UT[:, k, META + 128 * j:META + 128 * j + 128], W[:, k, :], k == 0, k == 7, mark=k == 7)
        t = evac((ac, dv)[j % 2], VA[:, j, :], PS[:, 4 + j, :], 4 + j, t)
        bank_free[4 + j] = (t,)
    UR = at3(OW + 3 * TK, 8, 128)
    dv.wait(t_ut)
    t = dv.run(ve.tensor_copy, UR.rearrange("p k (r m) -> p k r m", r=8),
               UT[:, :, 0:META].unsqueeze(2).to_broadcast([128, 8, 8, META]))
    pe.wait(t)
    claim(0)
    for k in range(8):
        t = mm(PS[:, 0, :], UR[:, k, :], W[:, k, :], k == 0, k == 7, mark=k == 7)
    release(PROJ[2], pe.now())
    VM = at(o_qlat + 4 * T, T)
    dv.wait(t)
    t = dv.run(ve.tensor_tensor, VM.rearrange("p (h d) -> p h d", h=8), PS[:, 0, :].rearrange("p (h d) -> p h d", h=8),
               CST[:, C_M8:C_M8 + 8].unsqueeze(2).to_broadcast([128, 8, 64]), ALU.mult)
    bank_free[0] = (t,)
    pe.wait(use(PROJ[3]))
    for j in range(4):
        b = (1, 2, 3, 4)[j]
        claim(b)
        t = proj(pos(PROJ[3], 8), 128 * j, 128, b, 0, XONLY, base=META)
        t = evac((ac, dv)[j % 2], QBN[:, j, :], PS[:, b, :], b, t, scale=0.125)
        bank_free[b] = (t,)
    release(PROJ[3], pe.now())

    dv.wait(t_tab)

    def rotated(W, ca, cb, m, hs, base, b, out, scale=1.0):
        n = sum(w for _, w in hs)
        nb = len(hs)
        w = n // nb
        claim(*range(b, b + 2 * nb))
        proj(W, ca, m, b, 0, hs, base=base)
        t = proj(W, cb, m, b + nb, 0, hs, base=base)
        dv.wait(t)
        co, si = (x[0:m, base:base + n].rearrange("p (a b) -> p a b", a=nb) for x in (COS, SIN))
        t1, t2, ou = (x[0:m, 0:n].rearrange("p (a b) -> p a b", a=nb) for x in (T1, T2, out))
        dv.run(ve.scalar_tensor_tensor, t1, PS[0:m, b:b + nb, 0:w], scale, co, ALU.mult, ALU.mult)
        t = dv.run(ve.scalar_tensor_tensor, t2, PS[0:m, b + nb:b + 2 * nb, 0:w], scale, si, ALU.mult, ALU.mult)
        for i in range(b, b + 2 * nb):
            bank_free[i] = (t,)
        dv.wait(t)
        return dv.run(ve.tensor_tensor, ou, t1, t2, ALU.add)

    pe.wait(use(PROJ[4]))
    W = pos(PROJ[4], 8)
    dv.wait(t)
    t = rotated(W, 0, 128, 128, XONLY, META, 0, RB, 0.125)
    dv.wait(t)
    t = rotated(W, 256, 384, 128, FULL, 0, 4, KR)
    t_kr = t
    release(PROJ[4], pe.now())
    pe.wait(use(PROJ[5]))
    W = pos(PROJ[5], 8)
    claim(2, 3)
    t = proj(W, 0, 128, 2, 0, FULL)
    t = evac(ac, CKT.rearrange("p (a b) -> p a b", a=2), PS[:, 2:4, 0:264], 2, t)
    bank_free[2] = bank_free[3] = (t,)
    claim(0)
    for i in range(4):
        for k in range(8):
            t = mm(PS[:, 0, 128 * i:128 * i + 128], UT[:, k, 128 * i:128 * i + 128], W[:, k, 0:128], k == 0, k == 7,
                   mark=k == 7)
    t = evac(dv, CKV[:, 0:4, :], PS[:, 0, :].rearrange("p (a b) -> p a b", a=4), 0, t)
    bank_free[0] = (t,)
    claim(1)
    for k in range(8):
        t = mm(PS[0:16, 1, 0:128], UT[:, k, 512:528], W[:, k, 0:128], k == 0, k == 7, mark=k == 7)
    t = evac(dv, CKV[0:16, 4, :], PS[0:16, 1, 0:128], 1, t)
    bank_free[1] = (t,)
    claim(4, 5)
    t = proj(W, 128, 128, 4, 0, FULL)
    t_kin = evac(ac, KI.rearrange("p (a b) -> p a b", a=2), PS[:, 4:6, 0:264], 4, t)
    bank_free[4] = bank_free[5] = (t_kin,)
    dv.wait(t_kr)
    RI = at(OW, T)
    t_ri = rotated(W, 256, 384, 128, XONLY, META, 6, RI)
    release(PROJ[5], pe.now())
    pe.wait(use(PROJ[6]))
    for j in range(4):
        claim(j)
        t = proj(pos(PROJ[6], 8), 128 * j, 128, j, 0, XONLY, base=META)
        t = evac((ac, dv)[j % 2], QI[:, j, :], PS[:, j, :], j, t)
        bank_free[j] = (t,)
    t_qin = (ac.now(), dv.now())
    release(PROJ[6], pe.now())
    pe.wait(use(PSM))
    W = pos(PSM, 8)
    dv.wait(t_ri)
    RK = at(OW + 5 * TK, TK)
    t_rk = rotated(W, 0, 16, 16, FULL, 0, 4, RK)
    claim(0)
    for i in range(4):
        for k in range(8):
            t = mm(PS[:, 0, 8 * i:8 * i + 8], UT[:, k, META + 128 * i:META + 128 * i + 128], W[:, k, 32:40], k == 0, k == 7,
                   mark=k == 7)
    t_wi = evac(dv, WI, PS[:, 0, 0:32].rearrange("p (a b) -> p a b", a=4), 0, t)
    bank_free[0] = (t_wi,)
    release(PSM, pe.now())
    sp.wait(t_kin, t_ri, t_rk, *t_qin)
    for h in range(8):
        p0 = 64 * (h % 2) + 48
        t_rot = sp.dma(sy.dma_start, QI[p0:p0 + 16, h // 2, :], RI[16 * h:16 * h + 16, :], s_w)
    t_rot = sp.dma(sy.dma_start, KI[48:64, :], RK[0:16, :], s_w)
    t_rot = sp.dma(sy.dma_start, KI[112:128, :], RK[0:16, :], s_w)
    for h in range(8):
        pass
    pe.wait(t_tab)
    for q in (ac, dv):
        pe.wait(q.now())
    claim(*range(8))
    for h in range(8):
        p0 = 64 * (h % 2)
        t = mm(PS[:, h, :], WUK[p0:p0 + 48, h // 2, :], QBN[p0:p0 + 48, h // 2, :], True, True, mark=True)
    t_all = t
    dv.wait(t_all)
    t_vm = dv.run(ve.tensor_copy, VM2, VM)
    VM = VM2
    ac.wait(t_all, t_vm)
    dv.wait(t_vm)
    for h in range(8):
        t = evac((ac, dv)[h % 2], QLAT[:, h, :], PS[:, h, :], h, t_all)
        bank_free[h] = (t,)
    for q in engines:
        q.wait(t_rot)
    barrier()

    ac.run(se.preload_act_table_set, "natural_log_exp_and_others", mark=False)
    t = po.run(ge.memset, KMB, 0.0)
    po.wait(t)
    for h in range(8):
        p0 = 64 * (h % 2)
        t_kmb = po.run(ge.tensor_copy, KMB[p0:p0 + 64, h // 2, 16 * h:16 * h + 16], KA[p0:p0 + 64, h // 2, 0:META])
    NQ = [T - 128 * kt for kt in range(4)]
    OFF = [0, 512, 896, 1152]

    def by_tile(off):
        return [AR[:, off + OFF[kt]:off + OFF[kt] + NQ[kt]] for kt in range(4)]

    EX = [by_tile(OW + 1280 * i) for i in range(2)]
    PT = [by_tile(OW + 2560 + 1280 * i) for i in range(2)]

    def softplus(z, e, out, p, marks):
        ac.wait(*marks)
        t = ac.run(se.activation, e, z, ACT.Abs)
        ac.wait(t)
        t = ac.run(se.activation, e, e, ACT.Exp, scale=-1.0)
        ac.wait(t)
        t = ac.run(se.activation, e, e, ACT.Ln, bias=1.0)
        dv.wait(t)
        return dv.run(ve.scalar_tensor_tensor, out, z, 0.0, e, ALU.max, ALU.add)

    def strict(x, t):
        po.wait(t)
        return po.run(ge.affine_select, out=x, in_=x, pattern=[[1, 128]], compare_op=ALU.is_gt, fill=0.0,
                      base=0, channel_multiplier=-1)

    pe.wait(t_kmb)
    claim(7)
    for j in range(4):
        t = mm(PS[:, 7, :], KMB[:, j, :], QA[:, j, :], j == 0, False, mark=j == 3)
    EM = EX[1][0]
    t_pm = softplus(PS[:, 7, :], EM, PM, 128, (t,))
    pe.wait(t_pm)
    t = mm(PS[:, 7, :], CST[:, C_TRIM:C_TRIM + 128], PM, False, False, mark=True)
    ex_free = [None, (t_pm,)]
    pt_free = [None, None]
    for h in range(8):
        i, j, p0 = h % 2, h // 2, 64 * (h % 2)
        tp = [None] * 4
        for kt in range(4):
            claim(kt)
            c = META + 128 * kt
            t = mm(PS[:, kt, 128 * kt:T], KA[p0:p0 + 64, j, c:c + 128], QA[p0:p0 + 64, j, 128 * kt:T], True, False, mark=True)
            if kt == 0:
                for x in (ex_free[i], pt_free[i]):
                    if x is not None:
                        ac.wait(*x)
                        dv.wait(*x)
            t = softplus(PS[:, kt, 128 * kt:T], EX[i][kt], PT[i][kt], 128, (t,))
            tp[kt] = strict(PT[i][kt][:, 0:128], t)
        ta = []
        for kt in (3, 2, 1, 0):
            pe.wait(tp[kt])
            mm(PS[:, kt, 128 * kt:T], TRI, PT[i][kt], False, kt == 3, mark=kt == 3)
            for k2 in range(kt + 1, 4):
                t = mm(PS[:, kt, 128 * k2:T], NEG, PT[i][k2], False, k2 == 3, mark=k2 == 3)
            t = pe.now()
            ac.wait(t)
            t = ac.run(se.activation, EX[i][kt], PS[:, kt, 128 * kt:T], ACT.Exp)
            bank_free[kt] = (t,)
            ta.append((kt, strict(EX[i][kt][:, 0:128], t)))
        sel = CST[:, C_SEL + 112 - 16 * h:C_SEL + 240 - 16 * h]
        for kt in range(4):
            t = mm(PS[:, 7, 128 * kt:T], sel, PT[i][kt], False, h == 7 and kt == 3, mark=True)
        pt_free[i] = (t,)
        b = 4 + j % 2
        if h % 2 == 0:
            claim(b)
        for kt, t in sorted(ta):
            pe.wait(t)
            t = mm(PS[p0:p0 + 64, b, 128 * kt:T], VA[:, kt, 64 * h:64 * h + 64], EX[i][kt], kt == 0, kt == 3, mark=kt == 3)
        ex_free[i] = (t,)
        if h % 2 == 1:
            dv.wait(t)
            t = dv.run(ve.tensor_copy, YA[:, j, :], PS[:, b, :])
            bank_free[b] = (t,)
    ac.wait(pt_free[1][0], pt_free[0][0])
    t = ac.run(se.activation, PM, PS[:, 7, :], ACT.Exp)
    bank_free[7] = (t,)
    pe.wait(t)
    for j in range(4):
        claim(j)
        t = mm(PS[:, j, :], VM2[:, 128 * j:128 * j + 128], PM, True, True, mark=True)
        dv.wait(t, dv.now())
        t = dv.run(ve.tensor_tensor, YA[:, j, :], YA[:, j, :], PS[:, j, :], ALU.add)
        bank_free[j] = (t,)
    barrier()

    OLAT = at3(O_TEMP + 8 * TK, 8, T)
    YB = QI
    o_va = O_TEMP + 8 * TK + 4 * TK + 4 * T
    RS = [at(o_va + TK * i, TK) for i in range(2)]
    QM = at3(o_va + 2 * TK, 4, 128)
    P = at3(OW, 4, TK)
    PTR = at3(OW + 4 * TK, 5, 512)
    SC = at(OW + 4 * TK + 2560, TK)
    MB = at(OW + 5 * TK + 2560, TK)
    o = OW + 6 * TK + 2560
    M8 = at(o, 8)
    MX = at(o + 8, 4)
    SM = at(o + 12, 4)
    assert o + 16 <= ARENA
    rs_free = [None, None]
    for n in range(4):
        nk = META + 128 * (n + 1)
        np_ = 1 if nk <= 512 else 2
        w = nk // np_
        ks = [(i * w, w) for i in range(np_)]
        q0 = 128 * n

        def view(x):
            return x[:, 0:nk].rearrange("p (a b) -> p a b", a=np_)

        def bank(b):
            return PS[:, b:b + np_, 0:w]

        sc = view(SC)
        for h in range(8):
            j, p0, b = h // 2, 64 * (h % 2), 2 * (h % 2)
            claim(*range(b, b + np_))
            for i, (a, ww) in enumerate(ks):
                t = mm(PS[:, b + i, 0:w], QI[p0:p0 + 64, j, q0:q0 + 128], KI[p0:p0 + 64, a:a + w], True, True, mark=True)
            r = view(RS[h % 2])
            if rs_free[h % 2] is not None:
                ac.wait(rs_free[h % 2])
            ac.wait(t)
            t = ac.run(se.activation, r, bank(b), ACT.Relu)
            for x in range(b, b + np_):
                bank_free[x] = (t,)
            dv.wait(t, dv.now())
            if h == 0:
                t = dv.run(ve.tensor_scalar, sc, r, WI[:, n, h:h + 1], None, ALU.mult)
            else:
                t = dv.run(ve.scalar_tensor_tensor, sc, r, WI[:, n, h:h + 1], sc, ALU.mult, ALU.add)
            rs_free[h % 2] = t
        dv.wait(t)
        t = dv.run(ve.memset, SC[0:64, nk - 64:nk], -3.0e38)
        for i in range(16):
            dv.wait(t)
            t = dv.run(ve.max, M8, SC[:, 0:nk])
            dv.wait(t)
            t = dv.run(ve.match_replace, SC[:, 0:nk], M8, SC[:, 0:nk], -3.3e38)
        dv.wait(t)
        t = dv.run(ve.tensor_scalar, MB[:, 0:nk], SC[:, 0:nk], -3.2e38, -1.0e30, ALU.is_gt, ALU.mult)
        dv.wait(t)
        t_mb = dv.run(ve.memset, MB[0:64, nk - 64:nk], -1.0e30)
        mb = view(MB)
        for g in range(2):
            if g or n:
                po.wait(t_qm)
            for h in range(4):
                t = po.run(ge.tensor_scalar, QM[:, h, :], RB[:, q0:q0 + 128], CST[:, C_M8 + 4 * g + h:C_M8 + 4 * g + h + 1],
                           None, ALU.mult)
            pe.wait(t)
            for h in range(4):
                b = 2 * (h % 2)
                claim(*range(b, b + np_))
                for i, (a, ww) in enumerate(ks):
                    mm(PS[:, b + i, 0:w], QLAT[:, 4 * g + h, q0:q0 + 128], CKT[:, a:a + w], True, False)
                    t = mm(PS[:, b + i, 0:w], QM[:, h, :], KR[:, a:a + w], False, True, mark=True)
                t_qm = t
                dv.wait(t, t_mb)
                if g or n:
                    dv.wait(t_ptr)
                p = view(P[:, h, :])
                t = dv.run(ve.tensor_tensor, p, bank(b), mb, ALU.add)
                for x in range(b, b + np_):
                    bank_free[x] = (t,)
                dv.wait(t)
                t = dv.run(ve.tensor_reduce, MX[:, h:h + 1], P[:, h, 0:nk], AX, ALU.max, negate=True)
                ac.wait(t)
                t = ac.run(se.activation, P[:, h, 0:nk], P[:, h, 0:nk], ACT.Exp, bias=MX[:, h:h + 1], accum_out=SM[:, h:h + 1])
                dv.wait(t)
                t = dv.run(ve.reciprocal, SM[:, h:h + 1], SM[:, h:h + 1])
                dv.wait(t)
                t_p = dv.run(ve.tensor_scalar, P[:, h, 0:nk], P[:, h, 0:nk], SM[:, h:h + 1], None, ALU.mult)
            pe.wait(t_p)
            for k in range(n + 2):
                m = 128 if k <= n else 16
                b = 4 + k % 2
                claim(b)
                for h in range(4):
                    t = turn(PS[0:m, b, 128 * h:128 * h + 128], P[:, h, 128 * k:128 * k + m], mark=h == 3)
                t_ptr = t
                q = (ac, dv)[k % 2]
                if g or n:
                    q.wait(t_ol)
                t = evac(q, PTR[0:m, k, :], PS[0:m, b, :], b, t)
                bank_free[b] = (t,)
            pe.wait(ac.now(), dv.now())
            claim(6 + g)
            for k in range(n + 2):
                m = 128 if k <= n else 16
                t = mm(PS[:, 6 + g, :], CKV[0:m, k, :], PTR[0:m, k, :], k == 0, k == n + 1, mark=k == n + 1)
            t_ol = t
            t = evac(ac, OLAT[:, 4 * g:4 * g + 4, q0:q0 + 128], PS[:, 6 + g, :].rearrange("p (a b) -> p a b", a=4), 6 + g, t)
            bank_free[6 + g] = (t,)
    pe.wait(t)
    for h in range(8):
        j, p0 = h // 2, 64 * (h % 2)
        if h % 2 == 0:
            claim(j)
        t = mm(PS[p0:p0 + 64, j, :], WUV[:, h, :], OLAT[:, h, :], True, True, mark=True)
        if h % 2 == 1:
            t = evac((ac, dv)[j % 2], YB[:, j, :], PS[:, j, :], j, t)
            bank_free[j] = (t,)
    barrier()

    o = O_TEMP + 8 * TK
    Z = at3(o, 8, T); o += 8 * T
    WUA = at3(o, 4, 1024); o += 4096
    assert o <= o_qi
    s_up = slot("up")
    WUB = at3(OW, 4, 1024)
    t_up = sp.dma(sy.dma_start, WUA, A["wupa"], s_up)
    t_up = sp.dma(sy.dma_start, WUB, A["wupb"], s_up)
    GS = [at(OW + 4096 + 512 * i, 512) for i in range(3)]
    gs_free = None
    for i in range(8):
        b = 4 * (i % 2)
        claim(b, b + 1, b + 2, b + 3)
        for x, gi in enumerate((i // 4, 2 + i // 4)):
            pe.wait(use(PG[gi]))
            proj(pos(PG[gi], 8), 128 * (i % 4), 128, b + x, 0, XONLY, base=META)
            if i % 4 == 3:
                release(PG[gi], pe.now())
        t_g = pe.now()
        pe.wait(t_up)
        for k in range(4):
            mm(PS[:, b + 2, :], WUA[:, k, 128 * i:128 * i + 128], YA[:, k, :], k == 0, k == 3)
        for k in range(4):
            t = mm(PS[:, b + 3, :], WUB[:, k, 128 * i:128 * i + 128], YB[:, k, :], k == 0, k == 3, mark=k == 3)
        ac.wait(t_g)
        if gs_free is not None:
            ac.wait(gs_free)
        ac.run(se.activation, GS[0], PS[:, b, :], ACT.Sigmoid)
        t2 = ac.run(se.activation, GS[1], PS[:, b + 1, :], ACT.Sigmoid)
        dv.wait(t, t2)
        t = dv.run(ve.tensor_tensor, GS[2], GS[0], PS[:, b + 2, :], ALU.mult)
        t = dv.run(ve.tensor_tensor, GS[1], GS[1], PS[:, b + 3, :], ALU.mult)
        bank_free[b] = bank_free[b + 1] = (t2,)
        bank_free[b + 2] = bank_free[b + 3] = (t,)
        dv.wait(t)
        t = dv.run(ve.tensor_tensor, Z[:, i, :], GS[2], GS[1], ALU.add)
        gs_free = t
    PO = [piece(A["wo"][i], 4096, (i, i * RING)) for i in range(2)]
    t_z = t
    pe.wait(t_z)
    for i in range(8):
        pe.wait(use(PO[i // 4]))
        claim(i)
        t = proj(pos(PO[i // 4], 8), 128 * (i % 4), 128, i, 0, XONLY, X=Z)
        if i % 4 == 3:
            release(PO[i // 4], pe.now())
        dv.wait(t)
        t = dv.run(ve.tensor_tensor, XT[:, i, META:TK], XT[:, i, META:TK], PS[:, i, :], ALU.add)
        bank_free[i] = (t,)
    barrier()


    o = O_TEMP + 2 * RING
    UT2 = at3(o, 8, T); o_ut2 = o; o += 8 * T
    UTOK = at3(o, 4, 1024); o_utok = o; o += 4096
    XR = [at(o + 1024 * i, 1024) for i in range(2)]; o += 2048
    XET = [at3(o + 1024 * i, 8, 128) for i in range(2)]; o += 2048
    o_w2x = o
    assert o + RING <= O_XT
    o = OW
    HS = [at(o + 256 * i, 256) for i in range(2)]; o += 512
    HT = [at3(o + 256 * i, 2, 128) for i in range(2)]; o += 512
    YS = [at(o + 512 * i, 512) for i in range(2)]; o += 1024
    MT = [at(o + 512 * i, 512) for i in range(2)]; o += 1024
    o_rt = o
    o = SMALL
    MOD = at(o, 48); o += 48
    ROW = at(o, 8).rearrange("p (n s) -> p n s", n=4); o += 8
    GATE = at(o, 8).rearrange("p (n s) -> p n s", n=4); o += 8
    XE = at(o, 32); o += 32
    FLAG = at(o, 1); o += 1
    S1 = at(o, 8); o += 8
    S2 = at(o, 8); o += 8
    SNK = at(o, 8); o += 8
    assert o <= O_WORK, (o, O_WORK)

    experts = []
    slots6 = [(0, 0), (1, RING), (2, 2 * RING), (3, 3 * RING), (4, O_TEMP), (5, O_TEMP + RING)]
    n_p = 2
    state[slots6[4]] = state[slots6[5]] = [q.now() for q in engines]
    PA = []

    def ada_piece():
        nonlocal n_p
        if len(PA) < 12:
            PA.append(piece(A["wada"][len(PA)], 4096, slots6[n_p % 6]))
            n_p += 1

    for e in range(32):
        ids = []
        for name in ("w1", "w3", "w2"):
            src = A[name][e].rearrange("(k p) n -> p k n", p=128)
            ids.append(piece(src, 4096, slots6[n_p % 6]))
            n_p += 1
        experts.append(ids)
        ada_piece()
    load_ready()

    s_sc = slot("scatter")

    def po_ind(n, i):
        s_sc.n += 16

        def emit(eng):
            eng.indirect_dma_start(out=xb, out_offset=bass.IndirectOffsetOnAxis(ap=ROW[:, n, i:i + 1].bitcast(U32), axis=0),
                                   in_=UTOK[:, n, :], in_offset=None).then_inc(s_sc.sem, 16)
        po.items.append(("call", emit))
        return s_sc.now()

    def gather(n, i):
        s_g[n].n += 16

        def emit(eng):
            eng.indirect_dma_start(out=GG[i][:, n, :], out_offset=None, in_=yb,
                                   in_offset=bass.IndirectOffsetOnAxis(ap=ROW[:, n, i:i + 1].bitcast(U32), axis=0),
                                   ).then_inc(s_g[n].sem, 16)
        po.items.append(("call", emit))
        return s_g[n].now()

    def toeplitz():
        for h in range(8):
            src = bass.AP(rs.tensor, 384 * h, [[1, 128], [1, 256]])
            t = sp.dma(sy.dma_start, BI[:, h, :], src, s_b)
        return t

    RT = o_rt
    WGR = at3(RT, 8, 36)
    BGR = at(RT + 288, 36)
    LG = at3(RT + 324, 4, 36)
    G8 = at3(RT + 468, 4, 8)
    GM = at3(RT + 500, 4, 8)
    GI = at3(RT + 532, 4, 8)
    EG = at3(RT + 564, 4, 4)
    GS4 = at(RT + 580, 4)
    MK = at3(RT + 584, 4, 4)
    EM = at3(RT + 600, 4, 32)
    EV = at3(RT + 728, 4, 8)
    EI = at3(RT + 760, 4, 8)
    IF_ = at3(RT + 792, 4, 2)
    OH = [at3(RT + 800 + 128 * i, 4, 32) for i in range(3)]
    RK = at3(RT + 1184, 4, 32)
    CN = at(RT + 1312, 32)
    XC = at(RT + 1344, 32)
    XP = at(RT + 1376, 32)
    B1 = at3(RT + 1408, 4, 32)
    B2 = at3(RT + 1536, 4, 32)
    TM = at(RT + 1664, 32)
    RF = at3(RT + 1696, 4, 2)
    NG = at(RT + 1704, 4)
    GF = at(RT + 1708, 4)
    assert RT + 1712 <= ARENA
    IO = CST[:, C_IOTA:C_IOTA + 128]

    s_rt = slot("rt")
    sp.dma(sy.dma_start, WGR, A["wgr"], s_rt)
    sp.dma(sy.dma_start, SNK, A["snk"], s_rt)
    t_rt = sp.dma(sy.dma_start, BGR, A["bgr"], s_rt)
    SQ2 = at3(OW, 2, T)
    RN2 = at(OW + 1024, T)
    t = norm(XT, META, T, UT2, V_FFN, SQ2, RN2, 0)
    for q in engines:
        q.wait(t, t_rt)
    for n in range(4):
        for k in range(8):
            t = mm(PS[:, 0, 36 * n:36 * n + 36], UT2[:, k, 128 * n:128 * n + 128], WGR[:, k, :], k == 0, k == 7, mark=k == 7)

    def d(method, *a, **kw):
        dv.wait(dv.now())
        return dv.run(method, *a, **kw)

    dv.wait(t)
    d(ve.tensor_tensor, LG, PS[:, 0, 0:144].rearrange("p (a b) -> p a b", a=4), BGR.unsqueeze(1).to_broadcast([128, 4, 36]),
      ALU.add)
    d(ve.memset, G8, -1.0e30)
    d(ve.tensor_copy, G8[:, :, 0:4], LG[:, :, 0:4])
    for n in range(4):
        d(ve.max, GM[:, n, :], G8[:, n, :])
        d(ve.max_index, GI[:, n, :].bitcast(U32), GM[:, n, :], G8[:, n, :])
    d(ve.tensor_copy, GF, GI[:, :, 0].bitcast(U32))
    t = d(ve.tensor_scalar, NG, GM[:, :, 0], -1.0, None, ALU.mult)
    ac.wait(t)
    for n in range(4):
        t = ac.run(se.activation, EG[:, n, :], LG[:, n, 0:4], ACT.Exp, bias=NG[:, n:n + 1], accum_out=GS4[:, n:n + 1])
    dv.wait(t)
    d(ve.reciprocal, GS4, GS4)
    d(ve.tensor_tensor, MK, IO[:, 0:4].unsqueeze(1).to_broadcast([128, 4, 4]), GF.unsqueeze(2).to_broadcast([128, 4, 4]),
      ALU.is_equal)
    mk8 = MK.unsqueeze(3).to_broadcast([128, 4, 4, 8])
    em = EM.rearrange("p n (g e) -> p n g e", g=4)
    d(ve.tensor_tensor, em, LG[:, :, 4:36].rearrange("p n (g e) -> p n g e", g=4), mk8, ALU.mult)
    d(ve.tensor_scalar, MK, MK, -1.0, 1.0e30, ALU.add, ALU.mult)
    d(ve.tensor_tensor, em, em, mk8, ALU.add)
    for n in range(4):
        d(ve.max, EV[:, n, :], EM[:, n, :])
        d(ve.max_index, EI[:, n, :].bitcast(U32), EV[:, n, :], EM[:, n, :])
    d(ve.tensor_copy, IF_, EI[:, :, 0:2].bitcast(U32))
    t = d(ve.tensor_tensor, NG, EV[:, :, 1], EV[:, :, 0], ALU.subtract)
    ac.wait(t)
    t = ac.run(se.activation, NG, NG, ACT.Exp)
    dv.wait(t)
    d(ve.tensor_scalar, GF, NG, 1.0, None, ALU.add)
    d(ve.reciprocal, GF, GF)
    d(ve.tensor_tensor, GATE[:, :, 0], GF, GS4, ALU.mult)
    d(ve.tensor_tensor, GATE[:, :, 1], GATE[:, :, 0], NG, ALU.mult)
    for i in range(2):
        d(ve.tensor_tensor, OH[i], IO[:, 0:32].unsqueeze(1).to_broadcast([128, 4, 32]),
          IF_[:, :, i:i + 1].to_broadcast([128, 4, 32]), ALU.is_equal)
    t = d(ve.tensor_tensor, OH[2], OH[0], OH[1], ALU.add)
    pe.wait(t)
    for n in range(4):
        for k in range(n):
            mm(PS[:, 1, 32 * n:32 * n + 32], ONE, OH[2][:, k, :], k == 0, False)
        mm(PS[:, 1, 32 * n:32 * n + 32], UP, OH[2][:, n, :], n == 0, True)
    for n in range(4):
        t = mm(PS[:, 2, 0:32], ONE, OH[2][:, n, :], n == 0, n == 3, mark=True)
    dv.wait(t)
    d(ve.tensor_copy, RK, PS[:, 1, 0:128].rearrange("p (a b) -> p a b", a=4))
    d(ve.tensor_copy, CN, PS[:, 2, 0:32])
    d(ve.tensor_scalar, XC, CN, float(CAP), None, ALU.is_gt)
    for m in range(2, (512 - 1) // CAP + 1):
        d(ve.tensor_scalar, TM, CN, float(CAP * m), None, ALU.is_gt)
        d(ve.tensor_tensor, XC, XC, TM, ALU.add)
    d(ve.tensor_tensor_scan, XP, ONE[:, 0:32], XC, 0.0, ALU.mult, ALU.add)
    d(ve.tensor_copy, FLAG.bitcast(U32), XP[:, 31:32])
    for i in range(NX):
        d(ve.tensor_scalar, TM, XP, float(i), None, ALU.is_le)
        d(ve.tensor_reduce, XE[:, i:i + 1], TM, AX, ALU.add)
    if True:
        d(ve.tensor_scalar, XE[:, 0:NX], XE[:, 0:NX], 31.0, None, ALU.min)
        d(ve.tensor_copy, XE[:, 0:NX].bitcast(U32), XE[:, 0:NX])
    d(ve.tensor_tensor, XP, XP, XC, ALU.subtract)
    d(ve.tensor_tensor, XP, XP, IO[:, 0:32], ALU.subtract)
    d(ve.tensor_scalar, XP, XP, 31.0, float(CAP), ALU.add, ALU.mult)
    d(ve.tensor_scalar, B1, RK, float(CAP), None, ALU.is_ge)
    d(ve.tensor_tensor, B1, B1, XP.unsqueeze(1).to_broadcast([128, 4, 32]), ALU.mult)
    d(ve.tensor_tensor, B1, B1, RK, ALU.add)
    d(ve.tensor_scalar, TM, IO[:, 0:32], float(CAP), None, ALU.mult)
    d(ve.tensor_tensor, B1, B1, TM.unsqueeze(1).to_broadcast([128, 4, 32]), ALU.add)
    for i in range(2):
        d(ve.tensor_tensor, B2, B1, OH[i], ALU.mult)
        d(ve.tensor_reduce, RF[:, :, i:i + 1], B2, AX, ALU.add)
    t_row = d(ve.tensor_copy, ROW.bitcast(U32), RF)
    for n in range(4):
        b = 4 + 2 * (n % 2)
        claim(b, b + 1)
        for k in range(8):
            t = turn(PS[:, b + k // 4, 128 * (k % 4):128 * (k % 4) + 128], UT2[:, k, 128 * n:128 * n + 128], mark=k == 7)
        t = evac(ac, UTOK[:, n, :].rearrange("p (a b) -> p a b", a=2), PS[:, b:b + 2, :], b, t)
        bank_free[b] = bank_free[b + 1] = (t,)
        po.wait(t, t_row, s_z.now())
        for i in range(2):
            t_sc = po_ind(n, i)
    barrier(t_sc)

    def expert(qs, w, rows, xt, x0, i, free, ysem):
        pe, ac, dv, sp = qs
        w1, w3, w2 = w

        def m2(out, l, r, start, stop):
            return pe.run(te.matmul, out, l, r, start=start, stop=stop, mark=stop, skip_group_check=True)

        b = 4 * i
        H1 = PS[:, b, 0:256]
        H3 = PS[:, b + 1, 0:256]
        if free["h"][i]:
            pe.wait(*free["h"][i])
        for wt, ho in ((w1, b), (w3, b + 1)):
            for k in range(8):
                for half in range(2):
                    t = m2(PS[64 * half:64 * half + CAP, ho, 0:256], xt[:, k, x0:x0 + CAP],
                           wt[:, k, 256 * half:256 * half + 256], k == 0, k == 7)
        if free["hs"][i]:
            ac.wait(*free["hs"][i])
            dv.wait(*free["hs"][i])
        ac.wait(t)
        dv.wait(t)
        hs = [slice(0, CAP), slice(64, 64 + CAP)] if CAP < 64 else [slice(0, 128)]
        for p in hs:
            t = ac.run(se.activation, HS[i][p, :], PS[p, b, 0:256], ACT.Silu)
        dv.wait(t)
        for p in hs:
            t = dv.run(ve.tensor_tensor, HS[i][p, :], HS[i][p, :], PS[p, b + 1, 0:256], ALU.mult)
        free["h"][i] = (t,)
        pe.wait(t)
        if free["t"][i]:
            pe.wait(*free["t"][i])
        for c in range(2):
            for p in hs:
                n = p.stop - p.start
                t = pe.run(te.transpose, PS[:, b + 2, 128 * c + p.start:128 * c + p.stop], HS[i][p, 128 * c:128 * c + 128],
                           CST[p, C_ID + p.start:C_ID + p.stop], mark=True)
                pe.wait(t)
        free["hs"][i] = (t,)
        dv.wait(t)
        for p in hs:
            t = dv.run(ve.tensor_copy, HT[i][:, :, p], PS[:, b + 2, 0:256].rearrange("p (a b) -> p a b", a=2)[:, :, p])
        free["t"][i] = (t,)
        pe.wait(t)
        if free["y"][i]:
            pe.wait(*free["y"][i])
        for kt in range(4):
            for half in range(2):
                t = m2(PS[64 * half:64 * half + CAP, b + 3, :], HT[i][:, kt % 2, 64 * (kt // 2):64 * (kt // 2) + CAP],
                       w2[:, kt, 512 * half:512 * half + 512], kt == 0, kt == 3)
        t_w = t
        ac.wait(t)
        if free["ys"][i]:
            ac.wait(*free["ys"][i])
        for p in hs:
            t = ac.run(se.activation, YS[i][p, :], PS[p, b + 3, :], ACT.Copy)
        free["y"][i] = (t,)
        sp.wait(t)
        for half in range(2):
            t = sp.dma(ge.dma_start if sp is po else sy.dma_start, yb[rows:rows + CAP, 512 * half:512 * half + 512],
                       YS[i][64 * half:64 * half + CAP, :], ysem[i])
        free["ys"][i] = (t,)
        return t_w

    SC8 = at(SMALL + 140, 8)
    assert SMALL + 148 <= O_WORK
    ac.wait(t_in)
    t_cond = ac.run(se.activation, SC8, VEC[:, V_COND:V_COND + 8], ACT.Silu)
    mt_free = [None, None]
    t_moda = []

    def ada(c):
        w = pos(PA[c], 8)
        m = MT[c % 2]
        dv.wait(use(PA[c]), t_cond)
        if mt_free[c % 2] is not None:
            dv.wait(mt_free[c % 2])
        d(ve.tensor_scalar, m, w[:, 0, :], SC8[:, 0:1], None, ALU.mult)
        for k in range(1, 8):
            t = d(ve.scalar_tensor_tensor, m, w[:, k, :], SC8[:, k:k + 1], m, ALU.mult, ALU.add)
        release(PA[c], t)
        pe.wait(t)
        claim(3)
        for i in range(4):
            t = mm(PS[:, 3, i:i + 1], m[:, 128 * i:128 * i + 128], ONE[:, 0:1], i == 0, i == 3, mark=i == 3)
        mt_free[c % 2] = t
        dv.wait(t)
        t = dv.run(ve.tensor_tensor, MOD[:, 4 * c:4 * c + 4], PS[:, 3, 0:4], VEC[:, V_BADA + 4 * c:V_BADA + 4 * c + 4], ALU.add)
        bank_free[3] = (t,)
        return t

    s_x = [slot(f"x{i}") for i in range(2)]
    s_y = [slot(f"y{i}") for i in range(2)]
    free = {k: [None, None] for k in ("h", "hs", "t", "y", "ys")}
    for b in range(8):
        bank_free[b] = None
    xr_free = [None, None]
    xt_free = [None, None]
    tx = {}

    def load_x(g):
        i = g % 2
        if xr_free[i] is not None:
            po.wait(*xr_free[i])
        tx[g] = po.dma(ge.dma_start, XR[i][0:2 * CAP, :], xb[2 * CAP * g:2 * CAP * g + 2 * CAP, :], s_x[i])

    load_x(0)
    load_x(1)
    for g in range(16):
        i = g % 2
        pe.wait(tx[g])
        for half in range(2):
            b = 4 * i + half
            f = free["h"][i]
            if f:
                pe.wait(*f)
            for k in range(4):
                kk = 4 * half + k
                t = turn(PS[:, b, 128 * k:128 * k + 2 * CAP], XR[i][0:2 * CAP, 128 * kk:128 * kk + 128], mark=k == 3)
            if xt_free[i]:
                (ac, dv)[half].wait(*xt_free[i])
            t2 = evac((ac, dv)[half], XET[i][:, 4 * half:4 * half + 4, 0:2 * CAP],
                      PS[:, b, :].rearrange("p (a b) -> p a b", a=4)[:, :, 0:2 * CAP], b, t)
            pe.wait(t2)
        xr_free[i] = (t,)
        if g + 2 < 16:
            load_x(g + 2)
        for x in range(2):
            e = 2 * g + x
            ids = experts[e]
            for y in ids:
                pe.wait(use(y))
            w = (pos(ids[0], 8), pos(ids[1], 8), pos(ids[2], 4))
            t = expert((pe, ac, dv, po), w, CAP * e, XET[i], CAP * x, x, free, s_y)
            for y in ids:
                release(y, t)
            if x == 1:
                xt_free[i] = (t,)
            if e < 12:
                pe.wait(*free["y"][0])
                t = ada(e)
                free["y"][0] = free["y"][0] + (t,)
    barrier(s_y[0].now(), s_y[1].now())

    if True:
        bq = [Queue(new_sem("b_" + n)) for n in ("pe", "act", "dve", "sp")]
        bsem = [Slot(new_sem(f"bw{i}")) for i in range(4)]
        bys = [Slot(new_sem(f"by{i}")) for i in range(2)]
        bfree = {k: [None, None] for k in free}
        WX = [at3(o_ut2, 8, 512), at3(o_utok, 8, 512), at3(o_w2x, 4, 1024)]
        bpe, bac, bdv, bsp = bq

        def load_block(i):
            def emit(eng):
                e = eng.value_load(XE[0:1, i:i + 1].bitcast(mybir.dt.int32), min_val=0, max_val=31)
                for j, name in enumerate(("w1", "w3", "w2")):
                    src = A[name][bass.ds(e, 1)].rearrange("o (k p) n -> p (o k) n", p=128)
                    eng.dma_start(out=WX[j], in_=src).then_inc(bsem[j].sem, 16)
            return emit

        for i in range(NX):
            if i:
                bsp.wait(t_w)
            bsp.items.append(("call", load_block(i)))
            for s in bsem[:3]:
                s.n += 16
            r0 = (32 + i) * CAP
            t = bsp.dma(sy.dma_start, XR[0][0:CAP, :], xb[r0:r0 + CAP, :], bsem[3])
            bpe.wait(t)
            for b in range(2):
                if bfree["h"][0]:
                    bpe.wait(*bfree["h"][0])
                for k in range(4):
                    kk = 4 * b + k
                    t = bpe.run(te.transpose, PS[:, b, 128 * k:128 * k + CAP], XR[0][0:CAP, 128 * kk:128 * kk + 128],
                                CST[0:CAP, C_ID:C_ID + CAP], mark=k == 3)
                bdv.wait(t)
                t = bdv.run(ve.tensor_copy, XET[0][:, 4 * b:4 * b + 4, 0:CAP],
                            PS[:, b, :].rearrange("p (a b) -> p a b", a=4)[:, :, 0:CAP])
                bpe.wait(t)
            for s in bsem[:3]:
                bpe.wait(s.now())
            t_w = expert((bpe, bac, bdv, bsp), WX, r0, XET[0], 0, 0, bfree, bys)
        for q in bq:
            q.wait(*[x.now() for x in bq[:3]], bys[0].now())

        def guard(queue):
            def emit(eng):
                v = eng.value_load(FLAG[0:1, :].bitcast(mybir.dt.int32), min_val=0, max_val=64)
                with eng.If(v > 0):
                    queue.flush(eng)
            return emit

        bpo = Queue(new_sem("b_pool"))
        bpo.wait(*[x.now() for x in bq[:3]], bys[0].now())
        for q, x in zip((pe, ac, dv, sp, po), bq + [bpo]):
            q.items.append(("call", guard(x)))

    GG = [at3(o_ut2 + 4096 * i, 4, 1024) for i in range(2)]
    s_g = [slot(f"g{i}") for i in range(4)]
    for n in range(4):
        for i in range(2):
            t = gather(n, i)
        dv.wait(t)
        d(ve.tensor_scalar, GG[0][:, n, :], GG[0][:, n, :], GATE[:, n, 0:1], None, ALU.mult)
        t = d(ve.scalar_tensor_tensor, GG[0][:, n, :], GG[1][:, n, :], GATE[:, n, 1:2], GG[0][:, n, :], ALU.mult, ALU.add)
        pe.wait(t)
        for k in range(8):
            t = turn(PS[:, k, 128 * n:128 * n + 128], GG[0][:, n, 128 * k:128 * k + 128], mark=k == 7)
    dv.wait(t)
    for k in range(8):
        t = dv.run(ve.tensor_tensor, XT[:, k, META:TK], XT[:, k, META:TK], PS[:, k, :], ALU.add)
        bank_free[k] = (t,)
    barrier()

    X = XT[:, :, META:TK]
    o = O_TEMP
    HN = at3(o, 8, T); o += 8 * T
    MIXED = at3(o, 8, T); o += 8 * T
    UC = at3(o, 4, 514); o += 2056
    YC = at3(o, 4, T); o += 2048
    Q2 = at3(o, 4, T); o += 2048
    K2 = at(o, T); o += T
    V2 = at3(o, 4, 128); o += 512
    BI = at3(o, 8, 256); o += 2048
    BIR = BI
    CB = at3(o, 4, T); o_cb = o; o += 2048
    YT2 = at3(o, 4, T); o += 2048
    assert o <= O_XT, o
    o = OW
    S8 = at3(o, 8, 256); o += 2048
    PT2 = [[at(o + 1024 * kc + 512 * g, 512) for g in range(2)] for kc in range(2)]; o += 2048
    SQ2 = at3(o, 2, T); o += 1024
    RN2 = at(o, T); o += 512
    ST = at(o, 40); o += 40
    RB8 = at(o, 8); o += 8
    HOT = at(o, 128); o += 128
    assert o <= ARENA
    RSC = AR[0:8, o_cb:o_cb + 384]

    key4 = [(i, i * RING) for i in range(4)]
    PW = [piece(A["win2"][i], 4096, key4[i % 4]) for i in range(4)]
    PW.append(piece(A["win2s"], 2048, key4[0]))
    PQ = [piece(A["wout2"][i], 4096, key4[1 + i]) for i in range(2)]
    PK = [piece(A["wq"][i], 4096, key4[(3 + i) % 4]) for i in range(4)]
    load_ready()

    rs = nc.dram_tensor("rs", [8, 384], F32, kind="Internal").ap()
    s_b = slot("bias")
    sp.dma(sy.dma_start, RB8[0:32, :], A["relb"], s_b)
    t = sp.dma(sy.dma_start, HOT[0:32, :], A["hot"], s_b)
    pe.wait(t)
    t = mm(PS[0:8, 7, 0:128], RB8[0:32, :], HOT[0:32, :], True, True, mark=True)
    dv.wait(t)
    d(ve.memset, RSC, -1.0e30)
    t = d(ve.tensor_copy, RSC[:, 127:255], PS[0:8, 7, 0:128])
    bank_free[7] = (t,)
    sp.wait(t)
    t = sp.dma(sy.dma_start, rs, RSC, s_b)
    sp.wait(t)
    t_bi = toeplitz()

    t = norm(XT, META, T, X, V_FIN, SQ2, RN2, 0)
    d(ve.tensor_scalar, S1, MOD[:, 8:16], 1.0, None, ALU.add)
    d(ve.tensor_tensor, S1, S1, VEC[:, V_N1:V_N1 + 8], ALU.mult)
    d(ve.tensor_scalar, S2, MOD[:, 32:40], 1.0, None, ALU.add)
    t = d(ve.tensor_tensor, S2, S2, VEC[:, V_N2:V_N2 + 8], ALU.mult)
    for q in engines:
        q.wait(t)

    def shifted_norm(U, g, shift):
        t = norm(XT, META, T, U, None, SQ2, RN2, 0, cols=g)
        ac.wait(t)
        for k in range(8):
            t = ac.run(se.activation, U[:, k, :], U[:, k, :], ACT.Identity, bias=MOD[:, shift + k:shift + k + 1])
        pe.wait(t)
        return t

    for b in range(8):
        bank_free[b] = (dv.now(),)
    shifted_norm(HN, S1, 0)

    dv.wait(t)
    t = d(ve.memset, UC[:, :, 0:2], 0.0)
    pe.wait(use(PW[0]))
    for j in range(4):
        claim(j)
        t = proj(pos(PW[0], 8), 128 * j, 128, j, 0, XONLY, X=HN)
        t = evac(ac, UC[:, j, 2:514], PS[:, j, :], j, t)
        bank_free[j] = (t,)
    release(PW[0], pe.now())
    pe.wait(use(PW[1]))
    for j in range(4):
        b = 4 + j
        claim(b)
        t = proj(pos(PW[1], 8), 128 * j, 128, b, 0, XONLY, X=HN)
        dv.wait(t, bank_free[j][0])
        t = dv.run(ve.tensor_tensor, UC[:, j, 2:514], UC[:, j, 2:514], PS[:, b, :], ALU.mult)
        bank_free[b] = (t,)
    release(PW[1], pe.now())
    pe.wait(use(PW[2]))
    for j in range(4):
        claim(j)
        tb = proj(pos(PW[2], 8), 128 * j, 128, j, 0, XONLY, X=HN)
        wc = [VEC[:, V_CONV + 4 * i + j:V_CONV + 4 * i + j + 1] for i in range(3)]
        d(ve.tensor_scalar, YC[:, j, :], UC[:, j, 0:T], wc[0], None, ALU.mult)
        for i in (1, 2):
            d(ve.scalar_tensor_tensor, YC[:, j, :], UC[:, j, i:T + i], wc[i], YC[:, j, :], ALU.mult, ALU.add)
        dv.wait(tb)
        t = d(ve.tensor_tensor, YC[:, j, :], YC[:, j, :], PS[:, j, :], ALU.mult)
        bank_free[j] = (t,)
    release(PW[2], pe.now())
    BLK = CST[:, C_BLK:C_BLK + 128]
    sqf = [None, None]
    seq = [0]

    def group_norm(x, out, gcol, scale=1.0):
        i = seq[0] % 2
        b = 6 + i
        seq[0] += 1
        if sqf[i] is not None:
            ac.wait(*sqf[i])
        ac.wait(dv.now())
        t = ac.run(se.activation, SQ2[:, i, :], x, ACT.Square)
        pe.wait(t)
        claim(b)
        t = mm(PS[:, b, :], BLK, SQ2[:, i, :], True, True, mark=True)
        dv.wait(t)
        t = dv.run(ve.tensor_scalar, SQ2[:, i, :], PS[:, b, :], 1.0, EPS, ALU.mult, ALU.add)
        bank_free[b] = (t,)
        ac.wait(t)
        t = ac.run(se.activation, SQ2[:, i, :], SQ2[:, i, :], ACT.Sqrt, scale=1.0)
        dv.wait(t)
        d(ve.reciprocal, SQ2[:, i, :], SQ2[:, i, :])
        if scale != 1.0:
            d(ve.tensor_scalar, SQ2[:, i, :], SQ2[:, i, :], scale, None, ALU.mult)
        t = d(ve.scalar_tensor_tensor, out, x, VEC[:, gcol:gcol + 1], SQ2[:, i, :], ALU.mult, ALU.mult)
        sqf[i] = (t,)
        return t

    pe.wait(use(PW[3]))
    for j in range(4):
        claim(j)
        t = proj(pos(PW[3], 8), 128 * j, 128, j, 0, XONLY, X=HN)
        t = evac(dv, Q2[:, j, :], PS[:, j, :], j, t)
        bank_free[j] = (t,)
    release(PW[3], pe.now())
    pe.wait(use(PW[4]))
    W = pos(PW[4], 8)
    claim(4)
    t = proj(W, 0, 128, 4, 0, XONLY, X=HN)
    t = evac(dv, K2, PS[:, 4, :], 4, t)
    bank_free[4] = (t,)
    claim(5)
    for n in range(4):
        for k in range(8):
            t = mm(PS[:, 5, 128 * n:128 * n + 128], HN[:, k, 128 * n:128 * n + 128], W[:, k, 128:256], k == 0, k == 7, mark=k == 7)
    t = evac(dv, V2, PS[:, 5, :].rearrange("p (a b) -> p a b", a=4), 5, t)
    bank_free[5] = (t,)
    release(PW[4], pe.now())
    for j in range(4):
        group_norm(Q2[:, j, :], Q2[:, j, :], V_QG, 0.125)
    t = group_norm(K2, K2, V_KG)
    for j in range(4):
        group_norm(YC[:, j, :], MIXED[:, j, :], V_CG + j)
    pe.wait(t)
    dv.wait(t_bi)
    s8_free = None
    pt_free2 = None
    for n in range(4):
        kc0 = 0 if n else 1
        nk = 128 * (2 - kc0)
        claim(0, 1, 2, 3)
        for h in range(8):
            j, g = h % 4, h // 4
            t = mm(PS[:, h // 2, 256 * (h % 2) + 128 * kc0:256 * (h % 2) + 256], Q2[64 * g:64 * g + 64, j, 128 * n:128 * n + 128],
                   K2[64 * g:64 * g + 64, 128 * n + 128 - nk:128 * n + 128], True, True, mark=True)
            if h in (3, 7):
                pe.wait(t)
        sc = S8[:, :, 128 * kc0:256]
        if s8_free is not None:
            dv.wait(s8_free)
        dv.wait(t)
        ps = PS[:, 0:4, :].rearrange("p b (a c) -> p (b a) c", a=2)[:, :, 128 * kc0:256]
        t = d(ve.tensor_tensor, sc, ps, BIR[:, :, 0:nk][:, :, ::-1], ALU.add)
        for b in range(4):
            bank_free[b] = (t,)
        d(ve.tensor_reduce, ST[:, 0:8], sc, AX, ALU.max)
        d(ve.tensor_tensor, ST[:, 0:8], ST[:, 0:8], SNK, ALU.max)
        d(ve.tensor_tensor, ST[:, 8:16], SNK, ST[:, 0:8], ALU.subtract)
        t = d(ve.tensor_scalar, ST[:, 0:8], ST[:, 0:8], -1.0, None, ALU.mult)
        ac.wait(t)
        ac.run(se.activation, ST[:, 16:24], ST[:, 8:16], ACT.Exp)
        for h in range(8):
            t = ac.run(se.activation, S8[:, h, 128 * kc0:256], S8[:, h, 128 * kc0:256], ACT.Exp, bias=ST[:, h:h + 1],
                       accum_out=ST[:, 24 + h:25 + h])
        dv.wait(t)
        d(ve.tensor_tensor, ST[:, 24:32], ST[:, 24:32], ST[:, 16:24], ALU.add)
        d(ve.reciprocal, ST[:, 24:32], ST[:, 24:32])
        t = d(ve.tensor_tensor, sc, sc, ST[:, 24:32].unsqueeze(2).to_broadcast([128, 8, nk]), ALU.mult)
        pe.wait(t)
        for kc in range(kc0, 2):
            for g in range(2):
                b = 4 + g
                claim(b)
                for j in range(4):
                    t = turn(PS[:, b, 128 * j:128 * j + 128], S8[:, 4 * g + j, 128 * kc:128 * kc + 128], mark=j == 3)
                s8_free = t
                q = (ac, dv)[g]
                if pt_free2 is not None:
                    q.wait(pt_free2)
                t = evac(q, PT2[kc][g], PS[:, b, :], b, t)
                bank_free[b] = (t,)
        pe.wait(ac.now(), dv.now())
        claim(7)
        for g in range(2):
            for kc in range(kc0, 2):
                t = mm(PS[64 * g:64 * g + 64, 7, :], V2[:, n - 1 + kc, 64 * g:64 * g + 64], PT2[kc][g], kc == kc0, kc == 1,
                       mark=True)
        pt_free2 = t
        t = evac(ac, YT2[:, :, 128 * n:128 * n + 128], PS[:, 7, :].rearrange("p (a b) -> p a b", a=4), 7, t)
        bank_free[7] = (t,)
    dv.wait(t)
    ac.wait(t)
    for j in range(4):
        t = group_norm(YT2[:, j, :], MIXED[:, 4 + j, :], V_AG + j)
    pe.wait(t)
    for i in range(8):
        b = i % 6
        pe.wait(use(PQ[i // 4]))
        claim(b)
        t = proj(pos(PQ[i // 4], 8), 128 * (i % 4), 128, b, 0, XONLY, X=MIXED)
        if i % 4 == 3:
            release(PQ[i // 4], pe.now())
        dv.wait(t)
        t = dv.run(ve.scalar_tensor_tensor, X[:, i, :], PS[:, b, :], MOD[:, 16 + i:17 + i], X[:, i, :], ALU.mult, ALU.add)
        bank_free[b] = (t,)
    barrier()

    H2 = at3(OW, 8, T)
    SQ2 = at3(O_TEMP, 2, T)
    RN2 = at(O_TEMP + 1024, T)
    shifted_norm(H2, S2, 24)
    xs = nc.dram_tensor("xs", [128, 8, 512], F32, kind="Internal").ap()
    s_xs = slot("xs")
    sp.wait(dv.now())
    t_xs = sp.dma(sy.dma_start, xs, X, s_xs)
    o = O_TEMP + 1536
    KEYS = at3(o, 16, 128); o += 2048
    QP = [at3(o + 2048 * i, 4, T) for i in range(2)]; o += 4096
    SS = [at3(o + 512 * i, 4, 128) for i in range(2)]; o += 1024
    SV = at(o, 1024).rearrange("p (n h k) -> p n h k", n=4, h=16); o += 1024
    SI = at(o, 1024).rearrange("p (n h k) -> p n h k", n=4, h=16); o += 1024
    SF = at(o, 1024).rearrange("p (n h k) -> p n h k", n=4, h=16); o += 1024
    CD = at(o, 256); o += 256
    CD2 = at(o, 256); o += 256
    TV = at(o, 512).rearrange("p (n h k) -> p n h k", n=4, h=8); o += 512
    TI = at(o, 512).rearrange("p (n h k) -> p n h k", n=4, h=8); o += 512
    PI = [at(o + 512 * i, 512).rearrange("p (n h k) -> p n h k", n=4, h=8) for i in range(2)]; o += 1024
    PX = at(o, 512).rearrange("p (n h k) -> p n h k", n=4, h=8); o += 512
    IAB = [at3(o + 512 * i, 4, 128) for i in range(2)]; o += 1024
    EQ = [at(o + 2048 * i, 2048).rearrange("p (h k i) -> p h k i", h=8, k=16) for i in range(2)]; o += 4096
    SMX = at(o, 32).rearrange("p (n h) -> p n h", n=4); o += 32
    assert o <= O_XT, o
    IT = [at(OW + 4096 + 512 * i, 512) for i in range(3)]
    s_k = slot("keys")
    t_keys = sp.dma(sy.dma_start, KEYS, A["keysT"], s_k)
    pe.wait(t_keys)

    def top16(src, tmp, v, idx):
        d(ve.max, v[:, 0:8], src)
        d(ve.max_index, idx[:, 0:8].bitcast(U32), v[:, 0:8], src)
        d(ve.match_replace, tmp, v[:, 0:8], src, -3.0e38)
        d(ve.max, v[:, 8:16], tmp)
        return d(ve.max_index, idx[:, 8:16].bitcast(U32), v[:, 8:16], tmp)

    qp_free = [None, None]
    ss_free = [None, None]
    c = 0
    for i in range(4):
        pe.wait(use(PK[i]))
        for f in range(4):
            claim(f)
            t = proj(pos(PK[i], 8), 128 * f, 128, f, 0, XONLY, X=H2)
            if qp_free[i % 2] is not None:
                ac.wait(qp_free[i % 2])
            t = evac(ac, QP[i % 2][:, f, :], PS[:, f, :], f, t)
            bank_free[f] = (t,)
        release(PK[i], pe.now())
        pe.wait(t)
        for n in range(4):
            b = 4 + n
            claim(b)
            for f in range(4):
                t = mm(PS[:, b, 128 * f:128 * f + 128], QP[i % 2][:, f, 128 * n:128 * n + 128], KEYS[:, 4 * i + f, :], True, True,
                       mark=True)
            qp_free[i % 2] = t
            s = SS[c % 2]
            if ss_free[c % 2] is not None:
                ac.wait(ss_free[c % 2])
            t = evac(ac, s, PS[:, b, :].rearrange("p (a b) -> p a b", a=4), b, t)
            bank_free[b] = (t,)
            dv.wait(t)
            for f in range(4):
                t = top16(s[:, f, :], CD[:, 0:128], SV[:, n, 4 * i + f, :], SI[:, n, 4 * i + f, :])
            ss_free[c % 2] = t
            c += 1
    d(ve.tensor_copy, SF, SI.bitcast(U32))
    for n in range(4):
        for h in range(8):
            va = SV[:, n, 2 * h, :].unsqueeze(2).to_broadcast([128, 16, 16])
            vb = SV[:, n, 2 * h + 1, :].unsqueeze(1).to_broadcast([128, 16, 16])
            d(ve.tensor_tensor, CD.rearrange("p (a b) -> p a b", a=16), va, vb, ALU.add)
            top16(CD, CD2, TV[:, n, h, :], TI[:, n, h, :])
    ti = TI.bitcast(U32)
    d(ve.tensor_scalar, PX.bitcast(U32), ti, 4, None, ALU.logical_shift_right)
    d(ve.tensor_copy, PI[0], PX.bitcast(U32))
    d(ve.tensor_scalar, PX.bitcast(U32), ti, 15, None, ALU.bitwise_and)
    d(ve.tensor_copy, PI[1], PX.bitcast(U32))
    io16 = IO[:, 0:16].unsqueeze(1).unsqueeze(1).to_broadcast([128, 8, 16, 16])
    for n in range(4):
        for s in range(2):
            e = EQ[s]
            d(ve.tensor_tensor, e, io16, PI[s][:, n].unsqueeze(3).to_broadcast([128, 8, 16, 16]), ALU.is_equal)
            sf = SF[:, n].rearrange("p (h s) k -> p h s k", s=2)[:, :, s, :].unsqueeze(2).to_broadcast([128, 8, 16, 16])
            d(ve.tensor_tensor, e, e, sf, ALU.mult)
            d(ve.tensor_reduce, IAB[s][:, n, :].rearrange("p (h k) -> p h k", h=8), e, AX, ALU.add)
    tvf = TV.rearrange("p n h k -> p (n h) k")
    smx = SMX.rearrange("p n h -> p (n h)")
    t = d(ve.tensor_tensor, PX.rearrange("p n h k -> p (n h) k"), tvf, TV.rearrange("p n h k -> p (n h) k")[:, :, 0:1].to_broadcast([128, 32, 16]),
          ALU.subtract)
    ac.wait(t)
    t = ac.run(se.activation, PX, PX, ACT.Exp)
    dv.wait(t)
    d(ve.tensor_reduce, smx, PX.rearrange("p n h k -> p (n h) k"), AX, ALU.add)
    d(ve.reciprocal, smx, smx)
    t = d(ve.tensor_tensor, PX.rearrange("p n h k -> p (n h) k"), PX.rearrange("p n h k -> p (n h) k"),
          smx.unsqueeze(2).to_broadcast([128, 32, 16]), ALU.mult)
    pe.wait(t)
    for s in range(3):
        claim(s)
        for n in range(4):
            src = IAB[s][:, n, :] if s < 2 else PX[:, n].rearrange("p h k -> p (h k)")
            t = turn(PS[:, s, 128 * n:128 * n + 128], src, mark=n == 3)
        t = evac(dv, IT[s], PS[:, s, :], s, t)
        bank_free[s] = (t,)
    barrier(t_xs)

    OG = 2 * RING
    HT_ = T // 2
    G = AR[:, OG:OG + 128 * HT_].rearrange("p (a t) -> p a t", a=128)
    assert OG + 128 * HT_ == O_XT
    o = O_XT
    NB = 4
    AH = [at3(o + 512 * i, 4, 128) for i in range(NB)]; o += 512 * NB
    BH = [at3(o + 512 * i, 4, 128) for i in range(NB)]; o += 512 * NB
    assert o <= O_CST
    GE = [at(O_XT + 256 * i, HT_) for i in range(4)]
    GP = [at(O_XT + 1024 + 256 * i, HT_) for i in range(4)]
    XH = at3(O_XT + 2048, 8, HT_)
    uv_key = [(i, 2048 * i) for i in range(4)]
    for k4 in uv_key:
        state[k4] = [q.now() for q in engines]
    PU = []
    for hf in range(2):
        for c in range(64):
            PU.append((piece(A["uT"][c], 2048, uv_key[2 * (c % 2)]), piece(A["v"][c], 2048, uv_key[2 * (c % 2) + 1])))
    load_ready()
    s_out = slot("out")
    for hf in range(2):
        ah_free = [None] * NB
        ah_made = [None] * NB
        for q4 in range(HT_ // 4):
            i = q4 % NB
            t0 = HT_ * hf + 4 * q4
            for q in (dv, po):
                if ah_free[i] is not None:
                    q.wait(ah_free[i])
            for x in range(4):
                ta = dv.run(ve.tensor_scalar, AH[i][:, x, :], IO, IT[0][:, t0 + x:t0 + x + 1], IT[2][:, t0 + x:t0 + x + 1],
                            ALU.is_equal, ALU.mult)
                tb = po.run(ge.tensor_scalar, BH[i][:, x, :], IO, IT[1][:, t0 + x:t0 + x + 1], None, ALU.is_equal)
            pe.wait(ta, tb)
            b = q4 % 8
            claim(b)
            for x in range(4):
                t = mm(PS[:, b, 128 * x:128 * x + 128], BH[i][:, x, :], AH[i][:, x, :], True, True, mark=x == 3)
            ah_free[i] = t
            q = ac
            t = evac(q, G[:, :, 4 * q4:4 * q4 + 4], PS[:, b, :].rearrange("p (x a) -> p a x", x=4), b, t)
            bank_free[b] = (t,)
        barrier()
        for b in range(8):
            bank_free[b] = None
        ge_free = [None] * 4
        gp_free = [None] * 4
        made = {}

        def first(a):
            c = PU[64 * hf + a // 2][0]
            pe.wait(use(c))
            u = pos(c, 16)
            b = a % 4
            claim(b)
            for k in range(8):
                t = mm(PS[:, b, 0:HT_], u[:, 8 * (a % 2) + k, :], H2[:, k, HT_ * hf:HT_ * hf + HT_], k == 0, k == 7, mark=k == 7)
            if a % 2 == 1:
                release(c, t)
            ac.wait(t)
            if ge_free[b] is not None:
                ac.wait(ge_free[b])
            t = ac.run(se.activation, GE[b], PS[:, b, 0:HT_], ACT.Gelu_apprx_tanh)
            bank_free[b] = (t,)
            dv.wait(t)
            if gp_free[b] is not None:
                dv.wait(gp_free[b])
            t = dv.run(ve.tensor_tensor, GP[b], GE[b], G[:, a, :], ALU.mult)
            ge_free[b] = t
            made[a] = t

        def second(a):
            c = PU[64 * hf + a // 2][1]
            pe.wait(use(c), made[a])
            v = pos(c, 2)[:, a % 2, :]
            for k in range(8):
                t = mm(PS[:, 4 + k // 2, HT_ * (k % 2):HT_ * (k % 2) + HT_], v[:, 128 * k:128 * k + 128], GP[a % 4],
                       a == 0 and k % 2 == 0, a == 127, mark=k == 7)
            gp_free[a % 4] = t
            if a % 2 == 1:
                release(c, t)
            return t

        first(0)
        first(1)
        for a in range(128):
            if a + 2 < 128:
                first(a + 2)
            t = second(a)
        sp.wait(dv.now())
        if hf:
            sp.wait(t_o)
        t_xh = sp.dma(sy.dma_start, XH, xs[:, :, HT_ * hf:HT_ * hf + HT_], s_xs)
        dv.wait(t, t_xh)
        for k in range(8):
            t = dv.run(ve.scalar_tensor_tensor, XH[:, k, :], PS[:, 4 + k // 2, HT_ * (k % 2):HT_ * (k % 2) + HT_],
                       MOD[:, 40 + k:41 + k], XH[:, k, :], ALU.mult, ALU.add)
        sp.wait(t)
        t_o = sp.dma(sy.dma_start, A["out"].rearrange("(k p) t -> p k t", p=128)[:, :, HT_ * hf:HT_ * hf + HT_], XH, s_out)
        barrier(t_o)
    sp.wait(t_o)
    block = ctx.enter_context(nc.Block())
    block.sync(sp.flush)
    block.tensor(pe.flush)
    block.scalar(ac.flush)
    block.vector(dv.flush)
    block.gpsimd(po.flush)



def layout(i):
    a = {k: np.asarray(v) for k, v in i.items()}
    f = np.float32
    c = np.ascontiguousarray
    o = {}
    o["xT"] = c(a["x"][0].T)
    o["metaT"] = c(a["meta_tokens"].T)
    w = a["w_in"][0]
    r = np.arange
    hd = lambda base, h: base + 64 * h
    QA, KA, VA, QB, CK, KRP, QI, KI, WI, GA, GB = 0, 512, 1024, 1536, 2048, 2176, 2192, 2704, 2768, 2776, 3800
    def nope(base):
        return np.concatenate([np.concatenate([hd(base, h) + 16 + r(48), hd(base, h) + r(16)]) for h in range(8)])
    sw = np.concatenate([8 + r(8), r(8)])
    def rope(base, step):
        return (np.concatenate([base + step * h + r(16) for h in range(8)]),
                np.concatenate([base + step * h + sw for h in range(8)]))
    rba, rbb = rope(QB, 64)
    kra, krb = rope(KRP, 0)
    ria, rib = rope(QI, 64)
    kin = np.concatenate([KI + 16 + r(48), KI + r(16)] * 2)
    main = np.concatenate([KA + r(512), QA + r(512), VA + r(512), nope(QB), rba, rbb, kra, krb, CK + r(128), kin,
                           ria, rib, nope(QI), GA + r(1024), GB + r(1024)])
    small = np.concatenate([KI + r(16), KI + sw, WI + r(8)])
    def tiles(m, n):
        k, nn = m.shape
        return c(m.reshape(k // 128, 128, nn // n, n).transpose(2, 1, 0, 3).reshape(nn // n, 128, -1))
    o["wp1"] = tiles(w[:, main], 512)
    o["wp1s"] = tiles(w[:, small], 40)[0]
    wk = np.zeros((128, 4, 128), f)
    uk = a["w_uk"][0].transpose(0, 2, 1)
    wk[0:48] = uk[0::2].transpose(1, 0, 2)
    wk[64:112] = uk[1::2].transpose(1, 0, 2)
    o["wukT"] = wk
    o["wuv"] = c(a["w_uv"][0].transpose(1, 0, 2))
    o["wupa"] = c(a["w_up_a"][0].reshape(4, 128, 1024).transpose(1, 0, 2))
    o["wupb"] = c(a["w_up_b"][0].reshape(4, 128, 1024).transpose(1, 0, 2))
    o["wo"] = tiles(a["w_o"][0], 512)
    inv = (f(500000.0) ** (-r(8).astype(f) / f(8))).astype(f)
    ang = r(528).astype(f)[:, None] * inv[None]
    p = r(128)
    o["cos"] = c(np.cos(ang)[:, p % 8].T.astype(f))
    o["sin"] = c((np.sin(ang)[:, p % 8].T * np.where((p // 8) % 2, 1, -1)[:, None]).astype(f))
    q = r(128)
    P_, Q_ = p[:, None], q[None]
    sel = np.zeros((128, 240), f); sel[:, 112:128] = -1
    blk = (P_ // 64 == Q_ // 64) / 64
    cst = [P_ == Q_, np.ones((128, 128)), -np.ones((128, 128)), -(P_ >= Q_).astype(f), P_ < Q_,
           -((P_ // 16 == Q_ // 16) & (P_ >= Q_)).astype(f), sel, P_ // 16 == r(8)[None], blk, Q_ + 0 * P_]
    o["cst"] = c(np.concatenate([x.astype(f) for x in cst], 1))
    col = lambda v: v.reshape(-1, 128).T
    o["vec"] = c(np.concatenate([col(x) for x in (
        a["norm_mix_g"][0], a["norm_ffn_g"][0], a["norm_final_g"], a["norm1_g_2"][0], a["norm2_g_2"][0], a["b_ada_2"][0],
        a["c_2"][0], a["conv_w_2"][0].reshape(-1), a["conv_out_g_2"][0], )], 1).astype(f))
    ag = a["attn_out_g_2"][0].reshape(8, 64)
    ag = np.concatenate([np.concatenate([ag[j], ag[j + 4]])[:, None] for j in range(4)], 1)
    qg = np.tile(a["q_norm_g_2"][0], 2)[:, None]; kg = np.tile(a["k_norm_g_2"][0], 2)[:, None]
    o["vec"] = c(np.concatenate([o["vec"], ag, qg, kg], 1))
    def rep(x): return c(np.broadcast_to(x[None], (128,) + x.shape).astype(f))
    gr = np.concatenate([a["w_group"][0], a["w_router"][0]], 1)
    o["wgr"] = tiles(gr, 36)[0]
    o["bgr"] = rep(np.concatenate([a["b_group"][0], a["b_router"][0]]))
    o["snk"] = rep(a["sinks_2"][0])
    o["wada"] = tiles(a["w_ada_2"][0], 512)
    w2i = a["w_in_2"][0]
    qp = np.concatenate([np.concatenate([1536 + 64 * j + r(64), 1536 + 64 * (j + 4) + r(64)]) for j in range(4)])
    o["win2"] = tiles(w2i[:, np.concatenate([512 + r(512), 1024 + r(512), r(512), qp])], 512)
    o["win2s"] = tiles(w2i[:, 2048:2304], 256)[0]
    rows = np.concatenate([r(512)] + [np.concatenate([512 + 64 * j + r(64), 512 + 64 * (j + 4) + r(64)]) for j in range(4)])
    o["wout2"] = tiles(a["w_out_2"][0][rows], 512)
    o["wq"] = tiles(a["peer_wq_2"][0], 512)
    o["keysT"] = c(a["peer_keys_2"][0].transpose(3, 1, 0, 2).reshape(128, 16, 128))
    o["relb"] = a["rel_bias_2"]
    d = np.maximum(r(128), 1).astype(f)
    big = 16 + (np.log(d / f(16)) / f(np.log(8.0)) * f(16)).astype(np.int32)
    bucket = np.where(r(128) < 16, r(128), np.minimum(big, 31))
    o["hot"] = c((r(32)[:, None] == bucket[None]).astype(f))
    u = a["peer_u_2"][0].reshape(64, 2, 128, 8, 128)
    o["uT"] = c(u.transpose(0, 4, 1, 3, 2).reshape(64, 128, 2048))
    v = a["peer_v_2"][0].reshape(64, 2, 128, 1024)
    o["v"] = c(v.transpose(0, 2, 1, 3).reshape(64, 128, 2048))
    o["w1"] = a["w1"][0]; o["w3"] = a["w3"][0]; o["w2"] = a["w2"][0]
    return o


def kernel(**inputs):
    import concourse.bacc as bacc
    from concourse.bass_utils import run_bass_kernel_spmd

    arrays = layout(inputs)
    nc = bacc.Bacc("TRN2", target_bir_lowering=False, num_devices=1)
    args = {}
    for name, a in arrays.items():
        args[name] = nc.dram_tensor(name, a.shape, mybir.dt.from_np(a.dtype), kind="ExternalInput").ap()
    args["out"] = nc.dram_tensor("out", (1024, 512), F32, kind="ExternalOutput").ap()
    program(nc, args)
    r = run_bass_kernel_spmd(nc, [arrays], core_ids=[0])
    return np.ascontiguousarray(r.results[0]["out"].T)[None]
```

```python
import numpy as np

import concourse.bass as bass
from concourse import mybir
from concourse.alu_op_type import AluOpType as ALU
from contextlib import ExitStack

F32 = mybir.dt.float32
F32R = mybir.dt.float32r
U32 = mybir.dt.uint32
ACT = mybir.ActivationFunctionType
AX = mybir.AxisListType.X

T = 512
META = 16
TK = T + META
EPS = 1e-6


class Queue:

    def __init__(self, sem):
        self.sem, self.n, self.items, self.seen = sem, 0, [], {}

    def wait(self, *marks):
        for sem, value in marks:
            if self.seen.get(id(sem), 0) < value:
                self.seen[id(sem)] = value
                self.items.append((None, sem, value, None))

    def run(self, method, *args, mark=True, **kw):
        if mark:
            self.n += 1
        self.items.append((method, args, kw, (self.sem, 1) if mark else None))
        return (self.sem, self.n)

    def dma(self, method, out, in_, slot, **kw):
        slot.n += 16
        kw["out"], kw["in_"] = out, in_
        self.items.append((method, (), kw, (slot.sem, 16)))
        return (slot.sem, slot.n)

    def now(self):
        return (self.sem, self.n)

    def flush(self, eng):
        for item in self.items:
            if item[0] is None:
                eng.wait_ge(item[1], item[2])
            elif item[0] == "call":
                item[1](eng)
            else:
                ins = item[0](*item[1], **item[2])
                if item[3] is not None:
                    ins.then_inc(*item[3])


class Slot:

    def __init__(self, sem):
        self.sem, self.n = sem, 0

    def now(self):
        return (self.sem, self.n)


ARENA = 53200
RING = 4096
O_TEMP = 16384
O_XT = 40960
O_CST = 45184
O_WORK = 47360

C_ID, C_ONE, C_NEG, C_TRI, C_UP, C_TRIM, C_SEL, C_M8, C_BLK, C_IOTA = (
    0, 128, 256, 384, 512, 640, 768, 1008, 1016, 1144)
C_N = 1272
V_MIX, V_FFN, V_FIN, V_N1, V_N2, V_BADA, V_COND, V_CONV, V_CG, V_AG, V_QG, V_KG = (
    0, 8, 16, 24, 32, 40, 88, 96, 108, 112, 116, 117)
V_N = 118


def program(nc, A):
    with ExitStack() as ctx:
        build(nc, A, ctx)


def build(nc, A, ctx):
    with nc.sbuf_tensor("arena", [128, ARENA], F32) as AR:
        pass
    PS = ctx.enter_context(nc.psum_tensor("psum", [128, 8, 512], F32))

    def new_sem(name):
        return ctx.enter_context(nc.semaphore(name))

    pe, ac, dv, po, sp = (Queue(new_sem("s_" + n)) for n in ("pe", "act", "dve", "pool", "sp"))
    engines = (pe, ac, dv, po)
    te, se, ve, ge, sy = nc.tensor, nc.scalar, nc.vector, nc.gpsimd, nc.sync

    def alias(off, words):
        with nc.sbuf_tensor(f"before_{off}_{words}", [128, off], F32):
            with nc.sbuf_tensor(f"rounded_{off}_{words}", [128, words], F32R) as r:
                return r

    def slot(name):
        return Slot(new_sem("d_" + name))

    def at(off, n):
        return AR[:, off:off + n]

    def at3(off, a, b):
        return AR[:, off:off + a * b].rearrange("p (a b) -> p a b", a=a)

    def mm(out, l, r, start, stop, mark=False):
        return pe.run(te.matmul, out, l, r, start=start, stop=stop, mark=mark, skip_group_check=True)

    def turn(out, i, mark=False):
        k = i.shape[0]
        return pe.run(te.transpose, out, i, CST[0:k, C_ID:C_ID + k], mark=mark)

    def barrier(*extra):
        marks = [q.now() for q in engines] + list(extra)
        for q in engines + (sp,):
            q.wait(*marks)

    ring_sem = [slot(f"ring{i}") for i in range(9)]
    pieces = []
    loaded = {}
    needs = {}

    def ring_at(s, width):
        return at(s * RING, width)

    def piece(src, width, s):
        pieces.append((src, width, s))
        return len(pieces) - 1

    state = {"next": 0}

    def load_ready():
        while state["next"] < len(pieces):
            src, width, (sem, off) = pieces[state["next"]]
            if (sem, off) in state and state[(sem, off)] is None:
                return
            mark = state.get((sem, off))
            if mark is not None:
                sp.wait(*mark)
            sp.wait(*needs.get(state["next"], ()))
            loaded[state["next"]] = sp.dma(sy.dma_start, at(off, width), src, ring_sem[sem])
            state[(sem, off)] = None
            state["next"] += 1

    def use(i):
        if i not in loaded:
            load_ready()
        return loaded[i]

    def release(i, *marks):
        _, _, key = pieces[i]
        state[key] = marks
        load_ready()

    def pos(i, kk):
        src, width, (sem, off) = pieces[i]
        return at3(off, kk, width // kk)

    XT = at3(O_XT, 8, TK)
    CST = at(O_CST, C_N)
    VEC = at(O_CST + C_N, V_N)
    SMALL = O_CST + C_N + V_N
    assert SMALL <= O_WORK
    ONE = CST[:, C_ONE:C_ONE + 128]
    NEG = CST[:, C_NEG:C_NEG + 128]
    TRI = CST[:, C_TRI:C_TRI + 128]
    UP = CST[:, C_UP:C_UP + 128]

    s_in = slot("in")
    s_misc = [slot(f"misc{i}") for i in range(8)]
    t_in = sp.dma(sy.dma_start, XT[:, :, 0:META], A["metaT"].rearrange("(k p) t -> p k t", p=128), s_in)
    t_in = sp.dma(sy.dma_start, XT[:, :, META:TK], A["xT"].rearrange("(k p) t -> p k t", p=128), s_in)
    t_in = sp.dma(sy.dma_start, CST, A["cst"], s_in)
    t_in = sp.dma(sy.dma_start, VEC, A["vec"], s_in)
    for q in engines:
        q.wait(t_in)

    PROJ = [piece(A["wp1"][i], 4096, (i % 4, (i % 4) * RING)) for i in range(7)]
    PSM = piece(A["wp1s"], 320, (3, 3 * RING))
    PA = [piece(A["wada"][i], 4096, (i % 4, (i % 4) * RING)) for i in range(12)]
    PG = [piece(A["wp1"][7 + i], 4096, (i % 2, (i % 2) * RING)) for i in range(4)]
    PUP = [piece(A[name], 4096, (i, i * RING)) for i, name in enumerate(("wupa", "wupb"))]
    MOD = at(SMALL, 48)
    SC8 = at(SMALL + 140, 8)
    assert SMALL + 148 <= O_WORK
    t_cond = ac.run(se.activation, SC8, VEC[:, V_COND:V_COND + 8], ACT.Silu)

    o = O_TEMP
    UT = at3(o, 8, TK); o += 8 * TK
    KA = at3(o, 4, TK); o += 4 * TK
    QA = at3(o, 4, T); o += 4 * T
    VA = at3(o, 4, T); o += 4 * T
    QLAT = at3(o, 8, T); o_qlat = o; o += 8 * T
    QI = at3(o, 4, T); o_qi = o; o += 4 * T
    KI = at(o, TK); o += TK
    CKT = at(o, TK); o += TK
    CKV = at3(o, 5, 128); o += 640
    RB = at(o, T); o += T
    KR = at(o, TK); o += TK
    WI = at3(o, 4, 8); o += 32
    WUK = at3(o, 4, 128); o += 512
    WUV = at3(o, 8, 64); o += 512
    KMB = at3(o, 4, 128); o += 512
    VM2 = at(o, T); o += T
    PM = at(o, T); o += T
    YA = at3(o, 4, T); o += 4 * T
    assert o <= O_XT, o
    OW = O_WORK
    SQ = at3(o_qi, 4, TK)
    RN = at(OW, TK)
    COS = at(OW + TK, TK)
    SIN = at(OW + 2 * TK, TK)
    T1 = at(OW + 3 * TK, TK)
    T2 = at(OW + 4 * TK, TK)
    QBN = at3(o_qlat, 4, T)
    s_w = slot("w")
    t_tab = sp.dma(sy.dma_start, COS, A["cos"], s_w)
    t_tab = sp.dma(sy.dma_start, SIN, A["sin"], s_w)
    t_tab = sp.dma(sy.dma_start, WUK, A["wukT"], s_w)
    t_tab = sp.dma(sy.dma_start, WUV, A["wuv"], s_w)
    load_ready()

    def halves(n):
        return [(0, n)] if n <= 512 else [(0, n // 2), (n // 2, n - n // 2)]

    def norm(X, c0, n, U, gcol, squares, r, bank, cols=None):
        hs = halves(n)
        done = []
        sq_free = {}
        for k in range(8):
            b = k % squares.shape[1]
            s = squares[:, b, 0:n]
            x = X[:, k, c0:c0 + n]
            if k % 2 == 0:
                if b in sq_free:
                    ac.wait(sq_free[b])
                t = ac.run(se.activation, s, x, ACT.Square)
            else:
                if b in sq_free:
                    po.wait(sq_free[b])
                t = po.run(ge.tensor_tensor, s, x, x, ALU.mult)
            pe.wait(t)
            for i, (a, w) in enumerate(hs):
                t = mm(PS[:, bank + i, 0:w], ONE, s[:, a:a + w], k == 0, k == 7, mark=True)
            sq_free[b] = t
        dv.wait(t)
        for i, (a, w) in enumerate(hs):
            t = dv.run(ve.tensor_scalar, r[:, a:a + w], PS[:, bank + i, 0:w], 1.0 / 1024, EPS, ALU.mult, ALU.add)
        ac.wait(t)
        t = ac.run(se.activation, r[:, 0:n], r[:, 0:n], ACT.Sqrt)
        dv.wait(t)
        t = dv.run(ve.reciprocal, r[:, 0:n], r[:, 0:n])
        dv.wait(t)
        for k in range(8):
            t = dv.run(ve.scalar_tensor_tensor, U[:, k, 0:n], X[:, k, c0:c0 + n], (VEC[:, gcol + k:gcol + k + 1] if cols is None else cols[:, k:k + 1]),
                       r[:, 0:n], ALU.mult, ALU.mult)
        return t

    t_ut = norm(XT, 0, TK, UT, V_MIX, SQ, RN, 0)
    pe.wait(t_ut)

    def proj(W, c, m, b, p0, hs, X=None, base=0, kk=8):
        X = UT if X is None else X
        for i, (a, w) in enumerate(hs):
            for k in range(kk):
                t = mm(PS[p0:p0 + m, b + i, 0:w], W[:, k, c:c + m], X[:, k, base + a:base + a + w],
                       k == 0, k == kk - 1, mark=(k == kk - 1))
        return t

    FULL = halves(TK)
    XONLY = [(0, T)]
    bank_free = [None] * 8

    def claim(*banks):
        for b in banks:
            if bank_free[b] is not None:
                pe.wait(*bank_free[b])

    def evac(q, out, in_, b, t, scale=None):
        q.wait(t)
        if q is ac:
            t = ac.run(se.activation, out, in_, ACT.Copy, scale=1.0 if scale is None else scale)
        elif scale is None:
            t = dv.run(ve.tensor_copy, out, in_)
        else:
            t = dv.run(ve.tensor_scalar, out, in_, scale, None, ALU.mult)
        return t

    ZERO = at(O_XT - 512, 512)
    s_z = slot("z")
    CAP = 64
    NX = (1024 - 32) // CAP
    ROWS = 32 * CAP + NX * CAP
    xb = nc.dram_tensor("xb", [ROWS, 1024], F32, kind="Internal").ap()
    yb = nc.dram_tensor("yb", [ROWS, 1024], F32, kind="Internal").ap()
    t = dv.run(ve.memset, ZERO, 0.0)
    sp.wait(t)
    n0 = NX * CAP * 2 // 128
    ybt = yb.rearrange("r (a c) -> (r a) c", a=2)[64 * CAP:2 * ROWS, :]
    sp.dma(sy.dma_start, ybt[0:128 * n0, :].rearrange("(n p) c -> p n c", p=128), ZERO.unsqueeze(1).to_broadcast([128, n0, 512]), s_z)
    if NX * CAP * 2 > 128 * n0:
        sp.dma(sy.dma_start, ybt[128 * n0:, :], ZERO[0:NX * CAP * 2 - 128 * n0, :], s_z)
    nz = ROWS * 2 // 128
    sp.dma(sy.dma_start, xb.rearrange("r (a c) -> (r a) c", a=2)[0:128 * nz, :].rearrange("(n p) c -> p n c", p=128),
           ZERO.unsqueeze(1).to_broadcast([128, nz, 512]), s_z)
    if ROWS * 2 > 128 * nz:
        sp.dma(sy.dma_start, xb.rearrange("r (a c) -> (r a) c", a=2)[128 * nz:2 * ROWS, :], ZERO[0:2 * ROWS - 128 * nz, :], s_z)

    pe.wait(use(PROJ[0]))
    for j in range(4):
        b = 2 * j
        claim(b, b + 1)
        t = proj(pos(PROJ[0], 8), 128 * j, 128, b, 0, FULL)
        t = evac((ac, dv)[j % 2], KA[:, j, :].rearrange("p (a b) -> p a b", a=2), PS[:, b:b + 2, 0:264], b, t)
        bank_free[b] = bank_free[b + 1] = (t,)
    release(PROJ[0], pe.now())
    t_ka = (ac.now(), dv.now())
    pe.wait(use(PROJ[1]))
    for j in range(4):
        claim(j)
        t = proj(pos(PROJ[1], 8), 128 * j, 128, j, 0, XONLY, base=META)
        t = evac((ac, dv)[j % 2], QA[:, j, :], PS[:, j, :], j, t, scale=0.125)
        bank_free[j] = (t,)
    release(PROJ[1], pe.now())
    pe.wait(use(PROJ[2]))
    W = pos(PROJ[2], 8)
    for j in range(4):
        claim(4 + j)
        for k in range(8):
            t = mm(PS[:, 4 + j, :], UT[:, k, META + 128 * j:META + 128 * j + 128], W[:, k, :], k == 0, k == 7, mark=k == 7)
        t = evac((ac, dv)[j % 2], VA[:, j, :], PS[:, 4 + j, :], 4 + j, t)
        bank_free[4 + j] = (t,)
    UR = at3(OW + 3 * TK, 8, 128)
    dv.wait(t_ut)
    t = dv.run(ve.tensor_copy, UR.rearrange("p k (r m) -> p k r m", r=8),
               UT[:, :, 0:META].unsqueeze(2).to_broadcast([128, 8, 8, META]))
    pe.wait(t)
    claim(0)
    for k in range(8):
        t = mm(PS[:, 0, :], UR[:, k, :], W[:, k, :], k == 0, k == 7, mark=k == 7)
    release(PROJ[2], pe.now())
    VM = at(o_qlat + 4 * T, T)
    dv.wait(t)
    t = dv.run(ve.tensor_tensor, VM.rearrange("p (h d) -> p h d", h=8), PS[:, 0, :].rearrange("p (h d) -> p h d", h=8),
               CST[:, C_M8:C_M8 + 8].unsqueeze(2).to_broadcast([128, 8, 64]), ALU.mult)
    bank_free[0] = (t,)
    pe.wait(use(PROJ[3]))
    for j in range(4):
        b = (1, 2, 3, 4)[j]
        claim(b)
        t = proj(pos(PROJ[3], 8), 128 * j, 128, b, 0, XONLY, base=META)
        t = evac((ac, dv)[j % 2], QBN[:, j, :], PS[:, b, :], b, t, scale=0.125)
        bank_free[b] = (t,)
    release(PROJ[3], pe.now())

    dv.wait(t_tab)

    def rotated(W, ca, cb, m, hs, base, b, out, scale=1.0):
        n = sum(w for _, w in hs)
        nb = len(hs)
        w = n // nb
        claim(*range(b, b + 2 * nb))
        proj(W, ca, m, b, 0, hs, base=base)
        t = proj(W, cb, m, b + nb, 0, hs, base=base)
        dv.wait(t)
        co, si = (x[0:m, base:base + n].rearrange("p (a b) -> p a b", a=nb) for x in (COS, SIN))
        t1, t2, ou = (x[0:m, 0:n].rearrange("p (a b) -> p a b", a=nb) for x in (T1, T2, out))
        dv.run(ve.scalar_tensor_tensor, t1, PS[0:m, b:b + nb, 0:w], scale, co, ALU.mult, ALU.mult)
        t = dv.run(ve.scalar_tensor_tensor, t2, PS[0:m, b + nb:b + 2 * nb, 0:w], scale, si, ALU.mult, ALU.mult)
        for i in range(b, b + 2 * nb):
            bank_free[i] = (t,)
        dv.wait(t)
        return dv.run(ve.tensor_tensor, ou, t1, t2, ALU.add)

    pe.wait(use(PROJ[4]))
    W = pos(PROJ[4], 8)
    dv.wait(t)
    t = rotated(W, 0, 128, 128, XONLY, META, 0, RB, 0.125)
    dv.wait(t)
    t = rotated(W, 256, 384, 128, FULL, 0, 4, KR)
    t_kr = t
    release(PROJ[4], pe.now())
    pe.wait(use(PROJ[5]))
    W = pos(PROJ[5], 8)
    claim(2, 3)
    t = proj(W, 0, 128, 2, 0, FULL)
    t = evac(ac, CKT.rearrange("p (a b) -> p a b", a=2), PS[:, 2:4, 0:264], 2, t)
    bank_free[2] = bank_free[3] = (t,)
    claim(0)
    for i in range(4):
        for k in range(8):
            t = mm(PS[:, 0, 128 * i:128 * i + 128], UT[:, k, 128 * i:128 * i + 128], W[:, k, 0:128], k == 0, k == 7,
                   mark=k == 7)
    t = evac(dv, CKV[:, 0:4, :], PS[:, 0, :].rearrange("p (a b) -> p a b", a=4), 0, t)
    bank_free[0] = (t,)
    claim(1)
    for k in range(8):
        t = mm(PS[0:16, 1, 0:128], UT[:, k, 512:528], W[:, k, 0:128], k == 0, k == 7, mark=k == 7)
    t = evac(dv, CKV[0:16, 4, :], PS[0:16, 1, 0:128], 1, t)
    bank_free[1] = (t,)
    claim(4, 5)
    t = proj(W, 128, 128, 4, 0, FULL)
    t_kin = evac(ac, KI.rearrange("p (a b) -> p a b", a=2), PS[:, 4:6, 0:264], 4, t)
    bank_free[4] = bank_free[5] = (t_kin,)
    dv.wait(t_kr)
    RI = at(OW, T)
    t_ri = rotated(W, 256, 384, 128, XONLY, META, 6, RI)
    release(PROJ[5], pe.now())
    pe.wait(use(PROJ[6]))
    for j in range(4):
        claim(j)
        t = proj(pos(PROJ[6], 8), 128 * j, 128, j, 0, XONLY, base=META)
        t = evac((ac, dv)[j % 2], QI[:, j, :], PS[:, j, :], j, t)
        bank_free[j] = (t,)
    t_qin = (ac.now(), dv.now())
    release(PROJ[6], pe.now())
    pe.wait(use(PSM))
    W = pos(PSM, 8)
    dv.wait(t_ri)
    RK = at(OW + 5 * TK, TK)
    t_rk = rotated(W, 0, 16, 16, FULL, 0, 4, RK)
    claim(0)
    for i in range(4):
        for k in range(8):
            t = mm(PS[:, 0, 8 * i:8 * i + 8], UT[:, k, META + 128 * i:META + 128 * i + 128], W[:, k, 32:40], k == 0, k == 7,
                   mark=k == 7)
    t_wi = evac(dv, WI, PS[:, 0, 0:32].rearrange("p (a b) -> p a b", a=4), 0, t)
    bank_free[0] = (t_wi,)
    release(PSM, pe.now())
    sp.wait(t_kin, t_ri, t_rk, *t_qin)
    for h in range(8):
        p0 = 64 * (h % 2) + 48
        t_rot = sp.dma(sy.dma_start, QI[p0:p0 + 16, h // 2, :], RI[16 * h:16 * h + 16, :], s_w)
    t_rot = sp.dma(sy.dma_start, KI[48:64, :], RK[0:16, :], s_w)
    t_rot = sp.dma(sy.dma_start, KI[112:128, :], RK[0:16, :], s_w)
    pe.wait(t_tab)
    for q in (ac, dv):
        pe.wait(q.now())
    claim(*range(8))
    for h in range(8):
        p0 = 64 * (h % 2)
        t = mm(PS[:, h, :], WUK[p0:p0 + 48, h // 2, :], QBN[p0:p0 + 48, h // 2, :], True, True, mark=True)
    t_all = t
    dv.wait(t_all)
    t_vm = dv.run(ve.tensor_copy, VM2, VM)
    VM = VM2
    ac.wait(t_all, t_vm)
    dv.wait(t_vm)
    for h in range(8):
        t = evac((ac, dv)[h % 2], QLAT[:, h, :], PS[:, h, :], h, t_all)
        bank_free[h] = (t,)
    for q in engines:
        q.wait(t_rot)
    barrier()

    ac.run(se.preload_act_table_set, "natural_log_exp_and_others", mark=False)
    t = po.run(ge.memset, KMB, 0.0)
    po.wait(t)
    for h in range(8):
        p0 = 64 * (h % 2)
        t_kmb = po.run(ge.tensor_copy, KMB[p0:p0 + 64, h // 2, 16 * h:16 * h + 16], KA[p0:p0 + 64, h // 2, 0:META])
    ada_done = []

    def ada_steps():
        dv.wait(t_cond)
        for c in range(12):
            w = pos(PA[c], 8)
            dv.wait(use(PA[c]))
            t = dv.run(ve.tensor_scalar, w[:, 0, :], w[:, 0, :], SC8[:, 0:1], None, ALU.mult)
            yield
            for k in range(1, 8):
                dv.wait(t)
                t = dv.run(ve.scalar_tensor_tensor, w[:, 0, :], w[:, k, :], SC8[:, k:k + 1], w[:, 0, :], ALU.mult, ALU.add)
                if k < 7:
                    yield
            ada_done.append((c, t))
            yield

    def ada_sums(b):
        if not ada_done:
            return
        claim(b)
        c0, n = ada_done[0][0], len(ada_done)
        for c, t in ada_done:
            pe.wait(t)
            for i in range(4):
                t = mm(PS[:, b, 4 * (c - c0) + i:4 * (c - c0) + i + 1], pos(PA[c], 8)[:, 0, 128 * i:128 * i + 128], ONE[:, 0:1],
                       False, True, mark=i == 3)
            release(PA[c], t)
        ada_done.clear()
        dv.wait(t)
        t = dv.run(ve.tensor_tensor, MOD[:, 4 * c0:4 * (c0 + n)], PS[:, b, 0:4 * n],
                   VEC[:, V_BADA + 4 * c0:V_BADA + 4 * (c0 + n)], ALU.add)
        bank_free[b] = (t,)

    ada = ada_steps()
    NQ = [T - 128 * kt for kt in range(4)]
    OFF = [0, 512, 896, 1152]

    def by_tile(off):
        return [AR[:, off + OFF[kt]:off + OFF[kt] + NQ[kt]] for kt in range(4)]

    EX = [by_tile(OW + 1280 * i) for i in range(2)]
    PT = [by_tile(OW + 2560 + 1280 * i) for i in range(2)]

    def softplus(z, e, out, p, marks):
        ac.wait(*marks)
        t = ac.run(se.activation, e, z, ACT.Abs)
        ac.wait(t)
        t = ac.run(se.activation, e, e, ACT.Exp, scale=-1.0)
        ac.wait(t)
        t = ac.run(se.activation, e, e, ACT.Ln, bias=1.0)
        dv.wait(t)
        t = dv.run(ve.scalar_tensor_tensor, out, z, 0.0, e, ALU.max, ALU.add)
        for _ in range(3):
            next(ada, None)
        return t

    def strict(x, t):
        po.wait(t)
        return po.run(ge.affine_select, out=x, in_=x, pattern=[[1, 128]], compare_op=ALU.is_gt, fill=0.0,
                      base=0, channel_multiplier=-1)

    pe.wait(t_kmb)
    claim(7)
    for j in range(4):
        t = mm(PS[:, 7, :], KMB[:, j, :], QA[:, j, :], j == 0, False, mark=j == 3)
    EM = EX[1][0]
    t_pm = softplus(PS[:, 7, :], EM, PM, 128, (t,))
    pe.wait(t_pm)
    t = mm(PS[:, 7, :], CST[:, C_TRIM:C_TRIM + 128], PM, False, False, mark=True)
    ex_free = [None, (t_pm,)]
    pt_free = [None, None]
    tps = {}

    def region(i, kt, a):
        return PS[:, 3 * i + 1, 0:128] if kt == 3 else PS[:, 3 * i + kt, a:T]

    def scores(h):
        i, j, p0 = h % 2, h // 2, 64 * (h % 2)
        claim(3 * i, 3 * i + 1, 3 * i + 2)
        ts = []
        for kt in range(4):
            c = META + 128 * kt
            ts.append(mm(region(i, kt, 128 * kt), KA[p0:p0 + 64, j, c:c + 128], QA[p0:p0 + 64, j, 128 * kt:T], kt < 3, False,
                         mark=True))
        yield
        for x in (ex_free[i], pt_free[i]):
            if x is not None:
                ac.wait(*x)
                dv.wait(*x)
        for kt in range(4):
            t = softplus(region(i, kt, 128 * kt), EX[i][kt], PT[i][kt], 128,
                         (ts[3 if kt == 1 else kt],) + ((t_1,) if kt == 3 else ()))
            if kt == 1:
                t_1 = t
            tps[h, kt] = strict(PT[i][kt][:, 0:128], t)
            yield

    for _ in scores(0):
        pass
    for h in range(8):
        i, j, p0 = h % 2, h // 2, 64 * (h % 2)
        following = scores(h + 1) if h < 7 else iter(())
        next(following, None)
        ta = []
        for kt in (3, 2, 1, 0):
            pe.wait(tps[h, kt])
            mm(region(i, kt, 128 * kt), TRI, PT[i][kt], False, kt == 3, mark=kt == 3)
            for k2 in range(kt + 1, 4):
                mm(region(i, kt, 128 * k2), NEG, PT[i][k2], False, k2 == 3, mark=k2 == 3)
            t = pe.now()
            next(following, None)
            ac.wait(t)
            for x in {3: (), 2: (2,), 1: (3, 1), 0: (0,)}[kt]:
                t = ac.run(se.activation, EX[i][x], region(i, x, 128 * x), ACT.Exp)
                bank_free[3 * i + x % 3 if x < 3 else 3 * i + 1] = (t,)
                ta.append((x, strict(EX[i][x][:, 0:128], t)))
        sel = CST[:, C_SEL + 112 - 16 * h:C_SEL + 240 - 16 * h]
        for kt in range(4):
            t = mm(PS[:, 7, 128 * kt:T], sel, PT[i][kt], False, h == 7 and kt == 3, mark=True)
        pt_free[i] = (t,)
        ada_sums(3 * i + 2)
        if h % 2 == 0:
            claim(6)
        for kt, t in sorted(ta):
            pe.wait(t)
            t = mm(PS[p0:p0 + 64, 6, 128 * kt:T], VA[:, kt, 64 * h:64 * h + 64], EX[i][kt], kt == 0, kt == 3, mark=kt == 3)
        ex_free[i] = (t,)
        if h % 2 == 1:
            dv.wait(t)
            t = dv.run(ve.tensor_copy, YA[:, j, :], PS[:, 6, :])
            bank_free[6] = (t,)
    for _ in ada:
        pass
    ada_sums(5)
    ac.wait(pt_free[1][0], pt_free[0][0])
    t = ac.run(se.activation, PM, PS[:, 7, :], ACT.Exp)
    bank_free[7] = (t,)
    pe.wait(t)
    for j in range(4):
        claim(j)
        t = mm(PS[:, j, :], VM2[:, 128 * j:128 * j + 128], PM, True, True, mark=True)
        dv.wait(t, dv.now())
        t = dv.run(ve.tensor_tensor, YA[:, j, :], YA[:, j, :], PS[:, j, :], ALU.add)
        bank_free[j] = (t,)
    barrier()

    OLAT = at3(O_TEMP + 8 * TK, 8, T)
    YB = QI
    o_va = O_TEMP + 8 * TK + 4 * TK + 4 * T
    RS = [at(o_va + TK * i, TK) for i in range(2)]
    QM = at3(o_va + 2 * TK, 4, 128)
    P = at3(OW, 4, TK)
    PTR = at3(OW + 4 * TK, 5, 512)
    SC = at(OW + 4 * TK + 2560, TK)
    MB = at(OW + 5 * TK + 2560, TK)
    o = OW + 6 * TK + 2560
    M8 = at(o, 8)
    MX = at(o + 8, 4)
    SM = at(o + 12, 4)
    assert o + 16 <= ARENA
    rs_free = [None, None]
    GAB = at3(2 * RING, 16, T)
    pending = []
    n_gate = [0]

    def gates(*banks):
        for b in banks:
            while pending:
                bb, gg, t = pending.pop()
                t = evac(ac, GAB[:, gg, :], PS[:, bb, :], bb, t)
                bank_free[bb] = (t,)
            i = n_gate[0]
            if i < 16:
                n_gate[0] += 1
                claim(b)
                pe.wait(use(PG[i // 4]))
                t = proj(pos(PG[i // 4], 8), 128 * (i % 4), 128, b, 0, XONLY, base=META)
                if i % 4 == 3:
                    release(PG[i // 4], t)
                pending.append((b, i, t))

    for n in range(4):
        nk = META + 128 * (n + 1)
        np_ = 1 if nk <= 512 else 2
        w = nk // np_
        ks = [(i * w, w) for i in range(np_)]
        q0 = 128 * n

        def view(x):
            return x[:, 0:nk].rearrange("p (a b) -> p a b", a=np_)

        def bank(b):
            return PS[:, b:b + np_, 0:w]

        sc = view(SC)
        for h in range(8):
            j, p0, b = h // 2, 64 * (h % 2), 2 * (h % 2)
            claim(*range(b, b + np_))
            for i, (a, ww) in enumerate(ks):
                t = mm(PS[:, b + i, 0:w], QI[p0:p0 + 64, j, q0:q0 + 128], KI[p0:p0 + 64, a:a + w], True, True, mark=True)
            r = view(RS[h % 2])
            if rs_free[h % 2] is not None:
                ac.wait(rs_free[h % 2])
            ac.wait(t)
            t = ac.run(se.activation, r, bank(b), ACT.Relu)
            for x in range(b, b + np_):
                bank_free[x] = (t,)
            dv.wait(t, dv.now())
            if h == 0:
                t = dv.run(ve.tensor_scalar, sc, r, WI[:, n, h:h + 1], None, ALU.mult)
            else:
                t = dv.run(ve.scalar_tensor_tensor, sc, r, WI[:, n, h:h + 1], sc, ALU.mult, ALU.add)
            rs_free[h % 2] = t
        dv.wait(t)
        t = dv.run(ve.memset, SC[0:64, nk - 64:nk], -3.0e38)
        for i in range(16):
            dv.wait(t)
            t = dv.run(ve.max, M8, SC[:, 0:nk])
            dv.wait(t)
            t = dv.run(ve.match_replace, SC[:, 0:nk], M8, SC[:, 0:nk], -3.3e38)
        dv.wait(t)
        t = dv.run(ve.tensor_scalar, MB[:, 0:nk], SC[:, 0:nk], -3.2e38, -1.0e30, ALU.is_gt, ALU.mult)
        dv.wait(t)
        t_mb = dv.run(ve.memset, MB[0:64, nk - 64:nk], -1.0e30)
        mb = view(MB)
        gates(*((7, 1, 7) if n < 3 else (7, 7)))
        for g in range(2):
            if g or n:
                po.wait(t_qm)
            for h in range(4):
                t = po.run(ge.tensor_scalar, QM[:, h, :], RB[:, q0:q0 + 128], CST[:, C_M8 + 4 * g + h:C_M8 + 4 * g + h + 1],
                           None, ALU.mult)
            pe.wait(t)
            for h in range(4):
                b = 2 * (h % 2)
                claim(*range(b, b + np_))
                for i, (a, ww) in enumerate(ks):
                    mm(PS[:, b + i, 0:w], QLAT[:, 4 * g + h, q0:q0 + 128], CKT[:, a:a + w], True, False)
                    t = mm(PS[:, b + i, 0:w], QM[:, h, :], KR[:, a:a + w], False, True, mark=True)
                t_qm = t
                dv.wait(t, t_mb)
                if g or n:
                    dv.wait(t_ptr)
                p = view(P[:, h, :])
                t = dv.run(ve.tensor_tensor, p, bank(b), mb, ALU.add)
                for x in range(b, b + np_):
                    bank_free[x] = (t,)
                dv.wait(t)
                t = dv.run(ve.tensor_reduce, MX[:, h:h + 1], P[:, h, 0:nk], AX, ALU.max, negate=True)
                ac.wait(t)
                t = ac.run(se.activation, P[:, h, 0:nk], P[:, h, 0:nk], ACT.Exp, bias=MX[:, h:h + 1], accum_out=SM[:, h:h + 1])
                dv.wait(t)
                t = dv.run(ve.reciprocal, SM[:, h:h + 1], SM[:, h:h + 1])
                dv.wait(t)
                t_p = dv.run(ve.tensor_scalar, P[:, h, 0:nk], P[:, h, 0:nk], SM[:, h:h + 1], None, ALU.mult)
            gates(7)
            pe.wait(t_p)
            for k in range(n + 2):
                m = 128 if k <= n else 16
                b = 4 + k % 2
                claim(b)
                for h in range(4):
                    t = turn(PS[0:m, b, 128 * h:128 * h + 128], P[:, h, 128 * k:128 * k + m], mark=h == 3)
                t_ptr = t
                q = (ac, dv)[k % 2]
                if g or n:
                    q.wait(t_ol)
                t = evac(q, PTR[0:m, k, :], PS[0:m, b, :], b, t)
                bank_free[b] = (t,)
            pe.wait(ac.now(), dv.now())
            claim(6)
            for k in range(n + 2):
                m = 128 if k <= n else 16
                t = mm(PS[:, 6, :], CKV[0:m, k, :], PTR[0:m, k, :], k == 0, k == n + 1, mark=k == n + 1)
            t_ol = t
            t = evac(ac, OLAT[:, 4 * g:4 * g + 4, q0:q0 + 128], PS[:, 6, :].rearrange("p (a b) -> p a b", a=4), 6, t)
            bank_free[6] = (t,)
    while n_gate[0] < 16 or pending:
        gates(7)
    pe.wait(t)
    for h in range(8):
        j, p0 = h // 2, 64 * (h % 2)
        if h % 2 == 0:
            claim(j)
        t = mm(PS[p0:p0 + 64, j, :], WUV[:, h, :], OLAT[:, h, :], True, True, mark=True)
        if h % 2 == 1:
            t = evac((ac, dv)[j % 2], YB[:, j, :], PS[:, j, :], j, t)
            bank_free[j] = (t,)
    barrier()

    o = O_TEMP + 8 * TK
    Z = at3(o, 8, T); o += 8 * T
    GS = [at(OW + 4096 + 512 * i, 512) for i in range(3)]
    key_po = [(4, O_TEMP), (5, OW)]
    for k4 in key_po:
        state[k4] = [q.now() for q in engines]
    PO = [piece(A["wo"][i], 4096, key_po[i]) for i in range(2)]
    load_ready()
    gs_free = None
    for i in range(8):
        b = 2 * (i % 4)
        claim(b, b + 1)
        for x, Y in enumerate((YA, YB)):
            pe.wait(use(PUP[x]))
            W = pos(PUP[x], 4)
            for k in range(4):
                t = mm(PS[:, b + x, :], W[:, k, 128 * i:128 * i + 128], Y[:, k, :], k == 0, k == 3, mark=k == 3)
        if gs_free is not None:
            ac.wait(gs_free)
        ac.run(se.activation, GS[0], GAB[:, i, :], ACT.Sigmoid)
        t2 = ac.run(se.activation, GS[1], GAB[:, 8 + i, :], ACT.Sigmoid)
        dv.wait(t, t2)
        t = dv.run(ve.tensor_tensor, GS[2], GS[0], PS[:, b, :], ALU.mult)
        t = dv.run(ve.tensor_tensor, GS[1], GS[1], PS[:, b + 1, :], ALU.mult)
        bank_free[b] = bank_free[b + 1] = (t,)
        dv.wait(t)
        t = dv.run(ve.tensor_tensor, Z[:, i, :], GS[2], GS[1], ALU.add)
        gs_free = t
    for i, t in enumerate((pe.now(), pe.now())):
        release(PUP[i], t)
    t_z = gs_free
    pe.wait(t_z)
    for i in range(8):
        pe.wait(use(PO[i // 4]))
        claim(i)
        t = proj(pos(PO[i // 4], 8), 128 * (i % 4), 128, i, 0, XONLY, X=Z)
        if i % 4 == 3:
            release(PO[i // 4], pe.now())
        dv.wait(t)
        t = dv.run(ve.tensor_tensor, XT[:, i, META:TK], XT[:, i, META:TK], PS[:, i, :], ALU.add)
        bank_free[i] = (t,)
    barrier()


    o = O_TEMP + 2 * RING
    UT2 = at3(o, 8, T); o_ut2 = o; o += 8 * T
    UTOK = at3(o, 4, 1024); o_utok = o; o += 4096
    XR = [at(o + 1024 * i, 1024) for i in range(2)]; o += 2048
    XET = [at3(o + 1024 * i, 8, 128) for i in range(2)]; o += 2048
    o_w2x = o
    assert o + RING <= O_XT
    o = OW
    HS = [at(o + 256 * i, 256) for i in range(2)]; o += 512
    HT = [at3(o + 256 * i, 2, 128) for i in range(2)]; o += 512
    YS = [at(o + 512 * i, 512) for i in range(2)]; o += 1024
    o_rt = o
    o = SMALL
    o += 48
    ROW = at(o, 8).rearrange("p (n s) -> p n s", n=4); o += 8
    GATE = at(o, 8).rearrange("p (n s) -> p n s", n=4); o += 8
    XE = at(o, 32); o += 32
    FLAG = at(o, 1); o += 1
    S1 = at(o, 8); o += 8
    S2 = at(o, 8); o += 8
    SNK = at(o, 8); o += 8
    assert o <= O_WORK, (o, O_WORK)

    WGR = at3(o_rt, 8, 36)
    BGR = at(o_rt + 288, 36)
    s_rt = slot("rt")
    sp.dma(sy.dma_start, WGR, A["wgr"], s_rt)
    sp.dma(sy.dma_start, SNK, A["snk"], s_rt)
    RB8 = at(OW + 5672, 8)
    HOT = at(OW + 5680, 128)
    sp.dma(sy.dma_start, RB8[0:32, :], A["relb"], s_rt)
    sp.dma(sy.dma_start, HOT[0:32, :], A["hot"], s_rt)
    t_rt = sp.dma(sy.dma_start, BGR, A["bgr"], s_rt)
    experts = []
    ring9 = [(2, 2 * RING), (3, 3 * RING), (4, O_TEMP), (5, O_TEMP + RING), (0, 0), (1, RING), (6, o_w2x), (7, o_ut2), (8, o_utok)]
    n_p = 0
    for k4 in ring9:
        state[k4] = [q.now() for q in engines]
    state[ring9[7]] = state[ring9[8]] = None
    for e in range(32):
        ids = []
        for name in ("w1", "w3", "w2"):
            src = A[name][e].rearrange("(k p) n -> p k n", p=128)
            ids.append(piece(src, 4096, ring9[n_p % 9]))
            n_p += 1
        experts.append(ids)
    load_ready()

    s_sc = slot("scatter")

    def po_ind(n, i):
        s_sc.n += 16

        def emit(eng):
            eng.indirect_dma_start(out=xb, out_offset=bass.IndirectOffsetOnAxis(ap=ROW[:, n, i:i + 1].bitcast(U32), axis=0),
                                   in_=UTOK[:, n, :], in_offset=None).then_inc(s_sc.sem, 16)
        po.items.append(("call", emit))
        return s_sc.now()

    def gather(n, i):
        s_g[n].n += 16

        def emit(eng):
            eng.indirect_dma_start(out=GG[i][:, n, :], out_offset=None, in_=yb,
                                   in_offset=bass.IndirectOffsetOnAxis(ap=ROW[:, n, i:i + 1].bitcast(U32), axis=0),
                                   ).then_inc(s_g[n].sem, 16)
        po.items.append(("call", emit))
        return s_g[n].now()

    def toeplitz():
        for h in range(8):
            src = bass.AP(rs.tensor, 384 * h, [[1, 128], [1, 256]])
            t = sp.dma(sy.dma_start, BI[:, h, :], src, s_b)
        return t

    RT = o_rt
    LG = at3(RT + 324, 4, 36)
    G8 = at3(RT + 468, 4, 8)
    GM = at3(RT + 500, 4, 8)
    GI = at3(RT + 532, 4, 8)
    EG = at3(RT + 564, 4, 4)
    GS4 = at(RT + 580, 4)
    MK = at3(RT + 584, 4, 4)
    EM = at3(RT + 600, 4, 32)
    EV = at3(RT + 728, 4, 8)
    EI = at3(RT + 760, 4, 8)
    IF_ = at3(RT + 792, 4, 2)
    OH = [at3(RT + 800 + 128 * i, 4, 32) for i in range(3)]
    RK = at3(RT + 1184, 4, 32)
    CN = at(RT + 1312, 32)
    XC = at(RT + 1344, 32)
    XP = at(RT + 1376, 32)
    B1 = at3(RT + 1408, 4, 32)
    B2 = at3(RT + 1536, 4, 32)
    TM = at(RT + 1664, 32)
    RF = at3(RT + 1696, 4, 2)
    NG = at(RT + 1704, 4)
    GF = at(RT + 1708, 4)
    assert RT + 1712 <= ARENA
    IO = CST[:, C_IOTA:C_IOTA + 128]

    SQ2 = at3(OW, 2, T)
    RN2 = at(OW + 1024, T)
    t = norm(XT, META, T, UT2, V_FFN, SQ2, RN2, 0)
    for q in engines:
        q.wait(t, t_rt)
    for n in range(4):
        for k in range(8):
            t = mm(PS[:, 0, 36 * n:36 * n + 36], UT2[:, k, 128 * n:128 * n + 128], WGR[:, k, :], k == 0, k == 7, mark=k == 7)

    t_lg = t
    t_tok = []
    for n in range(4):
        b = 4 + 2 * (n % 2)
        claim(b, b + 1)
        for k in range(8):
            t = turn(PS[:, b + k // 4, 128 * (k % 4):128 * (k % 4) + 128], UT2[:, k, 128 * n:128 * n + 128], mark=k == 7)
        t = evac(ac, UTOK[:, n, :].rearrange("p (a b) -> p a b", a=2), PS[:, b:b + 2, :], b, t)
        bank_free[b] = bank_free[b + 1] = (t,)
        t_tok.append(t)
    state[ring9[7]] = [pe.now()]
    load_ready()

    def d(method, *a, **kw):
        dv.wait(dv.now())
        return dv.run(method, *a, **kw)

    dv.wait(t_lg)
    d(ve.tensor_tensor, LG, PS[:, 0, 0:144].rearrange("p (a b) -> p a b", a=4), BGR.unsqueeze(1).to_broadcast([128, 4, 36]),
      ALU.add)
    d(ve.memset, G8, -1.0e30)
    d(ve.tensor_copy, G8[:, :, 0:4], LG[:, :, 0:4])
    for n in range(4):
        d(ve.max, GM[:, n, :], G8[:, n, :])
        d(ve.max_index, GI[:, n, :].bitcast(U32), GM[:, n, :], G8[:, n, :])
    d(ve.tensor_copy, GF, GI[:, :, 0].bitcast(U32))
    t = d(ve.tensor_scalar, NG, GM[:, :, 0], -1.0, None, ALU.mult)
    ac.wait(t)
    for n in range(4):
        t = ac.run(se.activation, EG[:, n, :], LG[:, n, 0:4], ACT.Exp, bias=NG[:, n:n + 1], accum_out=GS4[:, n:n + 1])
    dv.wait(t)
    d(ve.reciprocal, GS4, GS4)
    d(ve.tensor_tensor, MK, IO[:, 0:4].unsqueeze(1).to_broadcast([128, 4, 4]), GF.unsqueeze(2).to_broadcast([128, 4, 4]),
      ALU.is_equal)
    mk8 = MK.unsqueeze(3).to_broadcast([128, 4, 4, 8])
    em = EM.rearrange("p n (g e) -> p n g e", g=4)
    d(ve.tensor_tensor, em, LG[:, :, 4:36].rearrange("p n (g e) -> p n g e", g=4), mk8, ALU.mult)
    d(ve.tensor_scalar, MK, MK, -1.0, 1.0e30, ALU.add, ALU.mult)
    d(ve.tensor_tensor, em, em, mk8, ALU.add)
    for n in range(4):
        d(ve.max, EV[:, n, :], EM[:, n, :])
        d(ve.max_index, EI[:, n, :].bitcast(U32), EV[:, n, :], EM[:, n, :])
    d(ve.tensor_copy, IF_, EI[:, :, 0:2].bitcast(U32))
    t = d(ve.tensor_tensor, NG, EV[:, :, 1], EV[:, :, 0], ALU.subtract)
    ac.wait(t)
    t = ac.run(se.activation, NG, NG, ACT.Exp)
    dv.wait(t)
    d(ve.tensor_scalar, GF, NG, 1.0, None, ALU.add)
    d(ve.reciprocal, GF, GF)
    d(ve.tensor_tensor, GATE[:, :, 0], GF, GS4, ALU.mult)
    d(ve.tensor_tensor, GATE[:, :, 1], GATE[:, :, 0], NG, ALU.mult)
    for i in range(2):
        d(ve.tensor_tensor, OH[i], IO[:, 0:32].unsqueeze(1).to_broadcast([128, 4, 32]),
          IF_[:, :, i:i + 1].to_broadcast([128, 4, 32]), ALU.is_equal)
    t = d(ve.tensor_tensor, OH[2], OH[0], OH[1], ALU.add)
    pe.wait(t)
    for n in range(4):
        for k in range(n):
            mm(PS[:, 1, 32 * n:32 * n + 32], ONE, OH[2][:, k, :], k == 0, False)
        mm(PS[:, 1, 32 * n:32 * n + 32], UP, OH[2][:, n, :], n == 0, True)
    for n in range(4):
        t = mm(PS[:, 2, 0:32], ONE, OH[2][:, n, :], n == 0, n == 3, mark=True)
    dv.wait(t)
    d(ve.tensor_copy, RK, PS[:, 1, 0:128].rearrange("p (a b) -> p a b", a=4))
    d(ve.tensor_copy, CN, PS[:, 2, 0:32])
    d(ve.tensor_scalar, XC, CN, float(CAP), None, ALU.is_gt)
    for m in range(2, (512 - 1) // CAP + 1):
        d(ve.tensor_scalar, TM, CN, float(CAP * m), None, ALU.is_gt)
        d(ve.tensor_tensor, XC, XC, TM, ALU.add)
    d(ve.tensor_tensor_scan, XP, ONE[:, 0:32], XC, 0.0, ALU.mult, ALU.add)
    d(ve.tensor_copy, FLAG.bitcast(U32), XP[:, 31:32])
    for i in range(NX):
        d(ve.tensor_scalar, TM, XP, float(i), None, ALU.is_le)
        d(ve.tensor_reduce, XE[:, i:i + 1], TM, AX, ALU.add)
    if True:
        d(ve.tensor_scalar, XE[:, 0:NX], XE[:, 0:NX], 31.0, None, ALU.min)
        d(ve.tensor_copy, XE[:, 0:NX].bitcast(U32), XE[:, 0:NX])
    d(ve.tensor_tensor, XP, XP, XC, ALU.subtract)
    d(ve.tensor_tensor, XP, XP, IO[:, 0:32], ALU.subtract)
    d(ve.tensor_scalar, XP, XP, 31.0, float(CAP), ALU.add, ALU.mult)
    d(ve.tensor_scalar, B1, RK, float(CAP), None, ALU.is_ge)
    d(ve.tensor_tensor, B1, B1, XP.unsqueeze(1).to_broadcast([128, 4, 32]), ALU.mult)
    d(ve.tensor_tensor, B1, B1, RK, ALU.add)
    d(ve.tensor_scalar, TM, IO[:, 0:32], float(CAP), None, ALU.mult)
    d(ve.tensor_tensor, B1, B1, TM.unsqueeze(1).to_broadcast([128, 4, 32]), ALU.add)
    for i in range(2):
        d(ve.tensor_tensor, B2, B1, OH[i], ALU.mult)
        d(ve.tensor_reduce, RF[:, :, i:i + 1], B2, AX, ALU.add)
    t_row = d(ve.tensor_copy, ROW.bitcast(U32), RF)
    for n in range(4):
        po.wait(t_tok[n], t_row, s_z.now())
        for i in range(2):
            t_sc = po_ind(n, i)
    state[ring9[8]] = [t_sc]
    load_ready()
    barrier(t_sc)

    def expert(qs, w, rows, xt, x0, i, free, ysem):
        pe, ac, dv, sp = qs
        w1, w3, w2 = w

        def m2(out, l, r, start, stop):
            return pe.run(te.matmul, out, l, r, start=start, stop=stop, mark=stop, skip_group_check=True)

        b = 4 * i
        H1 = PS[:, b, 0:256]
        H3 = PS[:, b + 1, 0:256]
        if free["h"][i]:
            pe.wait(*free["h"][i])
        for wt, ho in ((w1, b), (w3, b + 1)):
            for k in range(8):
                for half in range(2):
                    t = m2(PS[64 * half:64 * half + CAP, ho, 0:256], xt[:, k, x0:x0 + CAP],
                           wt[:, k, 256 * half:256 * half + 256], k == 0, k == 7)
        if free["hs"][i]:
            ac.wait(*free["hs"][i])
            dv.wait(*free["hs"][i])
        ac.wait(t)
        dv.wait(t)
        hs = [slice(0, CAP), slice(64, 64 + CAP)] if CAP < 64 else [slice(0, 128)]
        for p in hs:
            t = ac.run(se.activation, HS[i][p, :], PS[p, b, 0:256], ACT.Silu)
        dv.wait(t)
        for p in hs:
            t = dv.run(ve.tensor_tensor, HS[i][p, :], HS[i][p, :], PS[p, b + 1, 0:256], ALU.mult)
        free["h"][i] = (t,)
        pe.wait(t)
        if free["t"][i]:
            pe.wait(*free["t"][i])
        for c in range(2):
            for p in hs:
                n = p.stop - p.start
                t = pe.run(te.transpose, PS[:, b + 2, 128 * c + p.start:128 * c + p.stop], HS[i][p, 128 * c:128 * c + 128],
                           CST[p, C_ID + p.start:C_ID + p.stop], mark=True)
                pe.wait(t)
        free["hs"][i] = (t,)
        dv.wait(t)
        for p in hs:
            t = dv.run(ve.tensor_copy, HT[i][:, :, p], PS[:, b + 2, 0:256].rearrange("p (a b) -> p a b", a=2)[:, :, p])
        free["t"][i] = (t,)
        pe.wait(t)
        if free["y"][i]:
            pe.wait(*free["y"][i])
        for kt in range(4):
            for half in range(2):
                t = m2(PS[64 * half:64 * half + CAP, b + 3, :], HT[i][:, kt % 2, 64 * (kt // 2):64 * (kt // 2) + CAP],
                       w2[:, kt, 512 * half:512 * half + 512], kt == 0, kt == 3)
        t_w = t
        ac.wait(t)
        if free["ys"][i]:
            ac.wait(*free["ys"][i])
        for p in hs:
            t = ac.run(se.activation, YS[i][p, :], PS[p, b + 3, :], ACT.Copy)
        free["y"][i] = (t,)
        sp.wait(t)
        for half in range(2):
            t = sp.dma(ge.dma_start if sp is po else sy.dma_start, yb[rows:rows + CAP, 512 * half:512 * half + 512],
                       YS[i][64 * half:64 * half + CAP, :], ysem[i])
        free["ys"][i] = (t,)
        return t_w

    s_x = [slot(f"x{i}") for i in range(2)]
    s_y = [slot(f"y{i}") for i in range(2)]
    free = {k: [None, None] for k in ("h", "hs", "t", "y", "ys")}
    for b in range(8):
        bank_free[b] = None
    xr_free = [None, None]
    xt_free = [None, None]
    tx = {}

    def load_x(g):
        i = g % 2
        if xr_free[i] is not None:
            po.wait(*xr_free[i])
        tx[g] = po.dma(ge.dma_start, XR[i][0:2 * CAP, :], xb[2 * CAP * g:2 * CAP * g + 2 * CAP, :], s_x[i])

    load_x(0)
    load_x(1)
    for g in range(16):
        i = g % 2
        pe.wait(tx[g])
        for half in range(2):
            b = 4 * i + half
            f = free["h"][i]
            if f:
                pe.wait(*f)
            for k in range(4):
                kk = 4 * half + k
                t = turn(PS[:, b, 128 * k:128 * k + 2 * CAP], XR[i][0:2 * CAP, 128 * kk:128 * kk + 128], mark=k == 3)
            if xt_free[i]:
                (ac, dv)[half].wait(*xt_free[i])
            t2 = evac((ac, dv)[half], XET[i][:, 4 * half:4 * half + 4, 0:2 * CAP],
                      PS[:, b, :].rearrange("p (a b) -> p a b", a=4)[:, :, 0:2 * CAP], b, t)
            pe.wait(t2)
        xr_free[i] = (t,)
        if g + 2 < 16:
            load_x(g + 2)
        for x in range(2):
            e = 2 * g + x
            ids = experts[e]
            for y in ids:
                pe.wait(use(y))
            w = (pos(ids[0], 8), pos(ids[1], 8), pos(ids[2], 4))
            t = expert((pe, ac, dv, po), w, CAP * e, XET[i], CAP * x, x, free, s_y)
            for y in ids:
                release(y, t)
            if x == 1:
                xt_free[i] = (t,)
    barrier(s_y[0].now(), s_y[1].now())

    if True:
        bq = [Queue(new_sem("b_" + n)) for n in ("pe", "act", "dve", "sp")]
        bsem = [Slot(new_sem(f"bw{i}")) for i in range(4)]
        bys = [Slot(new_sem(f"by{i}")) for i in range(2)]
        bfree = {k: [None, None] for k in free}
        WX = [at3(o_ut2, 8, 512), at3(o_utok, 8, 512), at3(o_w2x, 4, 1024)]
        bpe, bac, bdv, bsp = bq

        def load_block(i):
            def emit(eng):
                e = eng.value_load(XE[0:1, i:i + 1].bitcast(mybir.dt.int32), min_val=0, max_val=31)
                for j, name in enumerate(("w1", "w3", "w2")):
                    src = A[name][bass.ds(e, 1)].rearrange("o (k p) n -> p (o k) n", p=128)
                    eng.dma_start(out=WX[j], in_=src).then_inc(bsem[j].sem, 16)
            return emit

        for i in range(NX):
            if i:
                bsp.wait(t_w)
            bsp.items.append(("call", load_block(i)))
            for s in bsem[:3]:
                s.n += 16
            r0 = (32 + i) * CAP
            t = bsp.dma(sy.dma_start, XR[0][0:CAP, :], xb[r0:r0 + CAP, :], bsem[3])
            bpe.wait(t)
            for b in range(2):
                if bfree["h"][0]:
                    bpe.wait(*bfree["h"][0])
                for k in range(4):
                    kk = 4 * b + k
                    t = bpe.run(te.transpose, PS[:, b, 128 * k:128 * k + CAP], XR[0][0:CAP, 128 * kk:128 * kk + 128],
                                CST[0:CAP, C_ID:C_ID + CAP], mark=k == 3)
                bdv.wait(t)
                t = bdv.run(ve.tensor_copy, XET[0][:, 4 * b:4 * b + 4, 0:CAP],
                            PS[:, b, :].rearrange("p (a b) -> p a b", a=4)[:, :, 0:CAP])
                bpe.wait(t)
            for s in bsem[:3]:
                bpe.wait(s.now())
            t_w = expert((bpe, bac, bdv, bsp), WX, r0, XET[0], 0, 0, bfree, bys)
        for q in bq:
            q.wait(*[x.now() for x in bq[:3]], bys[0].now())

        def guard(queue):
            def emit(eng):
                v = eng.value_load(FLAG[0:1, :].bitcast(mybir.dt.int32), min_val=0, max_val=64)
                with eng.If(v > 0):
                    queue.flush(eng)
            return emit

        bpo = Queue(new_sem("b_pool"))
        bpo.wait(*[x.now() for x in bq[:3]], bys[0].now())
        for q, x in zip((pe, ac, dv, sp, po), bq + [bpo]):
            q.items.append(("call", guard(x)))

    key4 = [(i, i * RING) for i in range(4)]
    PW = [piece(A["win2"][i], 4096, key4[i % 4]) for i in range(4)]
    PW.append(piece(A["win2s"], 2048, key4[0]))
    PQ = [piece(A["wout2"][i], 4096, key4[1 + i]) for i in range(2)]
    PK = [piece(A["wq"][i], 4096, key4[(3 + i) % 4]) for i in range(4)]
    load_ready()

    GG = [at3(o_ut2 + 4096 * i, 4, 1024) for i in range(2)]
    s_g = [slot(f"g{i}") for i in range(4)]
    for n in range(4):
        for i in range(2):
            t = gather(n, i)
        dv.wait(t)
        d(ve.tensor_scalar, GG[0][:, n, :], GG[0][:, n, :], GATE[:, n, 0:1], None, ALU.mult)
        t = d(ve.scalar_tensor_tensor, GG[0][:, n, :], GG[1][:, n, :], GATE[:, n, 1:2], GG[0][:, n, :], ALU.mult, ALU.add)
        pe.wait(t)
        for k in range(8):
            t = turn(PS[:, k, 128 * n:128 * n + 128], GG[0][:, n, 128 * k:128 * k + 128], mark=k == 7)
    dv.wait(t)
    for k in range(8):
        t = dv.run(ve.tensor_tensor, XT[:, k, META:TK], XT[:, k, META:TK], PS[:, k, :], ALU.add)
        bank_free[k] = (t,)
    barrier()

    X = XT[:, :, META:TK]
    o = O_TEMP
    HN = at3(o, 8, T); o += 8 * T
    MIXED = at3(o, 8, T); o += 8 * T
    UC = at3(o, 4, 514); o += 2056
    YC = at3(o, 4, T); o += 2048
    Q2 = at3(o, 4, T); o += 2048
    K2 = at(o, T); o += T
    V2 = at3(o, 4, 128); o += 512
    BI = at3(o, 8, 256); o += 2048
    BIR = BI
    CB = at3(o, 4, T); o_cb = o; o += 2048
    YT2 = at3(o, 4, T); o += 2048
    assert o <= O_XT, o
    o = OW
    S8 = at3(o, 8, 256); o += 2048
    PT2 = [[at(o + 1024 * kc + 512 * g, 512) for g in range(2)] for kc in range(2)]; o += 2048
    SQ2 = at3(o, 2, T); o += 1024
    RN2 = at(o, T); o += 512
    ST = at(o, 40); o += 40
    assert o == OW + 5672
    o += 136
    assert o <= ARENA
    RSC = AR[0:8, o_cb:o_cb + 384]

    rs = nc.dram_tensor("rs", [8, 384], F32, kind="Internal").ap()
    s_b = slot("bias")
    t = mm(PS[0:8, 7, 0:128], RB8[0:32, :], HOT[0:32, :], True, True, mark=True)
    dv.wait(t)
    d(ve.memset, RSC, -1.0e30)
    t = d(ve.tensor_copy, RSC[:, 127:255], PS[0:8, 7, 0:128])
    bank_free[7] = (t,)
    sp.wait(t)
    t = sp.dma(sy.dma_start, rs, RSC, s_b)
    sp.wait(t)
    t_bi = toeplitz()

    t = norm(XT, META, T, X, V_FIN, SQ2, RN2, 0)
    d(ve.tensor_scalar, S1, MOD[:, 8:16], 1.0, None, ALU.add)
    d(ve.tensor_tensor, S1, S1, VEC[:, V_N1:V_N1 + 8], ALU.mult)
    d(ve.tensor_scalar, S2, MOD[:, 32:40], 1.0, None, ALU.add)
    t = d(ve.tensor_tensor, S2, S2, VEC[:, V_N2:V_N2 + 8], ALU.mult)
    for q in engines:
        q.wait(t)

    def shifted_norm(U, g, shift):
        t = norm(XT, META, T, U, None, SQ2, RN2, 0, cols=g)
        ac.wait(t)
        for k in range(8):
            t = ac.run(se.activation, U[:, k, :], U[:, k, :], ACT.Identity, bias=MOD[:, shift + k:shift + k + 1])
        pe.wait(t)
        return t

    for b in range(8):
        bank_free[b] = (dv.now(),)
    shifted_norm(HN, S1, 0)

    dv.wait(t)
    t = d(ve.memset, UC[:, :, 0:2], 0.0)
    pe.wait(use(PW[0]))
    for j in range(4):
        claim(j)
        t = proj(pos(PW[0], 8), 128 * j, 128, j, 0, XONLY, X=HN)
        t = evac(ac, UC[:, j, 2:514], PS[:, j, :], j, t)
        bank_free[j] = (t,)
    release(PW[0], pe.now())
    pe.wait(use(PW[1]))
    for j in range(4):
        b = 4 + j
        claim(b)
        t = proj(pos(PW[1], 8), 128 * j, 128, b, 0, XONLY, X=HN)
        dv.wait(t, bank_free[j][0])
        t = dv.run(ve.tensor_tensor, UC[:, j, 2:514], UC[:, j, 2:514], PS[:, b, :], ALU.mult)
        bank_free[b] = (t,)
    release(PW[1], pe.now())
    pe.wait(use(PW[2]))
    for j in range(4):
        claim(j)
        tb = proj(pos(PW[2], 8), 128 * j, 128, j, 0, XONLY, X=HN)
        wc = [VEC[:, V_CONV + 4 * i + j:V_CONV + 4 * i + j + 1] for i in range(3)]
        d(ve.tensor_scalar, YC[:, j, :], UC[:, j, 0:T], wc[0], None, ALU.mult)
        for i in (1, 2):
            d(ve.scalar_tensor_tensor, YC[:, j, :], UC[:, j, i:T + i], wc[i], YC[:, j, :], ALU.mult, ALU.add)
        dv.wait(tb)
        t = d(ve.tensor_tensor, YC[:, j, :], YC[:, j, :], PS[:, j, :], ALU.mult)
        bank_free[j] = (t,)
    release(PW[2], pe.now())
    BLK = CST[:, C_BLK:C_BLK + 128]
    sqf = [None, None]
    seq = [0]

    def group_norm(x, out, gcol, scale=1.0, in_loop=False):
        i = seq[0] % 2
        b = (6 + i) if not in_loop else 6
        seq[0] += 1
        if sqf[i] is not None:
            ac.wait(*sqf[i])
        ac.wait(dv.now())
        t = ac.run(se.activation, SQ2[:, i, :], x, ACT.Square)
        pe.wait(t)
        claim(b)
        t = mm(PS[:, b, :], BLK, SQ2[:, i, :], True, True, mark=True)
        dv.wait(t)
        t = dv.run(ve.tensor_scalar, SQ2[:, i, :], PS[:, b, :], 1.0, EPS, ALU.mult, ALU.add)
        bank_free[b] = (t,)
        ac.wait(t)
        t = ac.run(se.activation, SQ2[:, i, :], SQ2[:, i, :], ACT.Sqrt, scale=1.0)
        dv.wait(t)
        d(ve.reciprocal, SQ2[:, i, :], SQ2[:, i, :])
        if scale != 1.0:
            d(ve.tensor_scalar, SQ2[:, i, :], SQ2[:, i, :], scale, None, ALU.mult)
        t = d(ve.scalar_tensor_tensor, out, x, VEC[:, gcol:gcol + 1], SQ2[:, i, :], ALU.mult, ALU.mult)
        sqf[i] = (t,)
        return t

    pe.wait(use(PW[3]))
    for j in range(4):
        claim(j)
        t = proj(pos(PW[3], 8), 128 * j, 128, j, 0, XONLY, X=HN)
        t = evac(dv, Q2[:, j, :], PS[:, j, :], j, t)
        bank_free[j] = (t,)
    release(PW[3], pe.now())
    pe.wait(use(PW[4]))
    W = pos(PW[4], 8)
    claim(4)
    t = proj(W, 0, 128, 4, 0, XONLY, X=HN)
    t = evac(dv, K2, PS[:, 4, :], 4, t)
    bank_free[4] = (t,)
    claim(5)
    for n in range(4):
        for k in range(8):
            t = mm(PS[:, 5, 128 * n:128 * n + 128], HN[:, k, 128 * n:128 * n + 128], W[:, k, 128:256], k == 0, k == 7, mark=k == 7)
    t = evac(dv, V2, PS[:, 5, :].rearrange("p (a b) -> p a b", a=4), 5, t)
    bank_free[5] = (t,)
    release(PW[4], pe.now())
    for j in range(4):
        group_norm(Q2[:, j, :], Q2[:, j, :], V_QG, 0.125)
    t = group_norm(K2, K2, V_KG)
    pe.wait(t)
    dv.wait(t_bi)
    S8S = [S8, at3(o_cb, 8, 256)]
    STS = [ST, at(OW + 5808, 32)]
    s8_free = [None, None]
    pt_free2 = None

    def weights(n):
        S8, ST = S8S[n % 2], STS[n % 2]
        kc0 = 0 if n else 1
        nk = 128 * (2 - kc0)
        claim(0, 1, 2, 3)
        for h in range(8):
            j, g = h % 4, h // 4
            t = mm(PS[:, h // 2, 256 * (h % 2) + 128 * kc0:256 * (h % 2) + 256], Q2[64 * g:64 * g + 64, j, 128 * n:128 * n + 128],
                   K2[64 * g:64 * g + 64, 128 * n + 128 - nk:128 * n + 128], True, True, mark=True)
            if h in (3, 7):
                pe.wait(t)
        sc = S8[:, :, 128 * kc0:256]
        if s8_free[n % 2] is not None:
            dv.wait(s8_free[n % 2])
        dv.wait(t)
        ps = PS[:, 0:4, :].rearrange("p b (a c) -> p (b a) c", a=2)[:, :, 128 * kc0:256]
        t = d(ve.tensor_tensor, sc, ps, BIR[:, :, 0:nk][:, :, ::-1], ALU.add)
        for b in range(4):
            bank_free[b] = (t,)
        d(ve.tensor_reduce, ST[:, 0:8], sc, AX, ALU.max)
        d(ve.tensor_tensor, ST[:, 0:8], ST[:, 0:8], SNK, ALU.max)
        d(ve.tensor_tensor, ST[:, 8:16], SNK, ST[:, 0:8], ALU.subtract)
        t = d(ve.tensor_scalar, ST[:, 0:8], ST[:, 0:8], -1.0, None, ALU.mult)
        yield
        ac.wait(t)
        ac.run(se.activation, ST[:, 16:24], ST[:, 8:16], ACT.Exp)
        for h in range(8):
            t = ac.run(se.activation, S8[:, h, 128 * kc0:256], S8[:, h, 128 * kc0:256], ACT.Exp, bias=ST[:, h:h + 1],
                       accum_out=ST[:, 24 + h:25 + h])
        yield
        dv.wait(t)
        d(ve.tensor_tensor, ST[:, 24:32], ST[:, 24:32], ST[:, 16:24], ALU.add)
        d(ve.reciprocal, ST[:, 24:32], ST[:, 24:32])
        t = d(ve.tensor_tensor, sc, sc, ST[:, 24:32].unsqueeze(2).to_broadcast([128, 8, nk]), ALU.mult)
        w_made[n] = t
        yield

    w_made = {}
    for _ in weights(0):
        pass
    for n in range(4):
        kc0 = 0 if n else 1
        S8 = S8S[n % 2]
        following = weights(n + 1) if n < 3 else iter(())
        next(following, None)
        pe.wait(w_made[n])
        for kc in range(kc0, 2):
            for g in range(2):
                b = 4 + g
                claim(b)
                for j in range(4):
                    t = turn(PS[:, b, 128 * j:128 * j + 128], S8[:, 4 * g + j, 128 * kc:128 * kc + 128], mark=j == 3)
                s8_free[n % 2] = t
                q = (ac, dv)[g]
                if pt_free2 is not None:
                    q.wait(pt_free2)
                t = evac(q, PT2[kc][g], PS[:, b, :], b, t)
                bank_free[b] = (t,)
        made = (ac.now(), dv.now())
        next(following, None)
        group_norm(YC[:, n, :], MIXED[:, n, :], V_CG + n, in_loop=True)
        next(following, None)
        pe.wait(*made)
        claim(7)
        for g in range(2):
            for kc in range(kc0, 2):
                t = mm(PS[64 * g:64 * g + 64, 7, :], V2[:, n - 1 + kc, 64 * g:64 * g + 64], PT2[kc][g], kc == kc0, kc == 1,
                       mark=True)
        pt_free2 = t
        t = evac(ac, YT2[:, :, 128 * n:128 * n + 128], PS[:, 7, :].rearrange("p (a b) -> p a b", a=4), 7, t)
        bank_free[7] = (t,)
    dv.wait(t)
    ac.wait(t)
    for j in range(4):
        t = group_norm(YT2[:, j, :], MIXED[:, 4 + j, :], V_AG + j)
    pe.wait(t)
    for i in range(8):
        b = i % 6
        pe.wait(use(PQ[i // 4]))
        claim(b)
        t = proj(pos(PQ[i // 4], 8), 128 * (i % 4), 128, b, 0, XONLY, X=MIXED)
        if i % 4 == 3:
            release(PQ[i // 4], pe.now())
        dv.wait(t)
        t = dv.run(ve.scalar_tensor_tensor, X[:, i, :], PS[:, b, :], MOD[:, 16 + i:17 + i], X[:, i, :], ALU.mult, ALU.add)
        bank_free[b] = (t,)
    barrier()

    H2 = at3(OW, 8, T)
    s_k = slot("keys")
    KEYS = at3(O_TEMP + 1536, 16, 128)
    t_keys = sp.dma(sy.dma_start, KEYS, A["keysT"], s_k)
    SQ2 = at3(O_TEMP, 2, T)
    RN2 = at(O_TEMP + 1024, T)
    shifted_norm(H2, S2, 24)
    xs = nc.dram_tensor("xs", [128, 8, 512], F32, kind="Internal").ap()
    hs = nc.dram_tensor("hs", [128, 8, 512], F32, kind="Internal").ap()
    gd = nc.dram_tensor("gd", [4, 128, 128, 128], F32, kind="Internal").ap()
    s_xs = slot("xs")
    sp.wait(dv.now(), ac.now())
    sp.dma(sy.dma_start, xs, X, s_xs)
    t_xs = sp.dma(sy.dma_start, hs, H2, s_xs)
    o = O_TEMP + 1536
    o += 2048
    QP = [at3(o + 2048 * i, 4, T) for i in range(2)]; o += 4096
    SS = [at3(o + 512 * i, 4, 128) for i in range(2)]; o += 1024
    TM = at3(o, 4, 128); o += 512
    OG = [0, O_TEMP]
    assert o <= 2 * O_TEMP
    o = 2 * O_TEMP
    SV = at(o, 1024).rearrange("p (n h k) -> p n h k", n=4, h=16); o += 1024
    SI = at(o, 1024).rearrange("p (n h k) -> p n h k", n=4, h=16); o += 1024
    SF = at(o, 1024).rearrange("p (n h k) -> p n h k", n=4, h=16); o += 1024
    CD = [at3(o + 128 * i, 2, 64) for i in range(3)]; o += 384
    EQ = [at(o + 2048 * i, 2048).rearrange("p (h k i) -> p h k i", h=8, k=16) for i in range(2)]; o += 4096
    IT = [at(o + 512 * i, 512) for i in range(3)]; o += 1536
    TV, TI = (at(o + 512 * i, 512).rearrange("p (n h k) -> p n h k", n=4, h=8) for i in range(2)); o += 1024
    PX = at3(o, 8, 16); o += 128
    PI = [at3(o + 128 * i, 8, 16) for i in range(4)]; o += 512
    NB1 = at(o, 512); o += 512
    IAB = [at(o + 128 * i, 128) for i in range(2)]; o += 256
    SMX = at(o, 8); o += 8
    assert o <= O_CST, o
    NB = 4
    AH = [at3(OW + 512 * i, 4, 128) for i in range(NB)]
    BH = [at3(OW + 512 * (NB + i), 4, 128) for i in range(NB)]

    def each(method, args):
        dv.wait(dv.now())
        for a in args:
            t = dv.run(method, *a)
        return t

    def top16(srcs, tmps, vs, idxs):
        n = range(len(srcs))
        each(ve.max, [(vs[i][:, 0:8], srcs[i]) for i in n])
        each(ve.max_index, [(idxs[i][:, 0:8].bitcast(U32), vs[i][:, 0:8], srcs[i]) for i in n])
        each(ve.match_replace, [(tmps[i], vs[i][:, 0:8], srcs[i], -3.0e38) for i in n])
        each(ve.max, [(vs[i][:, 8:16], tmps[i]) for i in n])
        each(ve.max_index, [(idxs[i][:, 8:16].bitcast(U32), vs[i][:, 8:16], tmps[i]) for i in n])

    def sums(i, n):
        v = SV[:, n, 4 * i:4 * i + 4, :].rearrange("p (h s) k -> p h s k", s=2)
        va, vb = v[:, :, 0, :], v[:, :, 1, :]
        u = CD[2]
        args = [(u[:, :, 0:16], va[:, :, 0:1].to_broadcast([128, 2, 16]), vb, ALU.add)]
        for a0, a1, w, c in ((1, 4, 8, 16), (4, 8, 4, 40)):
            m = a1 - a0
            args.append((u[:, :, c:c + m * w].rearrange("p h (a b) -> p h a b", a=m),
                         va[:, :, a0:a1].unsqueeze(3).to_broadcast([128, 2, m, w]),
                         vb[:, :, 0:w].unsqueeze(2).to_broadcast([128, 2, m, w]), ALU.add))
        args.append((u[:, :, 56:64], va[:, :, 8:16], vb[:, :, 0:1].to_broadcast([128, 2, 8]), ALU.add))
        each(ve.tensor_tensor, args)
        return ([u[:, x, :] for x in range(2)], [CD[0][:, x, :] for x in range(2)], [TV[:, n, 2 * i + x, :] for x in range(2)],
                [TI[:, n, 2 * i + x, :] for x in range(2)])

    dv.wait(t_xs)
    last = None
    qp_free = [None, None]
    ss_free = [None, None]
    c = 0
    for i in range(4):
        pe.wait(use(PK[i]))
        for f in range(4):
            claim(f)
            t = proj(pos(PK[i], 8), 128 * f, 128, f, 0, XONLY, X=H2)
            if qp_free[i % 2] is not None:
                ac.wait(qp_free[i % 2])
            t = evac(ac, QP[i % 2][:, f, :], PS[:, f, :], f, t)
            bank_free[f] = (t,)
        release(PK[i], pe.now())
        pe.wait(t, t_keys)
        for n in range(4):
            b = 4 + n
            claim(b)
            for f in range(4):
                t = mm(PS[:, b, 128 * f:128 * f + 128], QP[i % 2][:, f, 128 * n:128 * n + 128], KEYS[:, 4 * i + f, :], True, True,
                       mark=True)
            qp_free[i % 2] = t
            s = SS[c % 2]
            if ss_free[c % 2] is not None:
                ac.wait(ss_free[c % 2])
            t = evac(ac, s, PS[:, b, :].rearrange("p (a b) -> p a b", a=4), b, t)
            bank_free[b] = (t,)
            dv.wait(t)
            cands = sums(*last) if last else ([], [], [], [])
            mine = ([s[:, f, :] for f in range(4)], [TM[:, f, :] for f in range(4)],
                    [SV[:, n, 4 * i + f, :] for f in range(4)], [SI[:, n, 4 * i + f, :] for f in range(4)])
            top16(*[x + y for x, y in zip(mine, cands)])
            last = (i, n)
            ss_free[c % 2] = dv.now()
            c += 1
    top16(*sums(*last))
    d(ve.tensor_copy, SF, SI.bitcast(U32))
    barrier(t_xs)

    io16 = IO[:, 0:16].unsqueeze(1).unsqueeze(1).to_broadcast([128, 8, 16, 16])
    it_made = [None] * 4
    t_m = [None, None]

    def choice(n):
        ti = TI[:, n].bitcast(U32)
        t = d(ve.tensor_tensor, PX, TV[:, n], TV[:, n, :, 0:1].to_broadcast([128, 8, 16]), ALU.subtract)
        ac.wait(t)
        t_e = ac.run(se.activation, PX, PX, ACT.Exp)
        each(ve.tensor_scalar, [(PI[3].bitcast(U32), ti, 3, None, ALU.logical_shift_right),
                                (PI[1].bitcast(U32), ti, 2, None, ALU.logical_shift_right)])
        yield
        each(ve.tensor_copy, [(PI[0], PI[3].bitcast(U32)), (PI[1], PI[1].bitcast(U32)), (PI[2], ti)])
        yield
        d(ve.tensor_scalar, PI[0], PI[0], -1.0, 0.0, ALU.add, ALU.max)
        d(ve.scalar_tensor_tensor, PI[0], PI[1], -6.0, PI[0], ALU.add, ALU.max)
        yield
        d(ve.scalar_tensor_tensor, PI[0], PI[2], -48.0, PI[0], ALU.add, ALU.max)
        each(ve.tensor_scalar, [(PI[1], PI[0], 8.0, 8.0, ALU.mult, ALU.add), (PI[3], PI[0], 4.0, 24.0, ALU.mult, ALU.add)])
        yield
        d(ve.scalar_tensor_tensor, PI[1], PI[0], 16.0, PI[1], ALU.mult, ALU.min)
        d(ve.scalar_tensor_tensor, PI[3], PI[0], 48.0, PI[3], ALU.add, ALU.min)
        yield
        d(ve.tensor_tensor, PI[1], PI[1], PI[3], ALU.min)
        d(ve.tensor_tensor, PI[1], PI[2], PI[1], ALU.subtract)
        yield
        dv.wait(t_e)
        d(ve.tensor_reduce, SMX, PX, AX, ALU.add)
        d(ve.reciprocal, SMX, SMX)
        yield
        d(ve.tensor_tensor, PX, PX, SMX.unsqueeze(2).to_broadcast([128, 8, 16]), ALU.mult)
        yield
        for s in range(2):
            t = d(ve.tensor_tensor, EQ[s], io16, PI[s].unsqueeze(3).to_broadcast([128, 8, 16, 16]), ALU.is_equal)
            sf = SF[:, n].rearrange("p (h s) k -> p h s k", s=2)[:, :, s, :].unsqueeze(2).to_broadcast([128, 8, 16, 16])
            po.wait(t)
            t_m[s] = po.run(ge.tensor_tensor, EQ[s], EQ[s], sf, ALU.mult)
            yield
        for s in range(4):
            yield
        for s in range(2):
            dv.wait(t_m[s])
            t = d(ve.tensor_reduce, IAB[s].rearrange("p (h k) -> p h k", h=8), EQ[s], AX, ALU.add)
            yield
        pe.wait(t)
        claim(7)
        for s in range(3):
            src = IAB[s] if s < 2 else PX.rearrange("p h k -> p (h k)")
            t = turn(PS[:, 7, 128 * s:128 * s + 128], src, mark=s == 2)
        yield
        dv.wait(t)
        for s in range(3):
            t = dv.run(ve.tensor_copy, IT[s][:, 128 * n:128 * n + 128], PS[:, 7, 128 * s:128 * s + 128])
        t2 = d(ve.tensor_scalar, NB1[:, 128 * n:128 * n + 128], PS[:, 7, 128:256], -1.0, None, ALU.mult)
        bank_free[7] = (t2,)
        it_made[n] = t2
        yield

    s_gd = [[slot(f"gd{i}{j}") for j in range(4)] for i in range(2)]
    g_out = [None, None]
    h_free = [None] * NB
    LEAD = 3
    ready = {}

    def one_hots(q4):
        i, t0, n = q4 % NB, 4 * q4, q4 // 32
        for q in (dv, po, ac):
            q.wait(it_made[n])
            if h_free[i] is not None:
                q.wait(h_free[i])
        on_ac = 2 if n < 3 else 1
        for x in range(4 - on_ac, 4):
            tc = ac.run(se.activation, BH[i][:, x, :], IO, ACT.Abs, bias=NB1[:, t0 + x:t0 + x + 1])
        ac.wait(tc)
        tc = ac.run(se.activation, BH[i][:, 4 - on_ac:4, :], BH[i][:, 4 - on_ac:4, :], ACT.Relu, scale=-1.0, bias=1.0)
        for x in range(4):
            if x < 2:
                tb = po.run(ge.tensor_scalar, BH[i][:, x, :], IO, IT[1][:, t0 + x:t0 + x + 1], None, ALU.is_equal)
            elif x < 4 - on_ac:
                ta = dv.run(ve.tensor_scalar, BH[i][:, x, :], IO, IT[1][:, t0 + x:t0 + x + 1], None, ALU.is_equal)
            ta = dv.run(ve.tensor_scalar, AH[i][:, x, :], IO, IT[0][:, t0 + x:t0 + x + 1], IT[2][:, t0 + x:t0 + x + 1],
                        ALU.is_equal, ALU.mult)
        ready[q4] = (ta, tb, tc)

    for _ in choice(0):
        pass
    for q4 in range(LEAD):
        one_hots(q4)
    for n in range(4):
        following = choice(n + 1) if n < 3 else iter(())
        GT = AR[:, OG[n % 2]:OG[n % 2] + 16384].rearrange("p (a t) -> p a t", a=128)
        for x4 in range(32):
            q4 = 32 * n + x4
            i = q4 % NB
            if x4 == 32 - LEAD:
                for _ in following:
                    pass
            if q4 + LEAD < 128:
                one_hots(q4 + LEAD)
            if x4 == 0 and g_out[n % 2] is not None:
                ac.wait(*g_out[n % 2])
            pe.wait(*ready[q4])
            b = q4 % 7
            claim(b)
            for x in range(4):
                t = mm(PS[:, b, 128 * x:128 * x + 128], BH[i][:, x, :], AH[i][:, x, :], True, True, mark=x == 3)
            h_free[i] = t
            t = evac(ac, GT[:, :, 4 * x4:4 * x4 + 4], PS[:, b, :].rearrange("p (x a) -> p a x", x=4), b, t)
            bank_free[b] = (t,)
            next(following, None)
        sp.wait(t)
        g_out[n % 2] = [sp.dma(sy.dma_start, gd[n][:, 32 * q:32 * q + 32, :], GT[:, 32 * q:32 * q + 32, :], s_gd[n % 2][q])
                        for q in range(4)]
        if n == 2:
            sp.wait(*g_out[0])

    HSR = [alias(8192 + 2048 * i, 2048) for i in range(4)]
    SPL = [alias(16384 + 2048 * i, 2048) for i in range(6)]
    GGR = [alias(28672 + 2048 * i, 2048) for i in range(4)]
    GE = [at(OW + 512 * i, 512) for i in range(4)]
    raw_key = [(i, 2048 * i) for i in range(4)]
    g_key = [(4 + i, 36864 + 1024 * i) for i in range(4)]
    for k4 in raw_key:
        state[k4] = g_out[0]
    gd_all = g_out[0] + g_out[1]
    for k4 in g_key:
        state[k4] = [q.now() for q in engines]
    units = []
    GPC = {}
    c = 0
    for g in range(16):
        for i in range(4):
            p = piece(A["uT"][4 * g + i], 2048, raw_key[c % 4]); c += 1
            GPC[4 * g + i] = piece(gd[:, :, 8 * g + 2 * i:8 * g + 2 * i + 2, :].rearrange("n b a t -> b n (a t)"), 1024, g_key[i])
            needs[GPC[4 * g + i]] = [m[(8 * g + 2 * i) // 32] for m in g_out]
            units += [("u", g, 2 * i, p, 0), ("u", g, 2 * i + 1, p, 1)]
        for hf in range(2):
            for i in range(2):
                p = piece(A["v"][2 * (2 * g + hf) + i], 2048, raw_key[c % 4]); c += 1
                units += [("v", 2 * g + hf, 4 * i, p, 0), ("v", 2 * g + hf, 4 * i + 2, p, 1)]
    H2R = at3(4096, 8, T)
    t = sp.dma(sy.dma_start, H2R, hs, s_xs)
    ac.wait(t)
    dv.wait(t)
    for i in range(4):
        hv = HSR[i][:, :].rearrange("p (s k t) -> p s k t", s=2, k=2)
        t = ac.run(se.activation, hv[:, 0], H2R[:, 2 * i:2 * i + 2, :], ACT.Copy)
        dv.wait(t)
        t = dv.run(ve.tensor_tensor, hv[:, 1], H2R[:, 2 * i:2 * i + 2, :], hv[:, 0].bitcast(F32), ALU.subtract)
    for k4 in raw_key[2:]:
        state[k4] = [t]
    pe.wait(t)
    sp.wait(*[q.now() for q in engines])
    t_x = sp.dma(sy.dma_start, X, xs, s_xs)
    load_ready()
    split_made = {}
    pe_done = {}
    parts = {}

    def split(j):
        kind, g, a, p, h = units[j]
        raw = at(pieces[p][2][1] + 1024 * h, 1024)
        s = SPL[j % 6]
        q = ac
        if j >= 6:
            q.wait(pe_done[j - 6])
        else:
            for m in g_out[1][0:(2048 * j + 2048 + 4095) // 4096]:
                q.wait(m)
        q.wait(use(p))
        t = q.run(se.activation, s[:, 0:1024], raw, ACT.Copy)
        dv.wait(t)
        t = dv.run(ve.tensor_tensor, s[:, 1024:2048], raw, s[:, 0:1024].bitcast(F32), ALU.subtract)
        split_made[j] = t
        if h == 1:
            release(p, t)

    ge_free = [None] * 4
    gg_made = [None] * 8
    gg_read = [None] * 8
    AHEAD = 4

    def experts(j):
        _, g, a, p, h = units[j]
        b = 4 * (g % 2) + a % 4
        pe.wait(split_made[j])
        claim(b)
        w = SPL[j % 6][:, :].rearrange("p (s k b) -> p s k b", s=2, k=8)
        for k in range(8):
            hv = HSR[k // 2][:, :].rearrange("p (s k t) -> p s k t", s=2, k=2)[:, :, k % 2, :]
            for i, (x, y) in enumerate(((0, 0), (0, 1), (1, 0))):
                t = mm(PS[:, b, :], w[:, x, k, :], hv[:, y, :], k == 0 and i == 0, k == 7 and i == 2, mark=k == 7 and i == 2)
        pe_done[j] = t
        e = GE[a % 4]
        ac.wait(t)
        if ge_free[a % 4] is not None:
            ac.wait(ge_free[a % 4])
        t = ac.run(se.activation, e, PS[:, b, :], ACT.Gelu_apprx_tanh)
        bank_free[b] = (t,)
        gp = GPC[4 * g + a // 2]
        dv.wait(t, use(gp))
        gates = pos(gp, 4)[:, :, 128 * (a % 2):128 * (a % 2) + 128]
        t = dv.run(ve.tensor_tensor, e.rearrange("p (n t) -> p n t", n=4), e.rearrange("p (n t) -> p n t", n=4), gates, ALU.mult)
        if a % 2:
            release(gp, t)
        ac.wait(t)
        if gg_read[a] is not None:
            ac.wait(gg_read[a])
        gg = GGR[a // 2][:, :].rearrange("p (s a t) -> p s a t", s=2, a=2)[:, :, a % 2, :]
        t = ac.run(se.activation, gg[:, 0, :], e, ACT.Copy)
        dv.wait(t)
        t = dv.run(ve.tensor_tensor, gg[:, 1, :], e, gg[:, 0, :].bitcast(F32), ALU.subtract)
        ge_free[a % 4] = t
        gg_made[a] = t

    def products(j):
        _, gh, a0, p, h = units[j]
        g, hf = gh // 2, gh % 2
        b0 = 4 * ((g + 1 + hf) % 2)
        pe.wait(split_made[j], gg_made[a0], gg_made[a0 + 1])
        if a0 == 0:
            claim(b0, b0 + 1, b0 + 2, b0 + 3)
        w = SPL[j % 6][:, :].rearrange("p (s a d) -> p s a d", s=2, a=2)
        for x in range(2):
            gg = GGR[a0 // 2][:, :].rearrange("p (s a t) -> p s a t", s=2, a=2)[:, :, x, :]
            for k in range(4):
                for i, (y, z) in enumerate(((0, 0), (0, 1), (1, 0))):
                    last = a0 == 6 and x == 1 and i == 2
                    t = mm(PS[:, b0 + k, :], w[:, y, x, 128 * k:128 * k + 128], gg[:, z, :], a0 == 0 and x == 0 and i == 0, last,
                           mark=last or (x == 1 and k == 3 and i == 2))
                if last:
                    dv.wait(t)
                    kk = 4 * hf + k
                    bank_free[b0 + k] = (dv.run(ve.scalar_tensor_tensor, X[:, kk, :], PS[:, b0 + k, :], MOD[:, 40 + kk:41 + kk],
                                                X[:, kk, :], ALU.mult, ALU.add),)
            if hf == 1:
                gg_read[a0 + x] = pe.now()
        pe_done[j] = t

    for j in range(AHEAD):
        split(j)
    dv_x = False
    for j in range(len(units)):
        if j + AHEAD < len(units):
            split(j + AHEAD)
        if units[j][0] == "u":
            experts(j)
        else:
            if not dv_x:
                dv.wait(t_x)
                dv_x = True
            products(j)
    s_out = slot("out")
    sp.wait(dv.now())
    t_o = sp.dma(sy.dma_start, A["out"].rearrange("(k p) t -> p k t", p=128), X, s_out)
    sp.wait(t_o)
    block = ctx.enter_context(nc.Block())
    block.sync(sp.flush)
    block.tensor(pe.flush)
    block.scalar(ac.flush)
    block.vector(dv.flush)
    block.gpsimd(po.flush)



def layout(i):
    a = {k: np.asarray(v) for k, v in i.items()}
    f = np.float32
    c = np.ascontiguousarray
    o = {}
    o["xT"] = c(a["x"][0].T)
    o["metaT"] = c(a["meta_tokens"].T)
    w = a["w_in"][0]
    r = np.arange
    hd = lambda base, h: base + 64 * h
    QA, KA, VA, QB, CK, KRP, QI, KI, WI, GA, GB = 0, 512, 1024, 1536, 2048, 2176, 2192, 2704, 2768, 2776, 3800
    def nope(base):
        return np.concatenate([np.concatenate([hd(base, h) + 16 + r(48), hd(base, h) + r(16)]) for h in range(8)])
    sw = np.concatenate([8 + r(8), r(8)])
    def rope(base, step):
        return (np.concatenate([base + step * h + r(16) for h in range(8)]),
                np.concatenate([base + step * h + sw for h in range(8)]))
    rba, rbb = rope(QB, 64)
    kra, krb = rope(KRP, 0)
    ria, rib = rope(QI, 64)
    kin = np.concatenate([KI + 16 + r(48), KI + r(16)] * 2)
    main = np.concatenate([KA + r(512), QA + r(512), VA + r(512), nope(QB), rba, rbb, kra, krb, CK + r(128), kin,
                           ria, rib, nope(QI), GA + r(1024), GB + r(1024)])
    small = np.concatenate([KI + r(16), KI + sw, WI + r(8)])
    def tiles(m, n):
        k, nn = m.shape
        return c(m.reshape(k // 128, 128, nn // n, n).transpose(2, 1, 0, 3).reshape(nn // n, 128, -1))
    o["wp1"] = tiles(w[:, main], 512)
    o["wp1s"] = tiles(w[:, small], 40)[0]
    wk = np.zeros((128, 4, 128), f)
    uk = a["w_uk"][0].transpose(0, 2, 1)
    wk[0:48] = uk[0::2].transpose(1, 0, 2)
    wk[64:112] = uk[1::2].transpose(1, 0, 2)
    o["wukT"] = wk
    o["wuv"] = c(a["w_uv"][0].transpose(1, 0, 2))
    o["wupa"] = c(a["w_up_a"][0].reshape(4, 128, 1024).transpose(1, 0, 2))
    o["wupb"] = c(a["w_up_b"][0].reshape(4, 128, 1024).transpose(1, 0, 2))
    o["wo"] = tiles(a["w_o"][0], 512)
    inv = (f(500000.0) ** (-r(8).astype(f) / f(8))).astype(f)
    ang = r(528).astype(f)[:, None] * inv[None]
    p = r(128)
    o["cos"] = c(np.cos(ang)[:, p % 8].T.astype(f))
    o["sin"] = c((np.sin(ang)[:, p % 8].T * np.where((p // 8) % 2, 1, -1)[:, None]).astype(f))
    q = r(128)
    P_, Q_ = p[:, None], q[None]
    sel = np.zeros((128, 240), f); sel[:, 112:128] = -1
    blk = (P_ // 64 == Q_ // 64) / 64
    cst = [P_ == Q_, np.ones((128, 128)), -np.ones((128, 128)), -(P_ >= Q_).astype(f), P_ < Q_,
           -((P_ // 16 == Q_ // 16) & (P_ >= Q_)).astype(f), sel, P_ // 16 == r(8)[None], blk, Q_ + 0 * P_]
    o["cst"] = c(np.concatenate([x.astype(f) for x in cst], 1))
    col = lambda v: v.reshape(-1, 128).T
    o["vec"] = c(np.concatenate([col(x) for x in (
        a["norm_mix_g"][0], a["norm_ffn_g"][0], a["norm_final_g"], a["norm1_g_2"][0], a["norm2_g_2"][0], a["b_ada_2"][0],
        a["c_2"][0], a["conv_w_2"][0].reshape(-1), a["conv_out_g_2"][0], )], 1).astype(f))
    ag = a["attn_out_g_2"][0].reshape(8, 64)
    ag = np.concatenate([np.concatenate([ag[j], ag[j + 4]])[:, None] for j in range(4)], 1)
    qg = np.tile(a["q_norm_g_2"][0], 2)[:, None]; kg = np.tile(a["k_norm_g_2"][0], 2)[:, None]
    o["vec"] = c(np.concatenate([o["vec"], ag, qg, kg], 1))
    def rep(x): return c(np.broadcast_to(x[None], (128,) + x.shape).astype(f))
    gr = np.concatenate([a["w_group"][0], a["w_router"][0]], 1)
    o["wgr"] = tiles(gr, 36)[0]
    o["bgr"] = rep(np.concatenate([a["b_group"][0], a["b_router"][0]]))
    o["snk"] = rep(a["sinks_2"][0])
    o["wada"] = tiles(a["w_ada_2"][0], 512)
    w2i = a["w_in_2"][0]
    qp = np.concatenate([np.concatenate([1536 + 64 * j + r(64), 1536 + 64 * (j + 4) + r(64)]) for j in range(4)])
    o["win2"] = tiles(w2i[:, np.concatenate([512 + r(512), 1024 + r(512), r(512), qp])], 512)
    o["win2s"] = tiles(w2i[:, 2048:2304], 256)[0]
    rows = np.concatenate([r(512)] + [np.concatenate([512 + 64 * j + r(64), 512 + 64 * (j + 4) + r(64)]) for j in range(4)])
    o["wout2"] = tiles(a["w_out_2"][0][rows], 512)
    o["wq"] = tiles(a["peer_wq_2"][0], 512)
    o["keysT"] = c(a["peer_keys_2"][0].transpose(3, 1, 0, 2).reshape(128, 16, 128))
    o["relb"] = a["rel_bias_2"]
    d = np.maximum(r(128), 1).astype(f)
    big = 16 + (np.log(d / f(16)) / f(np.log(8.0)) * f(16)).astype(np.int32)
    bucket = np.where(r(128) < 16, r(128), np.minimum(big, 31))
    o["hot"] = c((r(32)[:, None] == bucket[None]).astype(f))
    u = a["peer_u_2"][0].reshape(64, 2, 128, 8, 128)
    o["uT"] = c(u.transpose(0, 4, 1, 3, 2).reshape(64, 128, 2048))
    v = a["peer_v_2"][0].reshape(16, 2, 4, 128, 2, 512)
    o["v"] = c(v.transpose(0, 4, 1, 3, 2, 5).reshape(64, 128, 2048))
    o["w1"] = a["w1"][0]; o["w3"] = a["w3"][0]; o["w2"] = a["w2"][0]
    return o


def kernel(**inputs):
    import concourse.bacc as bacc
    from concourse.bass_utils import run_bass_kernel_spmd

    arrays = layout(inputs)
    nc = bacc.Bacc("TRN2", target_bir_lowering=False, num_devices=1)
    args = {}
    for name, a in arrays.items():
        args[name] = nc.dram_tensor(name, a.shape, mybir.dt.from_np(a.dtype), kind="ExternalInput").ap()
    args["out"] = nc.dram_tensor("out", (1024, 512), F32, kind="ExternalOutput").ap()
    program(nc, args)
    r = run_bass_kernel_spmd(nc, [arrays], core_ids=[0])
    return np.ascontiguousarray(r.results[0]["out"].T)[None]
```

```python
import numpy as np

import concourse.bass as bass
from concourse import mybir
from concourse.alu_op_type import AluOpType as ALU
from contextlib import ExitStack

F32 = mybir.dt.float32
F32R = mybir.dt.float32r
U32 = mybir.dt.uint32
ACT = mybir.ActivationFunctionType
AX = mybir.AxisListType.X

T = 512
META = 16
TK = T + META
EPS = 1e-6


class Queue:

    def __init__(self, sem):
        self.sem, self.n, self.items, self.seen = sem, 0, [], {}

    def wait(self, *marks):
        for sem, value in marks:
            if self.seen.get(id(sem), 0) < value:
                self.seen[id(sem)] = value
                self.items.append((None, sem, value, None))

    def run(self, method, *args, mark=True, **kw):
        if mark:
            self.n += 1
        self.items.append((method, args, kw, (self.sem, 1) if mark else None))
        return (self.sem, self.n)

    def dma(self, method, out, in_, slot, **kw):
        slot.n += 16
        kw["out"], kw["in_"] = out, in_
        self.items.append((method, (), kw, (slot.sem, 16)))
        return (slot.sem, slot.n)

    def now(self):
        return (self.sem, self.n)

    def flush(self, eng):
        for item in self.items:
            if item[0] is None:
                eng.wait_ge(item[1], item[2])
            elif item[0] == "call":
                item[1](eng)
            else:
                ins = item[0](*item[1], **item[2])
                if item[3] is not None:
                    ins.then_inc(*item[3])


class Slot:

    def __init__(self, sem):
        self.sem, self.n = sem, 0

    def now(self):
        return (self.sem, self.n)


ARENA = 53200
RING = 4096
O_TEMP = 16384
O_XT = 40960
O_CST = 45184
O_WORK = 47360

C_ID, C_ONE, C_NEG, C_TRI, C_UP, C_TRIM, C_SEL, C_M8, C_BLK, C_IOTA = (
    0, 128, 256, 384, 512, 640, 768, 1008, 1016, 1144)
C_N = 1272
V_MIX, V_FFN, V_FIN, V_N1, V_N2, V_BADA, V_COND, V_CONV, V_CG, V_AG, V_QG, V_KG = (
    0, 8, 16, 24, 32, 40, 88, 96, 108, 112, 116, 117)
V_N = 118


def program(nc, A):
    with ExitStack() as ctx:
        build(nc, A, ctx)


def build(nc, A, ctx):
    with nc.sbuf_tensor("arena", [128, ARENA], F32) as AR:
        pass
    PS = ctx.enter_context(nc.psum_tensor("psum", [128, 8, 512], F32))

    def new_sem(name):
        return ctx.enter_context(nc.semaphore(name))

    pe, ac, dv, po, sp = (Queue(new_sem("s_" + n)) for n in ("pe", "act", "dve", "pool", "sp"))
    engines = (pe, ac, dv, po)
    te, se, ve, ge, sy = nc.tensor, nc.scalar, nc.vector, nc.gpsimd, nc.sync

    names = {}

    def alias(off, words):
        if (off, words) not in names:
            with nc.sbuf_tensor(f"before_{off}_{words}", [128, off], F32):
                with nc.sbuf_tensor(f"rounded_{off}_{words}", [128, words], F32R) as r:
                    names[off, words] = r
        return names[off, words]

    def parts(tensor, a, b):
        return tensor[:, :].rearrange("p (s a b) -> p s a b", s=2, a=a)

    def to_parts(tensor, src, a, b, mark):
        v = parts(tensor, a, b)
        ac.wait(*mark)
        t = ac.run(se.activation, v[:, 0], src, ACT.Copy)
        dv.wait(t, *mark)
        return dv.run(ve.tensor_tensor, v[:, 1], src, v[:, 0].bitcast(F32), ALU.subtract)

    THREE = ((0, 0), (0, 1), (1, 0))

    def projector(places, seq):
        made, used = [], []

        def weights():
            j = len(used)
            while len(made) < min(j + len(places), len(seq)):
                i = len(made)
                p, c, last, kk = (seq[i] + (8,))[:4]
                mark = [use(p)] + ([used[i - len(places)]] if i >= len(places) else [])
                t = to_parts(places[i % len(places)], pos(p, kk)[:, :, c:c + 1024 // kk], kk, 1024 // kk, mark)
                made.append(t)
                if last:
                    release(p, t)
            pe.wait(made[j])
            kk = (seq[j] + (8,))[3]
            return parts(places[j % len(places)], kk, 1024 // kk)

        def project(R, ready, b, hs=((0, 512),), base=0):
            w = weights()
            claim(*range(b, b + len(hs)))
            for i, (a, n) in enumerate(hs):
                for k in range(8):
                    pe.wait(ready[k // 2])
                    h = parts(R[k // 2], 2, R[k // 2].shape[1] // 4)
                    for m, (x, y) in enumerate(THREE):
                        end = k == 7 and m == 2
                        t = mm(PS[:, b + i, 0:n], w[:, x, k, :], h[:, y, k % 2, base + a:base + a + n], k == 0 and m == 0, end,
                               mark=end)
            used.append(t)
            return t

        return project, weights, used

    def slot(name):
        return Slot(new_sem("d_" + name))

    def at(off, n):
        return AR[:, off:off + n]

    def at3(off, a, b):
        return AR[:, off:off + a * b].rearrange("p (a b) -> p a b", a=a)

    def mm(out, l, r, start, stop, mark=False):
        return pe.run(te.matmul, out, l, r, start=start, stop=stop, mark=mark, skip_group_check=True)

    def turn(out, i, mark=False):
        k = i.shape[0]
        return pe.run(te.transpose, out, i, CST[0:k, C_ID:C_ID + k], mark=mark)

    def barrier(*extra):
        marks = [q.now() for q in engines] + list(extra)
        for q in engines + (sp,):
            q.wait(*marks)

    ring_sem = [slot(f"ring{i}") for i in range(9)]
    pieces = []
    loaded = {}
    needs = {}

    def ring_at(s, width):
        return at(s * RING, width)

    def piece(src, width, s):
        pieces.append((src, width, s))
        return len(pieces) - 1

    state = {"next": 0}

    def load_ready():
        while state["next"] < len(pieces):
            src, width, (sem, off) = pieces[state["next"]]
            if (sem, off) in state and state[(sem, off)] is None:
                return
            mark = state.get((sem, off))
            if mark is not None:
                sp.wait(*mark)
            sp.wait(*needs.get(state["next"], ()))
            loaded[state["next"]] = sp.dma(sy.dma_start, at(off, width), src, ring_sem[sem])
            state[(sem, off)] = None
            state["next"] += 1

    def use(i):
        if i not in loaded:
            load_ready()
        return loaded[i]

    def release(i, *marks):
        _, _, key = pieces[i]
        state[key] = marks
        load_ready()

    def pos(i, kk):
        src, width, (sem, off) = pieces[i]
        return at3(off, kk, width // kk)

    XT = at3(O_XT, 8, TK)
    CST = at(O_CST, C_N)
    VEC = at(O_CST + C_N, V_N)
    SMALL = O_CST + C_N + V_N
    assert SMALL <= O_WORK
    ONE = CST[:, C_ONE:C_ONE + 128]
    NEG = CST[:, C_NEG:C_NEG + 128]
    TRI = CST[:, C_TRI:C_TRI + 128]
    UP = CST[:, C_UP:C_UP + 128]

    s_in = slot("in")
    t_in = sp.dma(sy.dma_start, XT[:, :, 0:META], A["metaT"].rearrange("(k p) t -> p k t", p=128), s_in)
    t_in = sp.dma(sy.dma_start, XT[:, :, META:TK], A["xT"].rearrange("(k p) t -> p k t", p=128), s_in)
    t_in = sp.dma(sy.dma_start, CST, A["cst"], s_in)
    t_in = sp.dma(sy.dma_start, VEC, A["vec"], s_in)
    for q in engines:
        q.wait(t_in)

    PROJ = [piece(A["wp1"][i], 4096, (i % 2, (i % 2) * RING)) for i in range(7)]
    PSM = piece(A["wp1s"], 320, (1, RING))
    state[2, 2 * RING] = state[3, 3 * RING] = None
    PA = [piece(A["wada"][i], 4096, (i % 4, (i % 4) * RING)) for i in range(12)]
    PG = [piece(A["wp1"][7 + i], 4096, (i % 2, (i % 2) * RING)) for i in range(4)]
    PUP = [piece(A[name], 4096, (i, i * RING)) for i, name in enumerate(("wupa", "wupb"))]
    MOD = at(SMALL, 48)
    SC8 = at(SMALL + 140, 8)
    assert SMALL + 148 <= O_WORK
    t_cond = ac.run(se.activation, SC8, VEC[:, V_COND:V_COND + 8], ACT.Silu)

    o = O_TEMP
    UT = at3(o, 8, TK); o += 8 * TK
    KA = at3(o, 4, TK); o += 4 * TK
    QA = at3(o, 4, T); o += 4 * T
    VA = at3(o, 4, T); o += 4 * T
    QLAT = at3(o, 8, T); o_qlat = o; o += 8 * T
    QI = at3(o, 4, T); o_qi = o; o += 4 * T
    KI = at(o, TK); o += TK
    CKT = at(o, TK); o += TK
    o_ckv = o
    CKV = at3(o, 5, 128); o += 640
    RB = at(o, T); o += T
    KR = at(o, TK); o += TK
    WI = at3(o, 4, 8); o += 32
    WUK = at3(o, 4, 128); o += 512
    WUV = at3(o, 8, 64); o += 512
    o_kmb = o
    KMB = at3(o, 4, 128); o += 512
    VM2 = at(o, T); o += T
    PM = at(o, T); o += T
    YA = at3(o, 4, T); o += 4 * T
    assert o <= O_XT, o
    OW = O_WORK
    SQ = at3(o_qi, 4, TK)
    RN = at(OW, TK)
    COS = at(OW + TK, TK)
    SIN = at(OW + 2 * TK, TK)
    T1 = at(OW + 3 * TK, TK)
    T2 = at(OW + 4 * TK, TK)
    QBN = at3(o_qlat, 4, T)
    s_w = slot("w")
    t_tab = sp.dma(sy.dma_start, COS, A["cos"], s_w)
    t_tab = sp.dma(sy.dma_start, SIN, A["sin"], s_w)
    t_tab = sp.dma(sy.dma_start, WUK, A["wukT"], s_w)
    t_tab = sp.dma(sy.dma_start, WUV, A["wuv"], s_w)
    load_ready()

    def halves(n):
        return [(0, n)] if n <= 512 else [(0, n // 2), (n // 2, n - n // 2)]

    def norm(X, c0, n, U, gcol, squares, r, bank, cols=None):
        hs = halves(n)
        sq_free = {}
        for k in range(8):
            b = k % squares.shape[1]
            s = squares[:, b, 0:n]
            x = X[:, k, c0:c0 + n]
            if k % 2 == 0:
                if b in sq_free:
                    ac.wait(sq_free[b])
                t = ac.run(se.activation, s, x, ACT.Square)
            else:
                if b in sq_free:
                    dv.wait(sq_free[b])
                t = dv.run(ve.tensor_tensor, s, x, x, ALU.mult)
            pe.wait(t)
            for i, (a, w) in enumerate(hs):
                t = mm(PS[:, bank + i, 0:w], ONE, s[:, a:a + w], k == 0, k == 7, mark=True)
            sq_free[b] = t
        dv.wait(t)
        for i, (a, w) in enumerate(hs):
            t = dv.run(ve.tensor_scalar, r[:, a:a + w], PS[:, bank + i, 0:w], 1.0 / 1024, EPS, ALU.mult, ALU.add)
        ac.wait(t)
        t = ac.run(se.activation, r[:, 0:n], r[:, 0:n], ACT.Sqrt)
        dv.wait(t)
        t = dv.run(ve.reciprocal, r[:, 0:n], r[:, 0:n])
        dv.wait(t)
        for k in range(8):
            t = dv.run(ve.scalar_tensor_tensor, U[:, k, 0:n], X[:, k, c0:c0 + n], (VEC[:, gcol + k:gcol + k + 1] if cols is None else cols[:, k:k + 1]),
                       r[:, 0:n], ALU.mult, ALU.mult)
        return t

    t_ut = norm(XT, 0, TK, UT, V_MIX, SQ, RN, 0)
    pe.wait(t_ut)

    def proj(W, c, m, b, p0, hs, X=None, base=0, kk=8):
        X = UT if X is None else X
        for i, (a, w) in enumerate(hs):
            for k in range(kk):
                t = mm(PS[p0:p0 + m, b + i, 0:w], W[:, k, c:c + m], X[:, k, base + a:base + a + w],
                       k == 0, k == kk - 1, mark=(k == kk - 1))
        return t

    FULL = halves(TK)
    XONLY = [(0, T)]
    bank_free = [None] * 8

    def claim(*banks):
        for b in banks:
            if bank_free[b] is not None:
                pe.wait(*bank_free[b])

    def evac(q, out, in_, b, t, scale=None):
        q.wait(t)
        if q is ac:
            t = ac.run(se.activation, out, in_, ACT.Copy, scale=1.0 if scale is None else scale)
        elif scale is None:
            t = dv.run(ve.tensor_copy, out, in_)
        else:
            t = dv.run(ve.tensor_scalar, out, in_, scale, None, ALU.mult)
        return t

    ZERO = at(o_ckv, 512)
    s_z = slot("z")
    CAP = 64
    NX = (1024 - 32) // CAP
    ROWS = 32 * CAP + NX * CAP
    xb = nc.dram_tensor("xb", [ROWS, 1024], F32, kind="Internal").ap()
    yb = nc.dram_tensor("yb", [ROWS, 1024], F32, kind="Internal").ap()
    t = dv.run(ve.memset, ZERO, 0.0)
    sp.wait(t)
    n0 = NX * CAP * 2 // 128
    ybt = yb.rearrange("r (a c) -> (r a) c", a=2)[64 * CAP:2 * ROWS, :]
    sp.dma(sy.dma_start, ybt[0:128 * n0, :].rearrange("(n p) c -> p n c", p=128), ZERO.unsqueeze(1).to_broadcast([128, n0, 512]), s_z)
    if NX * CAP * 2 > 128 * n0:
        sp.dma(sy.dma_start, ybt[128 * n0:, :], ZERO[0:NX * CAP * 2 - 128 * n0, :], s_z)
    nz = ROWS * 2 // 128
    sp.dma(sy.dma_start, xb.rearrange("r (a c) -> (r a) c", a=2)[0:128 * nz, :].rearrange("(n p) c -> p n c", p=128),
           ZERO.unsqueeze(1).to_broadcast([128, nz, 512]), s_z)
    if ROWS * 2 > 128 * nz:
        sp.dma(sy.dma_start, xb.rearrange("r (a c) -> (r a) c", a=2)[128 * nz:2 * ROWS, :], ZERO[0:2 * ROWS - 128 * nz, :], s_z)

    UTR = [alias(2 * RING + 2112 * i, 2112) for i in range(3)] + [alias(o_kmb + 2048, 2112)]
    assert o_kmb + 2048 + 2112 <= O_XT
    WSP = [alias(o_qlat + 4 * T, 2048), alias(o_kmb, 2048), alias(OW + 6 * TK, 2048)]
    ready = [to_parts(UTR[k], UT[:, 2 * k:2 * k + 2, :], 2, TK, [t_ut]) for k in range(4)]
    project, _, _ = projector(WSP, [(PROJ[p], 128 * c, c == 3) for p in (0, 1, 3, 4, 5, 6) for c in range(4)])
    for j in range(4):
        b = 2 * j
        t = project(UTR, ready, b, FULL)
        t = evac((ac, dv)[j % 2], KA[:, j, :].rearrange("p (a b) -> p a b", a=2), PS[:, b:b + 2, 0:264], b, t)
        bank_free[b] = bank_free[b + 1] = (t,)
    for j in range(4):
        t = project(UTR, ready, j, XONLY, META)
        t = evac((ac, dv)[j % 2], QA[:, j, :], PS[:, j, :], j, t, scale=0.125)
        bank_free[j] = (t,)
    pe.wait(use(PROJ[2]))
    W = pos(PROJ[2], 8)
    for j in range(4):
        claim(4 + j)
        for k in range(8):
            t = mm(PS[:, 4 + j, :], UT[:, k, META + 128 * j:META + 128 * j + 128], W[:, k, :], k == 0, k == 7, mark=k == 7)
        t = evac((ac, dv)[j % 2], VA[:, j, :], PS[:, 4 + j, :], 4 + j, t)
        bank_free[4 + j] = (t,)
    UR = at3(OW + 3 * TK, 8, 128)
    dv.wait(t_ut)
    t = dv.run(ve.tensor_copy, UR.rearrange("p k (r m) -> p k r m", r=8),
               UT[:, :, 0:META].unsqueeze(2).to_broadcast([128, 8, 8, META]))
    pe.wait(t)
    claim(0)
    for k in range(8):
        t = mm(PS[:, 0, :], UR[:, k, :], W[:, k, :], k == 0, k == 7, mark=k == 7)
    release(PROJ[2], pe.now())
    VM = at(OW + 6 * TK + 2048, T)
    dv.wait(t)
    t = dv.run(ve.tensor_tensor, VM.rearrange("p (h d) -> p h d", h=8), PS[:, 0, :].rearrange("p (h d) -> p h d", h=8),
               CST[:, C_M8:C_M8 + 8].unsqueeze(2).to_broadcast([128, 8, 64]), ALU.mult)
    bank_free[0] = (t,)
    for j in range(4):
        b = (1, 2, 3, 4)[j]
        t = project(UTR, ready, b, XONLY, META)
        t = evac((ac, dv)[j % 2], QBN[:, j, :], PS[:, b, :], b, t, scale=0.125)
        bank_free[b] = (t,)

    dv.wait(t_tab)

    def rotated(W, ca, cb, m, hs, base, b, out, scale=1.0):
        n = sum(w for _, w in hs)
        nb = len(hs)
        w = n // nb
        claim(*range(b, b + 2 * nb))
        if W is None:
            project(UTR, ready, b, hs, base)
            t = project(UTR, ready, b + nb, hs, base)
        else:
            proj(W, ca, m, b, 0, hs, base=base)
            t = proj(W, cb, m, b + nb, 0, hs, base=base)
        dv.wait(t)
        co, si = (x[0:m, base:base + n].rearrange("p (a b) -> p a b", a=nb) for x in (COS, SIN))
        t1, t2, ou = (x[0:m, 0:n].rearrange("p (a b) -> p a b", a=nb) for x in (T1, T2, out))
        dv.run(ve.scalar_tensor_tensor, t1, PS[0:m, b:b + nb, 0:w], scale, co, ALU.mult, ALU.mult)
        t = dv.run(ve.scalar_tensor_tensor, t2, PS[0:m, b + nb:b + 2 * nb, 0:w], scale, si, ALU.mult, ALU.mult)
        for i in range(b, b + 2 * nb):
            bank_free[i] = (t,)
        dv.wait(t)
        return dv.run(ve.tensor_tensor, ou, t1, t2, ALU.add)

    dv.wait(t)
    t = rotated(None, 0, 128, 128, XONLY, META, 0, RB, 0.125)
    dv.wait(t)
    t = rotated(None, 256, 384, 128, FULL, 0, 4, KR)
    t_kr = t
    t = project(UTR, ready, 2, FULL)
    t = evac(ac, CKT.rearrange("p (a b) -> p a b", a=2), PS[:, 2:4, 0:264], 2, t)
    bank_free[2] = bank_free[3] = (t,)
    t_kin = project(UTR, ready, 4, FULL)
    pe.wait(t)
    claim(0, 1)
    for i in range(4):
        t = turn(PS[:, 0, 128 * i:128 * i + 128], CKT[:, 128 * i:128 * i + 128], mark=True)
    dv.wait(s_z.now())
    t = evac(dv, CKV[:, 0:4, :], PS[:, 0, :].rearrange("p (a b) -> p a b", a=4), 0, t)
    bank_free[0] = (t,)
    t = turn(PS[0:16, 1, 0:128], CKT[:, 512:528], mark=True)
    t = evac(dv, CKV[0:16, 4, :], PS[0:16, 1, 0:128], 1, t)
    bank_free[1] = (t,)
    t_kin = evac(ac, KI.rearrange("p (a b) -> p a b", a=2), PS[:, 4:6, 0:264], 4, t_kin)
    bank_free[4] = bank_free[5] = (t_kin,)
    dv.wait(t_kr)
    RI = at(OW, T)
    t_ri = rotated(None, 256, 384, 128, XONLY, META, 6, RI)
    for j in range(4):
        t = project(UTR, ready, j, XONLY, META)
        t = evac((ac, dv)[j % 2], QI[:, j, :], PS[:, j, :], j, t)
        bank_free[j] = (t,)
    t_qin = (ac.now(), dv.now())
    pe.wait(use(PSM))
    W = pos(PSM, 8)
    dv.wait(t_ri)
    RK = at(OW + 5 * TK, TK)
    t_rk = rotated(W, 0, 16, 16, FULL, 0, 4, RK)
    claim(0)
    for i in range(4):
        for k in range(8):
            t = mm(PS[:, 0, 8 * i:8 * i + 8], UT[:, k, META + 128 * i:META + 128 * i + 128], W[:, k, 32:40], k == 0, k == 7,
                   mark=k == 7)
    t_wi = evac(dv, WI, PS[:, 0, 0:32].rearrange("p (a b) -> p a b", a=4), 0, t)
    bank_free[0] = (t_wi,)
    release(PSM, pe.now())
    sp.wait(t_kin, t_ri, t_rk, *t_qin)
    for h in range(8):
        p0 = 64 * (h % 2) + 48
        t_rot = sp.dma(sy.dma_start, QI[p0:p0 + 16, h // 2, :], RI[16 * h:16 * h + 16, :], s_w)
    t_rot = sp.dma(sy.dma_start, KI[48:64, :], RK[0:16, :], s_w)
    t_rot = sp.dma(sy.dma_start, KI[112:128, :], RK[0:16, :], s_w)
    pe.wait(t_tab)
    for q in (ac, dv):
        pe.wait(q.now())
    claim(*range(8))
    for h in range(8):
        p0 = 64 * (h % 2)
        t = mm(PS[:, h, :], WUK[p0:p0 + 48, h // 2, :], QBN[p0:p0 + 48, h // 2, :], True, True, mark=True)
    t_all = t
    dv.wait(t_all)
    t_vm = dv.run(ve.tensor_copy, VM2, VM)
    VM = VM2
    ac.wait(t_all, t_vm)
    dv.wait(t_vm)
    for h in range(8):
        t = evac((ac, dv)[h % 2], QLAT[:, h, :], PS[:, h, :], h, t_all)
        bank_free[h] = (t,)
    for q in engines:
        q.wait(t_rot)
    barrier()

    state[2, 2 * RING] = state[3, 3 * RING] = [q.now() for q in engines]
    load_ready()

    ac.run(se.preload_act_table_set, "natural_log_exp_and_others", mark=False)
    t = po.run(ge.memset, KMB, 0.0)
    po.wait(t)
    for h in range(8):
        p0 = 64 * (h % 2)
        t_kmb = po.run(ge.tensor_copy, KMB[p0:p0 + 64, h // 2, 16 * h:16 * h + 16], KA[p0:p0 + 64, h // 2, 0:META])
    ada_done = []

    def ada_steps():
        dv.wait(t_cond)
        for c in range(12):
            w = pos(PA[c], 8)
            dv.wait(use(PA[c]))
            t = dv.run(ve.tensor_scalar, w[:, 0, :], w[:, 0, :], SC8[:, 0:1], None, ALU.mult)
            yield
            for k in range(1, 8):
                dv.wait(t)
                t = dv.run(ve.scalar_tensor_tensor, w[:, 0, :], w[:, k, :], SC8[:, k:k + 1], w[:, 0, :], ALU.mult, ALU.add)
                if k < 7:
                    yield
            ada_done.append((c, t))
            yield

    def ada_sums(b):
        if not ada_done:
            return
        claim(b)
        c0, n = ada_done[0][0], len(ada_done)
        for c, t in ada_done:
            pe.wait(t)
            for i in range(4):
                t = mm(PS[:, b, 4 * (c - c0) + i:4 * (c - c0) + i + 1], pos(PA[c], 8)[:, 0, 128 * i:128 * i + 128], ONE[:, 0:1],
                       False, True, mark=i == 3)
            release(PA[c], t)
        ada_done.clear()
        dv.wait(t)
        t = dv.run(ve.tensor_tensor, MOD[:, 4 * c0:4 * (c0 + n)], PS[:, b, 0:4 * n],
                   VEC[:, V_BADA + 4 * c0:V_BADA + 4 * (c0 + n)], ALU.add)
        bank_free[b] = (t,)

    ada = ada_steps()
    NQ = [T - 128 * kt for kt in range(4)]
    OFF = [0, 512, 896, 1152]

    def by_tile(off):
        return [AR[:, off + OFF[kt]:off + OFF[kt] + NQ[kt]] for kt in range(4)]

    EX = [by_tile(OW + 1280 * i) for i in range(2)]
    PT = [by_tile(OW + 2560 + 1280 * i) for i in range(2)]

    def softplus(z, e, out, p, marks):
        ac.wait(*marks)
        t = ac.run(se.activation, e, z, ACT.Abs)
        ac.wait(t)
        t = ac.run(se.activation, e, e, ACT.Exp, scale=-1.0)
        ac.wait(t)
        t = ac.run(se.activation, e, e, ACT.Ln, bias=1.0)
        dv.wait(t)
        t = dv.run(ve.scalar_tensor_tensor, out, z, 0.0, e, ALU.max, ALU.add)
        for _ in range(3):
            next(ada, None)
        return t

    def strict(x, t):
        po.wait(t)
        return po.run(ge.affine_select, out=x, in_=x, pattern=[[1, 128]], compare_op=ALU.is_gt, fill=0.0,
                      base=0, channel_multiplier=-1)

    pe.wait(t_kmb)
    claim(7)
    for j in range(4):
        t = mm(PS[:, 7, :], KMB[:, j, :], QA[:, j, :], j == 0, False, mark=j == 3)
    EM = EX[1][0]
    t_pm = softplus(PS[:, 7, :], EM, PM, 128, (t,))
    pe.wait(t_pm)
    t = mm(PS[:, 7, :], CST[:, C_TRIM:C_TRIM + 128], PM, False, False, mark=True)
    ex_free = [None, (t_pm,)]
    pt_free = [None, None]
    tps = {}

    def region(i, kt, a):
        return PS[:, 3 * i + 1, 0:128] if kt == 3 else PS[:, 3 * i + kt, a:T]

    def scores(h):
        i, j, p0 = h % 2, h // 2, 64 * (h % 2)
        claim(3 * i, 3 * i + 1, 3 * i + 2)
        ts = []
        for kt in range(4):
            c = META + 128 * kt
            ts.append(mm(region(i, kt, 128 * kt), KA[p0:p0 + 64, j, c:c + 128], QA[p0:p0 + 64, j, 128 * kt:T], kt < 3, False,
                         mark=True))
        yield
        for x in (ex_free[i], pt_free[i]):
            if x is not None:
                ac.wait(*x)
                dv.wait(*x)
        for kt in range(4):
            t = softplus(region(i, kt, 128 * kt), EX[i][kt], PT[i][kt], 128,
                         (ts[3 if kt == 1 else kt],) + ((t_1,) if kt == 3 else ()))
            if kt == 1:
                t_1 = t
            tps[h, kt] = strict(PT[i][kt][:, 0:128], t)
            yield

    for _ in scores(0):
        pass
    for h in range(8):
        i, j, p0 = h % 2, h // 2, 64 * (h % 2)
        following = scores(h + 1) if h < 7 else iter(())
        next(following, None)
        ta = []
        for kt in (3, 2, 1, 0):
            pe.wait(tps[h, kt])
            mm(region(i, kt, 128 * kt), TRI, PT[i][kt], False, kt == 3, mark=kt == 3)
            for k2 in range(kt + 1, 4):
                mm(region(i, kt, 128 * k2), NEG, PT[i][k2], False, k2 == 3, mark=k2 == 3)
            t = pe.now()
            next(following, None)
            ac.wait(t)
            for x in {3: (), 2: (2,), 1: (3, 1), 0: (0,)}[kt]:
                t = ac.run(se.activation, EX[i][x], region(i, x, 128 * x), ACT.Exp)
                bank_free[3 * i + x % 3 if x < 3 else 3 * i + 1] = (t,)
                ta.append((x, strict(EX[i][x][:, 0:128], t)))
        sel = CST[:, C_SEL + 112 - 16 * h:C_SEL + 240 - 16 * h]
        for kt in range(4):
            t = mm(PS[:, 7, 128 * kt:T], sel, PT[i][kt], False, h == 7 and kt == 3, mark=True)
        pt_free[i] = (t,)
        ada_sums(3 * i + 2)
        if h % 2 == 0:
            claim(6)
        for kt, t in sorted(ta):
            pe.wait(t)
            t = mm(PS[p0:p0 + 64, 6, 128 * kt:T], VA[:, kt, 64 * h:64 * h + 64], EX[i][kt], kt == 0, kt == 3, mark=kt == 3)
        ex_free[i] = (t,)
        if h % 2 == 1:
            dv.wait(t)
            t = dv.run(ve.tensor_copy, YA[:, j, :], PS[:, 6, :])
            bank_free[6] = (t,)
    for _ in ada:
        pass
    ada_sums(5)
    ac.wait(pt_free[1][0], pt_free[0][0])
    t = ac.run(se.activation, PM, PS[:, 7, :], ACT.Exp)
    bank_free[7] = (t,)
    pe.wait(t)
    for j in range(4):
        claim(j)
        t = mm(PS[:, j, :], VM2[:, 128 * j:128 * j + 128], PM, True, True, mark=True)
        dv.wait(t, dv.now())
        t = dv.run(ve.tensor_tensor, YA[:, j, :], YA[:, j, :], PS[:, j, :], ALU.add)
        bank_free[j] = (t,)
    barrier()

    OLAT = at3(O_TEMP + 8 * TK, 8, T)
    YB = QI
    o_va = O_TEMP + 8 * TK + 4 * TK + 4 * T
    RS = [at(o_va + TK * i, TK) for i in range(2)]
    QM = at3(o_va + 2 * TK, 4, 128)
    P = at3(OW, 4, TK)
    PTR = at3(OW + 4 * TK, 5, 512)
    SC = at(OW + 4 * TK + 2560, TK)
    MB = at(OW + 5 * TK + 2560, TK)
    o = OW + 6 * TK + 2560
    M8 = at(o, 8)
    MX = at(o + 8, 4)
    SM = at(o + 12, 4)
    assert o + 16 <= ARENA
    rs_free = [None, None]
    GAB = at3(2 * RING, 16, T)
    pending = []
    n_gate = [0]

    def gates(*banks):
        for b in banks:
            while pending:
                bb, gg, t = pending.pop()
                t = evac(ac, GAB[:, 2 * (gg % 8) + gg // 8, :], PS[:, bb, :], bb, t)
                bank_free[bb] = (t,)
            i = n_gate[0]
            if i < 16:
                n_gate[0] += 1
                claim(b)
                pe.wait(use(PG[i // 4]))
                t = proj(pos(PG[i // 4], 8), 128 * (i % 4), 128, b, 0, XONLY, base=META)
                if i % 4 == 3:
                    release(PG[i // 4], t)
                pending.append((b, i, t))

    for n in range(4):
        nk = META + 128 * (n + 1)
        np_ = 1 if nk <= 512 else 2
        w = nk // np_
        ks = [(i * w, w) for i in range(np_)]
        q0 = 128 * n

        def view(x):
            return x[:, 0:nk].rearrange("p (a b) -> p a b", a=np_)

        def bank(b):
            return PS[:, b:b + np_, 0:w]

        sc = view(SC)
        for h in range(8):
            j, p0, b = h // 2, 64 * (h % 2), 2 * (h % 2)
            claim(*range(b, b + np_))
            for i, (a, _) in enumerate(ks):
                t = mm(PS[:, b + i, 0:w], QI[p0:p0 + 64, j, q0:q0 + 128], KI[p0:p0 + 64, a:a + w], True, True, mark=True)
            r = view(RS[h % 2])
            if rs_free[h % 2] is not None:
                ac.wait(rs_free[h % 2])
            ac.wait(t)
            t = ac.run(se.activation, r, bank(b), ACT.Relu)
            for x in range(b, b + np_):
                bank_free[x] = (t,)
            dv.wait(t, dv.now())
            if h == 0:
                t = dv.run(ve.tensor_scalar, sc, r, WI[:, n, h:h + 1], None, ALU.mult)
            else:
                t = dv.run(ve.scalar_tensor_tensor, sc, r, WI[:, n, h:h + 1], sc, ALU.mult, ALU.add)
            rs_free[h % 2] = t
        dv.wait(t)
        t = dv.run(ve.memset, SC[0:64, nk - 64:nk], -3.0e38)
        for i in range(16):
            dv.wait(t)
            t = dv.run(ve.max, M8, SC[:, 0:nk])
            dv.wait(t)
            t = dv.run(ve.match_replace, SC[:, 0:nk], M8, SC[:, 0:nk], -3.3e38)
        dv.wait(t)
        t = dv.run(ve.tensor_scalar, MB[:, 0:nk], SC[:, 0:nk], -3.2e38, -1.0e30, ALU.is_gt, ALU.mult)
        dv.wait(t)
        t_mb = dv.run(ve.memset, MB[0:64, nk - 64:nk], -1.0e30)
        mb = view(MB)
        gates(*((7, 1, 7) if n < 3 else (7, 7)))
        for g in range(2):
            if g or n:
                po.wait(t_qm)
            for h in range(4):
                t = po.run(ge.tensor_scalar, QM[:, h, :], RB[:, q0:q0 + 128], CST[:, C_M8 + 4 * g + h:C_M8 + 4 * g + h + 1],
                           None, ALU.mult)
            pe.wait(t)
            for h in range(4):
                b = 2 * (h % 2)
                claim(*range(b, b + np_))
                for i, (a, _) in enumerate(ks):
                    mm(PS[:, b + i, 0:w], QLAT[:, 4 * g + h, q0:q0 + 128], CKT[:, a:a + w], True, False)
                    t = mm(PS[:, b + i, 0:w], QM[:, h, :], KR[:, a:a + w], False, True, mark=True)
                t_qm = t
                dv.wait(t, t_mb)
                if g or n:
                    dv.wait(t_ptr)
                p = view(P[:, h, :])
                t = dv.run(ve.tensor_tensor, p, bank(b), mb, ALU.add)
                for x in range(b, b + np_):
                    bank_free[x] = (t,)
                dv.wait(t)
                t = dv.run(ve.tensor_reduce, MX[:, h:h + 1], P[:, h, 0:nk], AX, ALU.max, negate=True)
                ac.wait(t)
                t = ac.run(se.activation, P[:, h, 0:nk], P[:, h, 0:nk], ACT.Exp, bias=MX[:, h:h + 1], accum_out=SM[:, h:h + 1])
                dv.wait(t)
                t = dv.run(ve.reciprocal, SM[:, h:h + 1], SM[:, h:h + 1])
                dv.wait(t)
                t_p = dv.run(ve.tensor_scalar, P[:, h, 0:nk], P[:, h, 0:nk], SM[:, h:h + 1], None, ALU.mult)
            gates(7)
            pe.wait(t_p)
            for k in range(n + 2):
                m = 128 if k <= n else 16
                b = 4 + k % 2
                claim(b)
                for h in range(4):
                    t = turn(PS[0:m, b, 128 * h:128 * h + 128], P[:, h, 128 * k:128 * k + m], mark=h == 3)
                t_ptr = t
                q = (ac, dv)[k % 2]
                if g or n:
                    q.wait(t_ol)
                t = evac(q, PTR[0:m, k, :], PS[0:m, b, :], b, t)
                bank_free[b] = (t,)
            pe.wait(ac.now(), dv.now())
            claim(6)
            for k in range(n + 2):
                m = 128 if k <= n else 16
                t = mm(PS[:, 6, :], CKV[0:m, k, :], PTR[0:m, k, :], k == 0, k == n + 1, mark=k == n + 1)
            t_ol = t
            t = evac(ac, OLAT[:, 4 * g:4 * g + 4, q0:q0 + 128], PS[:, 6, :].rearrange("p (a b) -> p a b", a=4), 6, t)
            bank_free[6] = (t,)
    while n_gate[0] < 16 or pending:
        gates(7)
    pe.wait(t)
    for h in range(8):
        j, p0 = h // 2, 64 * (h % 2)
        if h % 2 == 0:
            claim(j)
        t = mm(PS[p0:p0 + 64, j, :], WUV[:, h, :], OLAT[:, h, :], True, True, mark=True)
        if h % 2 == 1:
            t = evac((ac, dv)[j % 2], YB[:, j, :], PS[:, j, :], j, t)
            bank_free[j] = (t,)
    barrier()

    o = O_TEMP + 8 * TK
    ZT = [at3(o + 1024 * i, 2, T) for i in range(2)]; o += 2048
    YR = [[alias(o + 4096 * x + 2048 * i, 2048) for i in range(2)] for x in range(2)]; o += 8192
    assert o <= o_qi
    WSP = [alias(x + 2048 * i, 2048) for x in (o_qi + 4 * T, OW) for i in range(2)]
    assert o_qi + 4 * T + 4096 <= O_TEMP + 21904
    ZR = [alias(2 * RING + 2048 * i, 2048) for i in range(4)]
    GS = [at(OW + 4096 + 512 * i, 512) for i in range(3)]
    key_po = [(4, O_TEMP), (0, 0)]
    state[key_po[0]] = [q.now() for q in engines]
    PO = [piece(A["wo"][i], 4096, key_po[i]) for i in range(2)]
    load_ready()
    y_ready = [[to_parts(YR[x][i], Y[:, 2 * i:2 * i + 2, :], 2, T, []) for i in range(2)] for x, Y in enumerate((YA, YB))]
    project, weights, used = projector(WSP, [(PUP[x], 256 * m, m == 3, 4) for m in range(4) for x in range(2)]
                                       + [(PO[i], 128 * c, c == 3) for i in range(2) for c in range(4)])
    gs_free = None
    z_ready = []
    for m in range(4):
        b = 4 * (m % 2)
        claim(b, b + 1, b + 2, b + 3)
        for x in range(2):
            w = weights()
            for i in range(2):
                for k in range(4):
                    pe.wait(y_ready[x][k // 2])
                    h = parts(YR[x][k // 2], 2, T)
                    for n, (y, z) in enumerate(THREE):
                        end = k == 3 and n == 2
                        t = mm(PS[:, b + 2 * i + x, :], w[:, y, k, 128 * i:128 * i + 128], h[:, z, k % 2, :], k == 0 and n == 0, end,
                               mark=end)
            used.append(t)
        zt = ZT[m % 2]
        if m > 1:
            dv.wait(z_ready[m - 2])
        for i in range(2):
            if gs_free is not None:
                ac.wait(gs_free)
            ac.run(se.activation, GS[0], GAB[:, 4 * m + 2 * i, :], ACT.Sigmoid)
            t2 = ac.run(se.activation, GS[1], GAB[:, 4 * m + 2 * i + 1, :], ACT.Sigmoid)
            dv.wait(t, t2)
            dv.run(ve.tensor_tensor, GS[2], GS[0], PS[:, b + 2 * i, :], ALU.mult)
            t3 = dv.run(ve.tensor_tensor, GS[1], GS[1], PS[:, b + 2 * i + 1, :], ALU.mult)
            bank_free[b + 2 * i] = bank_free[b + 2 * i + 1] = (t3,)
            dv.wait(t3)
            gs_free = dv.run(ve.tensor_tensor, zt[:, i, :], GS[2], GS[1], ALU.add)
        z_ready.append(to_parts(ZR[m], zt, 2, T, [gs_free]))
    for i in range(8):
        t = project(ZR, z_ready, i)
        dv.wait(t)
        t = dv.run(ve.tensor_tensor, XT[:, i, META:TK], XT[:, i, META:TK], PS[:, i, :], ALU.add)
        bank_free[i] = (t,)
    barrier()


    o = O_TEMP + 2 * RING
    UT2 = at3(o, 8, T); o_ut2 = o; o += 8 * T
    UTOK = at3(o, 4, 1024); o_utok = o; o += 4096
    XR = [at(o + 1024 * i, 1024) for i in range(2)]; o += 2048
    XET = [at3(o + 1024 * i, 8, 128) for i in range(2)]; o += 2048
    o_w2x = o
    assert o + RING <= O_XT
    o = OW
    HS = [at(o + 256 * i, 256) for i in range(2)]; o += 512
    HT = [at3(o + 256 * i, 2, 128) for i in range(2)]; o += 512
    YS = [at(o + 512 * i, 512) for i in range(2)]; o += 1024
    o_rt = o
    o = SMALL
    o += 48
    ROW = at(o, 8).rearrange("p (n s) -> p n s", n=4); o += 8
    GATE = at(o, 8).rearrange("p (n s) -> p n s", n=4); o += 8
    XE = at(o, 32); o += 32
    FLAG = at(o, 1); o += 1
    S1 = at(o, 8); o += 8
    S2 = at(o, 8); o += 8
    SNK = at(o, 8); o += 8
    assert o <= O_WORK, (o, O_WORK)

    WGR = at3(o_rt, 8, 36)
    BGR = at(o_rt + 288, 36)
    s_rt = slot("rt")
    sp.dma(sy.dma_start, WGR, A["wgr"], s_rt)
    sp.dma(sy.dma_start, SNK, A["snk"], s_rt)
    RB8 = at(OW + 5672, 8)
    HOT = at(OW + 5680, 128)
    sp.dma(sy.dma_start, RB8[0:32, :], A["relb"], s_rt)
    sp.dma(sy.dma_start, HOT[0:32, :], A["hot"], s_rt)
    t_rt = sp.dma(sy.dma_start, BGR, A["bgr"], s_rt)
    experts = []
    ring9 = [(2, 2 * RING), (3, 3 * RING), (4, O_TEMP), (5, O_TEMP + RING), (0, 0), (1, RING), (6, o_w2x), (7, o_ut2), (8, o_utok)]
    n_p = 0
    for k4 in ring9:
        state[k4] = [q.now() for q in engines]
    state[ring9[7]] = state[ring9[8]] = None
    for e in range(32):
        ids = []
        for name in ("w1", "w3", "w2"):
            src = A[name][e].rearrange("(k p) n -> p k n", p=128)
            ids.append(piece(src, 4096, ring9[n_p % 9]))
            n_p += 1
        experts.append(ids)
    load_ready()

    s_sc = slot("scatter")

    def po_ind(n, i):
        s_sc.n += 16

        def emit(eng):
            eng.indirect_dma_start(out=xb, out_offset=bass.IndirectOffsetOnAxis(ap=ROW[:, n, i:i + 1].bitcast(U32), axis=0),
                                   in_=UTOK[:, n, :], in_offset=None).then_inc(s_sc.sem, 16)
        po.items.append(("call", emit))
        return s_sc.now()

    def gather(n, i):
        s_g[n].n += 16

        def emit(eng):
            eng.indirect_dma_start(out=GG[i][:, n, :], out_offset=None, in_=yb,
                                   in_offset=bass.IndirectOffsetOnAxis(ap=ROW[:, n, i:i + 1].bitcast(U32), axis=0),
                                   ).then_inc(s_g[n].sem, 16)
        po.items.append(("call", emit))
        return s_g[n].now()

    def toeplitz():
        for h in range(8):
            src = bass.AP(rs.tensor, 384 * h, [[1, 128], [1, 256]])
            t = sp.dma(sy.dma_start, BI[:, h, :], src, s_b)
        return t

    RT = o_rt
    LG = at3(RT + 324, 4, 36)
    G8 = at3(RT + 468, 4, 8)
    GM = at3(RT + 500, 4, 8)
    GI = at3(RT + 532, 4, 8)
    EG = at3(RT + 564, 4, 4)
    GS4 = at(RT + 580, 4)
    MK = at3(RT + 584, 4, 4)
    EM = at3(RT + 600, 4, 32)
    EV = at3(RT + 728, 4, 8)
    EI = at3(RT + 760, 4, 8)
    IF_ = at3(RT + 792, 4, 2)
    OH = [at3(RT + 800 + 128 * i, 4, 32) for i in range(3)]
    RK = at3(RT + 1184, 4, 32)
    CN = at(RT + 1312, 32)
    XC = at(RT + 1344, 32)
    XP = at(RT + 1376, 32)
    B1 = at3(RT + 1408, 4, 32)
    B2 = at3(RT + 1536, 4, 32)
    TM = at(RT + 1664, 32)
    RF = at3(RT + 1696, 4, 2)
    NG = at(RT + 1704, 4)
    GF = at(RT + 1708, 4)
    assert RT + 1712 <= ARENA
    IO = CST[:, C_IOTA:C_IOTA + 128]

    SQ2 = at3(OW, 2, T)
    RN2 = at(OW + 1024, T)
    t = norm(XT, META, T, UT2, V_FFN, SQ2, RN2, 0)
    for q in engines:
        q.wait(t, t_rt)
    for n in range(4):
        for k in range(8):
            t = mm(PS[:, 0, 36 * n:36 * n + 36], UT2[:, k, 128 * n:128 * n + 128], WGR[:, k, :], k == 0, k == 7, mark=k == 7)

    t_lg = t
    t_tok = []
    for n in range(4):
        b = 4 + 2 * (n % 2)
        claim(b, b + 1)
        for k in range(8):
            t = turn(PS[:, b + k // 4, 128 * (k % 4):128 * (k % 4) + 128], UT2[:, k, 128 * n:128 * n + 128], mark=k == 7)
        t = evac(ac, UTOK[:, n, :].rearrange("p (a b) -> p a b", a=2), PS[:, b:b + 2, :], b, t)
        bank_free[b] = bank_free[b + 1] = (t,)
        t_tok.append(t)
    state[ring9[7]] = [pe.now()]
    load_ready()

    def d(method, *a, **kw):
        dv.wait(dv.now())
        return dv.run(method, *a, **kw)

    dv.wait(t_lg)
    d(ve.tensor_tensor, LG, PS[:, 0, 0:144].rearrange("p (a b) -> p a b", a=4), BGR.unsqueeze(1).to_broadcast([128, 4, 36]),
      ALU.add)
    d(ve.memset, G8, -1.0e30)
    d(ve.tensor_copy, G8[:, :, 0:4], LG[:, :, 0:4])
    for n in range(4):
        d(ve.max, GM[:, n, :], G8[:, n, :])
        d(ve.max_index, GI[:, n, :].bitcast(U32), GM[:, n, :], G8[:, n, :])
    d(ve.tensor_copy, GF, GI[:, :, 0].bitcast(U32))
    t = d(ve.tensor_scalar, NG, GM[:, :, 0], -1.0, None, ALU.mult)
    ac.wait(t)
    for n in range(4):
        t = ac.run(se.activation, EG[:, n, :], LG[:, n, 0:4], ACT.Exp, bias=NG[:, n:n + 1], accum_out=GS4[:, n:n + 1])
    dv.wait(t)
    d(ve.reciprocal, GS4, GS4)
    d(ve.tensor_tensor, MK, IO[:, 0:4].unsqueeze(1).to_broadcast([128, 4, 4]), GF.unsqueeze(2).to_broadcast([128, 4, 4]),
      ALU.is_equal)
    mk8 = MK.unsqueeze(3).to_broadcast([128, 4, 4, 8])
    em = EM.rearrange("p n (g e) -> p n g e", g=4)
    d(ve.tensor_tensor, em, LG[:, :, 4:36].rearrange("p n (g e) -> p n g e", g=4), mk8, ALU.mult)
    d(ve.tensor_scalar, MK, MK, -1.0, 1.0e30, ALU.add, ALU.mult)
    d(ve.tensor_tensor, em, em, mk8, ALU.add)
    for n in range(4):
        d(ve.max, EV[:, n, :], EM[:, n, :])
        d(ve.max_index, EI[:, n, :].bitcast(U32), EV[:, n, :], EM[:, n, :])
    d(ve.tensor_copy, IF_, EI[:, :, 0:2].bitcast(U32))
    t = d(ve.tensor_tensor, NG, EV[:, :, 1], EV[:, :, 0], ALU.subtract)
    ac.wait(t)
    t = ac.run(se.activation, NG, NG, ACT.Exp)
    dv.wait(t)
    d(ve.tensor_scalar, GF, NG, 1.0, None, ALU.add)
    d(ve.reciprocal, GF, GF)
    d(ve.tensor_tensor, GATE[:, :, 0], GF, GS4, ALU.mult)
    d(ve.tensor_tensor, GATE[:, :, 1], GATE[:, :, 0], NG, ALU.mult)
    for i in range(2):
        d(ve.tensor_tensor, OH[i], IO[:, 0:32].unsqueeze(1).to_broadcast([128, 4, 32]),
          IF_[:, :, i:i + 1].to_broadcast([128, 4, 32]), ALU.is_equal)
    t = d(ve.tensor_tensor, OH[2], OH[0], OH[1], ALU.add)
    pe.wait(t)
    for n in range(4):
        for k in range(n):
            mm(PS[:, 1, 32 * n:32 * n + 32], ONE, OH[2][:, k, :], k == 0, False)
        mm(PS[:, 1, 32 * n:32 * n + 32], UP, OH[2][:, n, :], n == 0, True)
    for n in range(4):
        t = mm(PS[:, 2, 0:32], ONE, OH[2][:, n, :], n == 0, n == 3, mark=True)
    dv.wait(t)
    d(ve.tensor_copy, RK, PS[:, 1, 0:128].rearrange("p (a b) -> p a b", a=4))
    d(ve.tensor_copy, CN, PS[:, 2, 0:32])
    d(ve.tensor_scalar, XC, CN, float(CAP), None, ALU.is_gt)
    for m in range(2, (512 - 1) // CAP + 1):
        d(ve.tensor_scalar, TM, CN, float(CAP * m), None, ALU.is_gt)
        d(ve.tensor_tensor, XC, XC, TM, ALU.add)
    d(ve.tensor_tensor_scan, XP, ONE[:, 0:32], XC, 0.0, ALU.mult, ALU.add)
    d(ve.tensor_copy, FLAG.bitcast(U32), XP[:, 31:32])
    for i in range(NX):
        d(ve.tensor_scalar, TM, XP, float(i), None, ALU.is_le)
        d(ve.tensor_reduce, XE[:, i:i + 1], TM, AX, ALU.add)
    d(ve.tensor_scalar, XE[:, 0:NX], XE[:, 0:NX], 31.0, None, ALU.min)
    d(ve.tensor_copy, XE[:, 0:NX].bitcast(U32), XE[:, 0:NX])
    d(ve.tensor_tensor, XP, XP, XC, ALU.subtract)
    d(ve.tensor_tensor, XP, XP, IO[:, 0:32], ALU.subtract)
    d(ve.tensor_scalar, XP, XP, 31.0, float(CAP), ALU.add, ALU.mult)
    d(ve.tensor_scalar, B1, RK, float(CAP), None, ALU.is_ge)
    d(ve.tensor_tensor, B1, B1, XP.unsqueeze(1).to_broadcast([128, 4, 32]), ALU.mult)
    d(ve.tensor_tensor, B1, B1, RK, ALU.add)
    d(ve.tensor_scalar, TM, IO[:, 0:32], float(CAP), None, ALU.mult)
    d(ve.tensor_tensor, B1, B1, TM.unsqueeze(1).to_broadcast([128, 4, 32]), ALU.add)
    for i in range(2):
        d(ve.tensor_tensor, B2, B1, OH[i], ALU.mult)
        d(ve.tensor_reduce, RF[:, :, i:i + 1], B2, AX, ALU.add)
    t_row = d(ve.tensor_copy, ROW.bitcast(U32), RF)
    for n in range(4):
        po.wait(t_tok[n], t_row, s_z.now())
        for i in range(2):
            t_sc = po_ind(n, i)
    state[ring9[8]] = [t_sc]
    load_ready()
    barrier(t_sc)

    def expert(qs, w, rows, xt, x0, i, free, ysem):
        pe, ac, dv, sp = qs
        w1, w3, w2 = w

        def m2(out, l, r, start, stop):
            return pe.run(te.matmul, out, l, r, start=start, stop=stop, mark=stop, skip_group_check=True)

        b = 4 * i
        if free["h"][i]:
            pe.wait(*free["h"][i])
        for wt, ho in ((w1, b), (w3, b + 1)):
            for k in range(8):
                for half in range(2):
                    t = m2(PS[64 * half:64 * half + CAP, ho, 0:256], xt[:, k, x0:x0 + CAP],
                           wt[:, k, 256 * half:256 * half + 256], k == 0, k == 7)
        if free["hs"][i]:
            ac.wait(*free["hs"][i])
            dv.wait(*free["hs"][i])
        ac.wait(t)
        dv.wait(t)
        hs = [slice(0, CAP), slice(64, 64 + CAP)] if CAP < 64 else [slice(0, 128)]
        for p in hs:
            t = ac.run(se.activation, HS[i][p, :], PS[p, b, 0:256], ACT.Silu)
        dv.wait(t)
        for p in hs:
            t = dv.run(ve.tensor_tensor, HS[i][p, :], HS[i][p, :], PS[p, b + 1, 0:256], ALU.mult)
        free["h"][i] = (t,)
        pe.wait(t)
        if free["t"][i]:
            pe.wait(*free["t"][i])
        for c in range(2):
            for p in hs:
                n = p.stop - p.start
                t = pe.run(te.transpose, PS[:, b + 2, 128 * c + p.start:128 * c + p.stop], HS[i][p, 128 * c:128 * c + 128],
                           CST[p, C_ID + p.start:C_ID + p.stop], mark=True)
                pe.wait(t)
        free["hs"][i] = (t,)
        dv.wait(t)
        for p in hs:
            t = dv.run(ve.tensor_copy, HT[i][:, :, p], PS[:, b + 2, 0:256].rearrange("p (a b) -> p a b", a=2)[:, :, p])
        free["t"][i] = (t,)
        pe.wait(t)
        if free["y"][i]:
            pe.wait(*free["y"][i])
        for kt in range(4):
            for half in range(2):
                t = m2(PS[64 * half:64 * half + CAP, b + 3, :], HT[i][:, kt % 2, 64 * (kt // 2):64 * (kt // 2) + CAP],
                       w2[:, kt, 512 * half:512 * half + 512], kt == 0, kt == 3)
        t_w = t
        ac.wait(t)
        if free["ys"][i]:
            ac.wait(*free["ys"][i])
        for p in hs:
            t = ac.run(se.activation, YS[i][p, :], PS[p, b + 3, :], ACT.Copy)
        free["y"][i] = (t,)
        sp.wait(t)
        for half in range(2):
            t = sp.dma(ge.dma_start if sp is po else sy.dma_start, yb[rows:rows + CAP, 512 * half:512 * half + 512],
                       YS[i][64 * half:64 * half + CAP, :], ysem[i])
        free["ys"][i] = (t,)
        return t_w

    s_x = [slot(f"x{i}") for i in range(2)]
    s_y = [slot(f"y{i}") for i in range(2)]
    free = {k: [None, None] for k in ("h", "hs", "t", "y", "ys")}
    for b in range(8):
        bank_free[b] = None
    xr_free = [None, None]
    xt_free = [None, None]
    tx = {}

    def load_x(g):
        i = g % 2
        if xr_free[i] is not None:
            po.wait(*xr_free[i])
        tx[g] = po.dma(ge.dma_start, XR[i][0:2 * CAP, :], xb[2 * CAP * g:2 * CAP * g + 2 * CAP, :], s_x[i])

    load_x(0)
    load_x(1)
    for g in range(16):
        i = g % 2
        pe.wait(tx[g])
        for half in range(2):
            b = 4 * i + half
            f = free["h"][i]
            if f:
                pe.wait(*f)
            for k in range(4):
                kk = 4 * half + k
                t = turn(PS[:, b, 128 * k:128 * k + 2 * CAP], XR[i][0:2 * CAP, 128 * kk:128 * kk + 128], mark=k == 3)
            if xt_free[i]:
                (ac, dv)[half].wait(*xt_free[i])
            t2 = evac((ac, dv)[half], XET[i][:, 4 * half:4 * half + 4, 0:2 * CAP],
                      PS[:, b, :].rearrange("p (a b) -> p a b", a=4)[:, :, 0:2 * CAP], b, t)
            pe.wait(t2)
        xr_free[i] = (t,)
        if g + 2 < 16:
            load_x(g + 2)
        for x in range(2):
            e = 2 * g + x
            ids = experts[e]
            for y in ids:
                pe.wait(use(y))
            w = (pos(ids[0], 8), pos(ids[1], 8), pos(ids[2], 4))
            t = expert((pe, ac, dv, po), w, CAP * e, XET[i], CAP * x, x, free, s_y)
            for y in ids:
                release(y, t)
            if x == 1:
                xt_free[i] = (t,)
    barrier(s_y[0].now(), s_y[1].now())

    bq = [Queue(new_sem("b_" + n)) for n in ("pe", "act", "dve", "sp")]
    bsem = [Slot(new_sem(f"bw{i}")) for i in range(4)]
    bys = [Slot(new_sem(f"by{i}")) for i in range(2)]
    bfree = {k: [None, None] for k in free}
    WX = [at3(o_ut2, 8, 512), at3(o_utok, 8, 512), at3(o_w2x, 4, 1024)]
    bpe, bac, bdv, bsp = bq

    def load_block(i):
        def emit(eng):
            e = eng.value_load(XE[0:1, i:i + 1].bitcast(mybir.dt.int32), min_val=0, max_val=31)
            for j, name in enumerate(("w1", "w3", "w2")):
                src = A[name][bass.ds(e, 1)].rearrange("o (k p) n -> p (o k) n", p=128)
                eng.dma_start(out=WX[j], in_=src).then_inc(bsem[j].sem, 16)
        return emit

    for i in range(NX):
        if i:
            bsp.wait(t_w)
        bsp.items.append(("call", load_block(i)))
        for s in bsem[:3]:
            s.n += 16
        r0 = (32 + i) * CAP
        t = bsp.dma(sy.dma_start, XR[0][0:CAP, :], xb[r0:r0 + CAP, :], bsem[3])
        bpe.wait(t)
        for b in range(2):
            if bfree["h"][0]:
                bpe.wait(*bfree["h"][0])
            for k in range(4):
                kk = 4 * b + k
                t = bpe.run(te.transpose, PS[:, b, 128 * k:128 * k + CAP], XR[0][0:CAP, 128 * kk:128 * kk + 128],
                            CST[0:CAP, C_ID:C_ID + CAP], mark=k == 3)
            bdv.wait(t)
            t = bdv.run(ve.tensor_copy, XET[0][:, 4 * b:4 * b + 4, 0:CAP],
                        PS[:, b, :].rearrange("p (a b) -> p a b", a=4)[:, :, 0:CAP])
            bpe.wait(t)
        for s in bsem[:3]:
            bpe.wait(s.now())
        t_w = expert((bpe, bac, bdv, bsp), WX, r0, XET[0], 0, 0, bfree, bys)
    for q in bq:
        q.wait(*[x.now() for x in bq[:3]], bys[0].now())

    def guard(queue):
        def emit(eng):
            v = eng.value_load(FLAG[0:1, :].bitcast(mybir.dt.int32), min_val=0, max_val=64)
            with eng.If(v > 0):
                queue.flush(eng)
        return emit

    bpo = Queue(new_sem("b_pool"))
    bpo.wait(*[x.now() for x in bq[:3]], bys[0].now())
    for q, x in zip((pe, ac, dv, sp, po), bq + [bpo]):
        q.items.append(("call", guard(x)))

    key4 = [(i, i * RING) for i in range(4)]
    PW = [piece(A["win2"][i], 4096, key4[i % 2]) for i in range(4)]
    PW.append(piece(A["win2s"], 2048, key4[0]))
    PQ = [piece(A["wout2"][i], 4096, key4[(1 + i) % 2]) for i in range(2)]
    PK = [piece(A["wq"][i], 4096, key4[(1, 2, 3, 0)[i]]) for i in range(4)]
    state[key4[2]] = state[key4[3]] = None
    load_ready()

    GG = [at3(o_ut2 + 4096 * i, 4, 1024) for i in range(2)]
    s_g = [slot(f"g{i}") for i in range(4)]
    for n in range(4):
        for i in range(2):
            t = gather(n, i)
        dv.wait(t)
        d(ve.tensor_scalar, GG[0][:, n, :], GG[0][:, n, :], GATE[:, n, 0:1], None, ALU.mult)
        t = d(ve.scalar_tensor_tensor, GG[0][:, n, :], GG[1][:, n, :], GATE[:, n, 1:2], GG[0][:, n, :], ALU.mult, ALU.add)
        pe.wait(t)
        for k in range(8):
            t = turn(PS[:, k, 128 * n:128 * n + 128], GG[0][:, n, 128 * k:128 * k + 128], mark=k == 7)
    dv.wait(t)
    for k in range(8):
        t = dv.run(ve.tensor_tensor, XT[:, k, META:TK], XT[:, k, META:TK], PS[:, k, :], ALU.add)
        bank_free[k] = (t,)
    barrier()

    X = XT[:, :, META:TK]
    o = O_TEMP
    HNR = [alias(o + 2048 * i, 2048) for i in range(4)]; o += 16 * T
    HNF = at3(o, 8, T)
    UC = at3(o, 4, 514); o += 2056
    YC = at3(o, 4, T); o += 2048
    Q2 = at3(o, 4, T); o += 2048
    K2 = at(o, T); o += T
    V2 = at3(o, 4, 128); o += 512
    BI = at3(o, 8, 256); o += 2048
    BIR = BI
    o_cb = o; o += 2048
    YT2 = at3(o, 4, T); o += 2048
    assert o <= O_XT, o
    o = OW
    S8 = at3(o, 8, 256); o += 2048
    PT2 = [[at(o + 1024 * kc + 512 * g, 512) for g in range(2)] for kc in range(2)]; o += 2048
    SQ2 = at3(o, 2, T); o += 1024
    RN2 = at(o, T); o += 512
    ST = at(o, 40); o += 40
    assert o == OW + 5672
    o += 136
    assert o <= ARENA
    RSC = AR[0:8, o_cb:o_cb + 384]

    rs = nc.dram_tensor("rs", [8, 384], F32, kind="Internal").ap()
    s_b = slot("bias")
    t = mm(PS[0:8, 7, 0:128], RB8[0:32, :], HOT[0:32, :], True, True, mark=True)
    dv.wait(t)
    d(ve.memset, RSC, -1.0e30)
    t = d(ve.tensor_copy, RSC[:, 127:255], PS[0:8, 7, 0:128])
    bank_free[7] = (t,)
    sp.wait(t)
    t = sp.dma(sy.dma_start, rs, RSC, s_b)
    sp.wait(t)
    t_bi = toeplitz()

    WSP = [alias(2 * RING + 2048 * i, 2048) for i in range(4)]
    wseq = [(p, c, i == (1 if p == PW[4] else 3)) for p in PW + PQ for i, c in enumerate(range(0, 256 if p == PW[4] else 512, 128))]
    project, _, _ = projector(WSP, wseq)

    t = norm(XT, META, T, X, V_FIN, SQ2, RN2, 0)
    d(ve.tensor_scalar, S1, MOD[:, 8:16], 1.0, None, ALU.add)
    d(ve.tensor_tensor, S1, S1, VEC[:, V_N1:V_N1 + 8], ALU.mult)
    d(ve.tensor_scalar, S2, MOD[:, 32:40], 1.0, None, ALU.add)
    t = d(ve.tensor_tensor, S2, S2, VEC[:, V_N2:V_N2 + 8], ALU.mult)
    for q in engines:
        q.wait(t)

    def shifted_norm(U, g, shift):
        t = norm(XT, META, T, U, None, SQ2, RN2, 0, cols=g)
        marks = []
        for k in range(8):
            ac.wait((t[0], t[1] - 7 + k))
            marks.append(ac.run(se.activation, U[:, k, :], U[:, k, :], ACT.Identity, bias=MOD[:, shift + k:shift + k + 1]))
        return marks

    for b in range(8):
        bank_free[b] = (dv.now(),)
    t_hn = shifted_norm(HNF, S1, 0)
    t = t_hn[7]
    ready = []
    for k in range(4):
        ready.append(to_parts(HNR[k], HNF[:, 2 * k:2 * k + 2, :], 2, T, [t_hn[2 * k + 1]]))

    dv.wait(t)
    t = d(ve.memset, UC[:, :, 0:2], 0.0)
    for j in range(4):
        t = project(HNR, ready, j)
        t = evac(ac, UC[:, j, 2:514], PS[:, j, :], j, t)
        bank_free[j] = (t,)
    for j in range(4):
        b = 4 + j
        t = project(HNR, ready, b)
        dv.wait(t, bank_free[j][0])
        t = dv.run(ve.tensor_tensor, UC[:, j, 2:514], UC[:, j, 2:514], PS[:, b, :], ALU.mult)
        bank_free[b] = (t,)
    for j in range(4):
        tb = project(HNR, ready, j)
        wc = [VEC[:, V_CONV + 4 * i + j:V_CONV + 4 * i + j + 1] for i in range(3)]
        d(ve.tensor_scalar, YC[:, j, :], UC[:, j, 0:T], wc[0], None, ALU.mult)
        for i in (1, 2):
            d(ve.scalar_tensor_tensor, YC[:, j, :], UC[:, j, i:T + i], wc[i], YC[:, j, :], ALU.mult, ALU.add)
        dv.wait(tb)
        t = d(ve.tensor_tensor, YC[:, j, :], YC[:, j, :], PS[:, j, :], ALU.mult)
        bank_free[j] = (t,)
    BLK = CST[:, C_BLK:C_BLK + 128]
    sqf = [None, None]
    seq = [0]

    def group_norm(x, out, gcol, scale=1.0, in_loop=False):
        i = seq[0] % 2
        b = (6 + i) if not in_loop else 6
        seq[0] += 1
        if sqf[i] is not None:
            ac.wait(*sqf[i])
        ac.wait(dv.now())
        t = ac.run(se.activation, SQ2[:, i, :], x, ACT.Square)
        pe.wait(t)
        claim(b)
        t = mm(PS[:, b, :], BLK, SQ2[:, i, :], True, True, mark=True)
        dv.wait(t)
        t = dv.run(ve.tensor_scalar, SQ2[:, i, :], PS[:, b, :], 1.0, EPS, ALU.mult, ALU.add)
        bank_free[b] = (t,)
        ac.wait(t)
        t = ac.run(se.activation, SQ2[:, i, :], SQ2[:, i, :], ACT.Sqrt, scale=1.0)
        dv.wait(t)
        d(ve.reciprocal, SQ2[:, i, :], SQ2[:, i, :])
        if scale != 1.0:
            d(ve.tensor_scalar, SQ2[:, i, :], SQ2[:, i, :], scale, None, ALU.mult)
        t = d(ve.scalar_tensor_tensor, out, x, VEC[:, gcol:gcol + 1], SQ2[:, i, :], ALU.mult, ALU.mult)
        sqf[i] = (t,)
        return t

    def group_norms(items, squares, banks):
        n = range(len(items))
        ac.wait(dv.now())
        ts = [ac.run(se.activation, squares[i], items[i][0], ACT.Square) for i in n]
        yield
        for i in n:
            pe.wait(ts[i])
            claim(banks[i])
            ts[i] = mm(PS[:, banks[i], :], BLK, squares[i], True, True, mark=True)
        yield
        for i in n:
            dv.wait(ts[i])
            ts[i] = dv.run(ve.tensor_scalar, squares[i], PS[:, banks[i], :], 1.0, EPS, ALU.mult, ALU.add)
            bank_free[banks[i]] = (ts[i],)
        for i in n:
            ac.wait(ts[i])
            ts[i] = ac.run(se.activation, squares[i], squares[i], ACT.Sqrt, scale=items[i][3] ** -2)
        for i in n:
            dv.wait(ts[i])
            ts[i] = dv.run(ve.reciprocal, squares[i], squares[i])
        for i in n:
            x, out, g, _ = items[i]
            dv.wait(ts[i])
            ts[i] = dv.run(ve.scalar_tensor_tensor, out, x, VEC[:, g:g + 1], squares[i], ALU.mult, ALU.mult)
        marks.extend(ts)
        yield

    marks = []
    SQ4 = [at(OW + 512 * i, 512) for i in range(4)]
    for j in range(4):
        t = project(HNR, ready, j)
        t = evac(dv, Q2[:, j, :], PS[:, j, :], j, t)
        bank_free[j] = (t,)
    qn = group_norms([(Q2[:, j, :], Q2[:, j, :], V_QG, 0.125) for j in range(4)], SQ4, range(4))
    next(qn)
    t = project(HNR, ready, 4)
    next(qn)
    next(qn)
    t = evac(ac, K2, PS[:, 4, :], 4, t)
    bank_free[4] = (t,)
    ac.wait(t)
    kn = group_norms([(K2, K2, V_KG, 1.0)], [SQ2[:, 1, :]], (4,))
    next(kn)
    t = project(HNR, ready, 5)
    next(kn)
    next(kn)
    t = evac(ac, SQ2[:, 0, :], PS[:, 5, :], 5, t)
    pe.wait(t)
    for n in range(4):
        t = turn(PS[:, 5, 128 * n:128 * n + 128], SQ2[:, 0, 128 * n:128 * n + 128], mark=n == 3)
    t = evac(dv, V2, PS[:, 5, :].rearrange("p (a b) -> p a b", a=4), 5, t)
    bank_free[5] = (t,)
    pe.wait(t)
    dv.wait(t_bi)
    S8S = [S8, at3(o_cb, 8, 256)]
    STS = [ST, at(OW + 5808, 32)]
    s8_free = [None, None]
    pt_free2 = None

    def weights(n):
        S8, ST = S8S[n % 2], STS[n % 2]
        kc0 = 0 if n else 1
        nk = 128 * (2 - kc0)
        claim(0, 1, 2, 3)
        for h in range(8):
            j, g = h % 4, h // 4
            t = mm(PS[:, h // 2, 256 * (h % 2) + 128 * kc0:256 * (h % 2) + 256], Q2[64 * g:64 * g + 64, j, 128 * n:128 * n + 128],
                   K2[64 * g:64 * g + 64, 128 * n + 128 - nk:128 * n + 128], True, True, mark=True)
            if h in (3, 7):
                pe.wait(t)
        sc = S8[:, :, 128 * kc0:256]
        if s8_free[n % 2] is not None:
            dv.wait(s8_free[n % 2])
        dv.wait(t)
        ps = PS[:, 0:4, :].rearrange("p b (a c) -> p (b a) c", a=2)[:, :, 128 * kc0:256]
        t = d(ve.tensor_tensor, sc, ps, BIR[:, :, 0:nk][:, :, ::-1], ALU.add)
        for b in range(4):
            bank_free[b] = (t,)
        d(ve.tensor_reduce, ST[:, 0:8], sc, AX, ALU.max)
        d(ve.tensor_tensor, ST[:, 0:8], ST[:, 0:8], SNK, ALU.max)
        d(ve.tensor_tensor, ST[:, 8:16], SNK, ST[:, 0:8], ALU.subtract)
        t = d(ve.tensor_scalar, ST[:, 0:8], ST[:, 0:8], -1.0, None, ALU.mult)
        yield
        ac.wait(t)
        ac.run(se.activation, ST[:, 16:24], ST[:, 8:16], ACT.Exp)
        for h in range(8):
            t = ac.run(se.activation, S8[:, h, 128 * kc0:256], S8[:, h, 128 * kc0:256], ACT.Exp, bias=ST[:, h:h + 1],
                       accum_out=ST[:, 24 + h:25 + h])
        yield
        dv.wait(t)
        d(ve.tensor_tensor, ST[:, 24:32], ST[:, 24:32], ST[:, 16:24], ALU.add)
        d(ve.reciprocal, ST[:, 24:32], ST[:, 24:32])
        t = d(ve.tensor_tensor, sc, sc, ST[:, 24:32].unsqueeze(2).to_broadcast([128, 8, nk]), ALU.mult)
        w_made[n] = t
        yield

    w_made = {}
    for _ in weights(0):
        pass
    for n in range(4):
        kc0 = 0 if n else 1
        S8 = S8S[n % 2]
        following = weights(n + 1) if n < 3 else iter(())
        next(following, None)
        pe.wait(w_made[n])
        for kc in range(kc0, 2):
            for g in range(2):
                b = 4 + g
                claim(b)
                for j in range(4):
                    t = turn(PS[:, b, 128 * j:128 * j + 128], S8[:, 4 * g + j, 128 * kc:128 * kc + 128], mark=j == 3)
                s8_free[n % 2] = t
                q = (ac, dv)[g]
                if pt_free2 is not None:
                    q.wait(pt_free2)
                t = evac(q, PT2[kc][g], PS[:, b, :], b, t)
                bank_free[b] = (t,)
        made = (ac.now(), dv.now())
        next(following, None)
        group_norm(YC[:, n, :], YC[:, n, :], V_CG + n, in_loop=True)
        next(following, None)
        pe.wait(*made)
        claim(7)
        for g in range(2):
            for kc in range(kc0, 2):
                t = mm(PS[64 * g:64 * g + 64, 7, :], V2[:, n - 1 + kc, 64 * g:64 * g + 64], PT2[kc][g], kc == kc0, kc == 1,
                       mark=True)
        pt_free2 = t
        t = evac(ac, YT2[:, :, 128 * n:128 * n + 128], PS[:, 7, :].rearrange("p (a b) -> p a b", a=4), 7, t)
        bank_free[7] = (t,)
    dv.wait(t)
    ac.wait(t)
    ac.wait(t)
    dv.wait(t)
    for j in range(2):
        to_parts(HNR[j], YC[:, 2 * j:2 * j + 2, :], 2, T, [t, dv.now()])
    ac.wait(pe.now())
    marks = []
    for _ in group_norms([(YT2[:, j, :], YT2[:, j, :], V_AG + j, 1.0) for j in range(4)], SQ4, range(4)):
        pass
    for j in range(2):
        t = to_parts(HNR[2 + j], YT2[:, 2 * j:2 * j + 2, :], 2, T, marks[2 * j:2 * j + 2])
    pe.wait(t)
    for i in range(8):
        b = i % 6
        t = project(HNR, ready, b)
        dv.wait(t)
        t = dv.run(ve.scalar_tensor_tensor, X[:, i, :], PS[:, b, :], MOD[:, 16 + i:17 + i], X[:, i, :], ALU.mult, ALU.add)
        bank_free[b] = (t,)
    barrier()

    H2 = at3(OW, 8, T)
    state[key4[2]] = state[key4[3]] = [q.now() for q in engines]
    load_ready()
    s_k = slot("keys")
    KEYS = at3(O_TEMP + 1536, 16, 128)
    t_keys = sp.dma(sy.dma_start, KEYS, A["keysT"], s_k)
    SQ2 = at3(O_TEMP, 2, T)
    RN2 = at(O_TEMP + 1024, T)
    pe.wait(*shifted_norm(H2, S2, 24))
    xs = nc.dram_tensor("xs", [128, 8, 512], F32, kind="Internal").ap()
    hs = nc.dram_tensor("hs", [128, 8, 512], F32, kind="Internal").ap()
    gd = nc.dram_tensor("gd", [4, 128, 128, 128], F32, kind="Internal").ap()
    s_xs = slot("xs")
    sp.wait(dv.now(), ac.now())
    sp.dma(sy.dma_start, xs, X, s_xs)
    t_xs = sp.dma(sy.dma_start, hs, H2, s_xs)
    o = O_TEMP + 1536
    o += 2048
    QP = [at3(o + 2048 * i, 4, T) for i in range(2)]; o += 4096
    SS = [at3(o + 512 * i, 4, 128) for i in range(2)]; o += 1024
    TM = at3(o, 4, 128); o += 512
    OG = [0, O_TEMP]
    assert o <= 2 * O_TEMP
    o = 2 * O_TEMP
    SV = at(o, 1024).rearrange("p (n h k) -> p n h k", n=4, h=16); o += 1024
    SI = at(o, 1024).rearrange("p (n h k) -> p n h k", n=4, h=16); o += 1024
    SF = at(o, 1024).rearrange("p (n h k) -> p n h k", n=4, h=16); o += 1024
    CD = [at3(o + 128 * i, 2, 64) for i in range(3)]; o += 384
    EQ = [at(o + 2048 * i, 2048).rearrange("p (h k i) -> p h k i", h=8, k=16) for i in range(2)]; o += 4096
    IT = [at(o + 512 * i, 512) for i in range(3)]; o += 1536
    TV, TI = (at(o + 512 * i, 512).rearrange("p (n h k) -> p n h k", n=4, h=8) for i in range(2)); o += 1024
    PX = at3(o, 8, 16); o += 128
    PI = [at3(o + 128 * i, 8, 16) for i in range(4)]; o += 512
    NB1 = at(o, 512); o += 512
    IAB = [at(o + 128 * i, 128) for i in range(2)]; o += 256
    SMX = at(o, 8); o += 8
    assert o <= O_CST, o
    NB = 4
    AH = [at3(OW + 512 * i, 4, 128) for i in range(NB)]
    BH = [at3(OW + 512 * (NB + i), 4, 128) for i in range(NB)]

    def each(method, args):
        dv.wait(dv.now())
        for a in args:
            t = dv.run(method, *a)
        return t

    def top16(srcs, tmps, vs, idxs):
        n = range(len(srcs))
        each(ve.max, [(vs[i][:, 0:8], srcs[i]) for i in n])
        each(ve.max_index, [(idxs[i][:, 0:8].bitcast(U32), vs[i][:, 0:8], srcs[i]) for i in n])
        each(ve.match_replace, [(tmps[i], vs[i][:, 0:8], srcs[i], -3.0e38) for i in n])
        each(ve.max, [(vs[i][:, 8:16], tmps[i]) for i in n])
        each(ve.max_index, [(idxs[i][:, 8:16].bitcast(U32), vs[i][:, 8:16], tmps[i]) for i in n])

    def sums(i, n):
        v = SV[:, n, 4 * i:4 * i + 4, :].rearrange("p (h s) k -> p h s k", s=2)
        va, vb = v[:, :, 0, :], v[:, :, 1, :]
        u = CD[2]
        args = [(u[:, :, 0:16], va[:, :, 0:1].to_broadcast([128, 2, 16]), vb, ALU.add)]
        for a0, a1, w, c in ((1, 4, 8, 16), (4, 8, 4, 40)):
            m = a1 - a0
            args.append((u[:, :, c:c + m * w].rearrange("p h (a b) -> p h a b", a=m),
                         va[:, :, a0:a1].unsqueeze(3).to_broadcast([128, 2, m, w]),
                         vb[:, :, 0:w].unsqueeze(2).to_broadcast([128, 2, m, w]), ALU.add))
        args.append((u[:, :, 56:64], va[:, :, 8:16], vb[:, :, 0:1].to_broadcast([128, 2, 8]), ALU.add))
        each(ve.tensor_tensor, args)
        return ([u[:, x, :] for x in range(2)], [CD[0][:, x, :] for x in range(2)], [TV[:, n, 2 * i + x, :] for x in range(2)],
                [TI[:, n, 2 * i + x, :] for x in range(2)])

    dv.wait(t_xs)
    last = None
    qp_free = [None, None]
    ss_free = [None, None]
    c = 0
    for i in range(4):
        pe.wait(use(PK[i]))
        for f in range(4):
            claim(f)
            t = proj(pos(PK[i], 8), 128 * f, 128, f, 0, XONLY, X=H2)
            if qp_free[i % 2] is not None:
                ac.wait(qp_free[i % 2])
            t = evac(ac, QP[i % 2][:, f, :], PS[:, f, :], f, t)
            bank_free[f] = (t,)
        release(PK[i], pe.now())
        pe.wait(t, t_keys)
        for n in range(4):
            b = 4 + n
            claim(b)
            for f in range(4):
                t = mm(PS[:, b, 128 * f:128 * f + 128], QP[i % 2][:, f, 128 * n:128 * n + 128], KEYS[:, 4 * i + f, :], True, True,
                       mark=True)
            qp_free[i % 2] = t
            s = SS[c % 2]
            if ss_free[c % 2] is not None:
                ac.wait(ss_free[c % 2])
            t = evac(ac, s, PS[:, b, :].rearrange("p (a b) -> p a b", a=4), b, t)
            bank_free[b] = (t,)
            dv.wait(t)
            cands = sums(*last) if last else ([], [], [], [])
            mine = ([s[:, f, :] for f in range(4)], [TM[:, f, :] for f in range(4)],
                    [SV[:, n, 4 * i + f, :] for f in range(4)], [SI[:, n, 4 * i + f, :] for f in range(4)])
            top16(*[x + y for x, y in zip(mine, cands)])
            last = (i, n)
            ss_free[c % 2] = dv.now()
            c += 1
    top16(*sums(*last))
    d(ve.tensor_copy, SF, SI.bitcast(U32))
    barrier(t_xs)

    io16 = IO[:, 0:16].unsqueeze(1).unsqueeze(1).to_broadcast([128, 8, 16, 16])
    it_made = [None] * 4
    t_m = [None, None]

    def choice(n):
        ti = TI[:, n].bitcast(U32)
        t = d(ve.tensor_tensor, PX, TV[:, n], TV[:, n, :, 0:1].to_broadcast([128, 8, 16]), ALU.subtract)
        ac.wait(t)
        t_e = ac.run(se.activation, PX, PX, ACT.Exp)
        each(ve.tensor_scalar, [(PI[3].bitcast(U32), ti, 3, None, ALU.logical_shift_right),
                                (PI[1].bitcast(U32), ti, 2, None, ALU.logical_shift_right)])
        yield
        each(ve.tensor_copy, [(PI[0], PI[3].bitcast(U32)), (PI[1], PI[1].bitcast(U32)), (PI[2], ti)])
        yield
        d(ve.tensor_scalar, PI[0], PI[0], -1.0, 0.0, ALU.add, ALU.max)
        d(ve.scalar_tensor_tensor, PI[0], PI[1], -6.0, PI[0], ALU.add, ALU.max)
        yield
        d(ve.scalar_tensor_tensor, PI[0], PI[2], -48.0, PI[0], ALU.add, ALU.max)
        each(ve.tensor_scalar, [(PI[1], PI[0], 8.0, 8.0, ALU.mult, ALU.add), (PI[3], PI[0], 4.0, 24.0, ALU.mult, ALU.add)])
        yield
        d(ve.scalar_tensor_tensor, PI[1], PI[0], 16.0, PI[1], ALU.mult, ALU.min)
        d(ve.scalar_tensor_tensor, PI[3], PI[0], 48.0, PI[3], ALU.add, ALU.min)
        yield
        d(ve.tensor_tensor, PI[1], PI[1], PI[3], ALU.min)
        d(ve.tensor_tensor, PI[1], PI[2], PI[1], ALU.subtract)
        yield
        dv.wait(t_e)
        d(ve.tensor_reduce, SMX, PX, AX, ALU.add)
        d(ve.reciprocal, SMX, SMX)
        yield
        d(ve.tensor_tensor, PX, PX, SMX.unsqueeze(2).to_broadcast([128, 8, 16]), ALU.mult)
        yield
        for s in range(2):
            t = d(ve.tensor_tensor, EQ[s], io16, PI[s].unsqueeze(3).to_broadcast([128, 8, 16, 16]), ALU.is_equal)
            sf = SF[:, n].rearrange("p (h s) k -> p h s k", s=2)[:, :, s, :].unsqueeze(2).to_broadcast([128, 8, 16, 16])
            po.wait(t)
            t_m[s] = po.run(ge.tensor_tensor, EQ[s], EQ[s], sf, ALU.mult)
            yield
        for s in range(4):
            yield
        for s in range(2):
            dv.wait(t_m[s])
            t = d(ve.tensor_reduce, IAB[s].rearrange("p (h k) -> p h k", h=8), EQ[s], AX, ALU.add)
            yield
        pe.wait(t)
        claim(7)
        for s in range(3):
            src = IAB[s] if s < 2 else PX.rearrange("p h k -> p (h k)")
            t = turn(PS[:, 7, 128 * s:128 * s + 128], src, mark=s == 2)
        yield
        dv.wait(t)
        for s in range(3):
            t = dv.run(ve.tensor_copy, IT[s][:, 128 * n:128 * n + 128], PS[:, 7, 128 * s:128 * s + 128])
        t2 = d(ve.tensor_scalar, NB1[:, 128 * n:128 * n + 128], PS[:, 7, 128:256], -1.0, None, ALU.mult)
        bank_free[7] = (t2,)
        it_made[n] = t2
        yield

    HSR = [alias(8192 + 2048 * i, 2048) for i in range(4)]
    SPL = [alias(16384 + 2048 * i, 2048) for i in range(6)]
    GGR = [alias(32768 + 2048 * i, 2048) for i in range(2)] + [alias(28672 + 2048 * i, 2048) for i in range(2)]
    GE = [at(OW + 512 * i, 512) for i in range(4)]
    raw_key = [(i, 2048 * i) for i in range(4)]
    g_key = [(4 + i, 36864 + 1024 * i) for i in range(4)]
    for k4 in raw_key + g_key:
        state[k4] = None
    units = []
    GPC = {}
    g_out = [None, None]
    c = 0
    for g in range(16):
        for i in range(4):
            p = piece(A["uT"][4 * g + i], 2048, raw_key[c % 4]); c += 1
            units += [("u", g, 2 * i, p, 0), ("u", g, 2 * i + 1, p, 1)]
            if i % 2:
                for y in (i - 1, i):
                    GPC[4 * g + y] = piece(gd[:, :, 8 * g + 2 * y:8 * g + 2 * y + 2, :].rearrange("n b a t -> b n (a t)"), 1024,
                                           g_key[y])
        for hf in range(2):
            for i in range(2):
                p = piece(A["v"][2 * (2 * g + hf) + i], 2048, raw_key[c % 4]); c += 1
                units += [("v", 2 * g + hf, 4 * i, p, 0), ("v", 2 * g + hf, 4 * i + 2, p, 1)]
    H2R = at3(4096, 8, T)

    s_gd = [[slot(f"gd{i}{j}") for j in range(4)] for i in range(2)]
    h_free = [None] * NB
    LEAD = 3
    ready = {}

    def one_hots(q4):
        i, t0, n = q4 % NB, 4 * q4, q4 // 32
        for q in (dv, po, ac):
            q.wait(it_made[n])
            if h_free[i] is not None:
                q.wait(h_free[i])
        on_ac = 2 if n < 3 else 1
        for x in range(4 - on_ac, 4):
            tc = ac.run(se.activation, BH[i][:, x, :], IO, ACT.Abs, bias=NB1[:, t0 + x:t0 + x + 1])
        ac.wait(tc)
        tc = ac.run(se.activation, BH[i][:, 4 - on_ac:4, :], BH[i][:, 4 - on_ac:4, :], ACT.Relu, scale=-1.0, bias=1.0)
        for x in range(4):
            if x < 2:
                tb = po.run(ge.tensor_scalar, BH[i][:, x, :], IO, IT[1][:, t0 + x:t0 + x + 1], None, ALU.is_equal)
            elif x < 4 - on_ac:
                ta = dv.run(ve.tensor_scalar, BH[i][:, x, :], IO, IT[1][:, t0 + x:t0 + x + 1], None, ALU.is_equal)
            ta = dv.run(ve.tensor_scalar, AH[i][:, x, :], IO, IT[0][:, t0 + x:t0 + x + 1], IT[2][:, t0 + x:t0 + x + 1],
                        ALU.is_equal, ALU.mult)
        ready[q4] = (ta, tb, tc)

    for _ in choice(0):
        pass
    for q4 in range(LEAD):
        one_hots(q4)
    for n in range(4):
        following = choice(n + 1) if n < 3 else iter(())
        GT = AR[:, OG[n % 2]:OG[n % 2] + 16384].rearrange("p (a t) -> p a t", a=128)
        for x4 in range(32):
            q4 = 32 * n + x4
            i = q4 % NB
            if x4 == 32 - LEAD:
                for _ in following:
                    pass
            if q4 + LEAD < 128:
                one_hots(q4 + LEAD)
            if x4 == 0 and g_out[n % 2] is not None:
                ac.wait(*g_out[n % 2])
            pe.wait(*ready[q4])
            b = q4 % 7
            claim(b)
            for x in range(4):
                t = mm(PS[:, b, 128 * x:128 * x + 128], BH[i][:, x, :], AH[i][:, x, :], True, True, mark=x == 3)
            h_free[i] = t
            t = evac(ac, GT[:, :, 4 * x4:4 * x4 + 4], PS[:, b, :].rearrange("p (x a) -> p a x", x=4), b, t)
            bank_free[b] = (t,)
            next(following, None)
            if n == 3 and x4 == 24:
                ac.wait(t_h)
                dv.wait(t_h)
                for y in range(4):
                    hv = HSR[y][:, :].rearrange("p (s k t) -> p s k t", s=2, k=2)
                    t2 = ac.run(se.activation, hv[:, 0], H2R[:, 2 * y:2 * y + 2, :], ACT.Copy)
                    dv.wait(t2)
                    t_hs = dv.run(ve.tensor_tensor, hv[:, 1], H2R[:, 2 * y:2 * y + 2, :], hv[:, 0].bitcast(F32), ALU.subtract)
        sp.wait(t)

        def write(q):
            return sp.dma(sy.dma_start, gd[n][:, 32 * q:32 * q + 32, :], GT[:, 32 * q:32 * q + 32, :], s_gd[n % 2][q])

        if n < 3:
            g_out[n % 2] = [write(q) for q in range(4)]
        if n == 2:
            sp.wait(*g_out[0])
            t_h = sp.dma(sy.dma_start, H2R, hs, s_xs)
            state[raw_key[0]] = state[raw_key[1]] = g_out[0]
            load_ready()
    sp.wait(*[q.now() for q in engines])
    g_out[1] = [write(0)]
    for y in range(2):
        needs[GPC[y]] = [g_out[0][0], g_out[1][0]]
    state[g_key[0]] = g_out[0]
    load_ready()
    g_out[1].append(write(1))
    state[g_key[1]] = g_out[0]
    state[raw_key[2]] = state[raw_key[3]] = [t_hs]
    load_ready()
    g_out[1] += [write(2), write(3)]
    for y in range(2, 64):
        needs[GPC[y]] = [x[y // 16] for x in g_out]
    t_x = sp.dma(sy.dma_start, X, xs, s_xs)
    state[g_key[2]] = state[g_key[3]] = g_out[0]
    load_ready()
    pe.wait(t_hs)

    split_made = {}
    pe_done = {}

    def split(j):
        _, _, _, p, h = units[j]
        raw = at(pieces[p][2][1] + 1024 * h, 1024)
        s = SPL[j % 6]
        if j >= 6:
            ac.wait(pe_done[j - 6])
        else:
            ac.wait(*g_out[1][0:j // 2 + 1])
        ac.wait(use(p))
        t = ac.run(se.activation, s[:, 0:1024], raw, ACT.Copy)
        dv.wait(t)
        t = dv.run(ve.tensor_tensor, s[:, 1024:2048], raw, s[:, 0:1024].bitcast(F32), ALU.subtract)
        split_made[j] = t
        if h == 1:
            release(p, t)

    ge_free = [None] * 4
    gg_made = [None] * 8
    gg_read = [None] * 8
    AHEAD = 4

    def experts(j):
        _, g, a, p, h = units[j]
        b = 4 * (g % 2) + a % 4
        pe.wait(split_made[j])
        claim(b)
        w = SPL[j % 6][:, :].rearrange("p (s k b) -> p s k b", s=2, k=8)
        for k in range(8):
            hv = HSR[k // 2][:, :].rearrange("p (s k t) -> p s k t", s=2, k=2)[:, :, k % 2, :]
            for i, (x, y) in enumerate(((0, 0), (0, 1), (1, 0))):
                t = mm(PS[:, b, :], w[:, x, k, :], hv[:, y, :], k == 0 and i == 0, k == 7 and i == 2, mark=k == 7 and i == 2)
        pe_done[j] = t
        e = GE[a % 4]
        ac.wait(t)
        if ge_free[a % 4] is not None:
            ac.wait(ge_free[a % 4])
        t = ac.run(se.activation, e, PS[:, b, :], ACT.Gelu_apprx_tanh)
        bank_free[b] = (t,)
        gp = GPC[4 * g + a // 2]
        dv.wait(t, use(gp))
        gates = pos(gp, 4)[:, :, 128 * (a % 2):128 * (a % 2) + 128]
        t = dv.run(ve.tensor_tensor, e.rearrange("p (n t) -> p n t", n=4), e.rearrange("p (n t) -> p n t", n=4), gates, ALU.mult)
        if a % 2:
            release(gp, t)
        ac.wait(t)
        if g == 0:
            ac.wait(g_out[1][3 if a > 3 else 0])
        if gg_read[a] is not None:
            ac.wait(gg_read[a])
        gg = GGR[a // 2][:, :].rearrange("p (s a t) -> p s a t", s=2, a=2)[:, :, a % 2, :]
        t = ac.run(se.activation, gg[:, 0, :], e, ACT.Copy)
        dv.wait(t)
        t = dv.run(ve.tensor_tensor, gg[:, 1, :], e, gg[:, 0, :].bitcast(F32), ALU.subtract)
        ge_free[a % 4] = t
        gg_made[a] = t

    def products(j):
        _, gh, a0, p, h = units[j]
        g, hf = gh // 2, gh % 2
        b0 = 4 * ((g + 1 + hf) % 2)
        pe.wait(split_made[j], gg_made[a0], gg_made[a0 + 1])
        if a0 == 0:
            claim(b0, b0 + 1, b0 + 2, b0 + 3)
        w = SPL[j % 6][:, :].rearrange("p (s a d) -> p s a d", s=2, a=2)
        for x in range(2):
            gg = GGR[a0 // 2][:, :].rearrange("p (s a t) -> p s a t", s=2, a=2)[:, :, x, :]
            for k in range(4):
                for i, (y, z) in enumerate(((0, 0), (0, 1), (1, 0))):
                    last = a0 == 6 and x == 1 and i == 2
                    t = mm(PS[:, b0 + k, :], w[:, y, x, 128 * k:128 * k + 128], gg[:, z, :], a0 == 0 and x == 0 and i == 0, last,
                           mark=last or (x == 1 and k == 3 and i == 2))
                if last:
                    dv.wait(t)
                    kk = 4 * hf + k
                    bank_free[b0 + k] = (dv.run(ve.scalar_tensor_tensor, X[:, kk, :], PS[:, b0 + k, :], MOD[:, 40 + kk:41 + kk],
                                                X[:, kk, :], ALU.mult, ALU.add),)
            if hf == 1:
                gg_read[a0 + x] = pe.now()
        pe_done[j] = t

    for j in range(AHEAD):
        split(j)
    dv_x = False
    s_out = slot("out")
    for j in range(len(units)):
        if j + AHEAD < len(units):
            split(j + AHEAD)
        if units[j][0] == "u":
            experts(j)
        else:
            if not dv_x:
                dv.wait(t_x)
                dv_x = True
            products(j)
            if units[j][1:3] in ((30, 6), (31, 6)):
                h0 = 4 * (units[j][1] - 30)
                sp.wait(dv.now())
                t_o = sp.dma(sy.dma_start, A["out"].rearrange("(k p) t -> p k t", p=128)[:, h0:h0 + 4, :], X[:, h0:h0 + 4, :], s_out)
    sp.wait(t_o)
    block = ctx.enter_context(nc.Block())
    block.sync(sp.flush)
    block.tensor(pe.flush)
    block.scalar(ac.flush)
    block.vector(dv.flush)
    block.gpsimd(po.flush)



def layout(i):
    a = {k: np.asarray(v) for k, v in i.items()}
    f = np.float32
    c = np.ascontiguousarray
    o = {}
    o["xT"] = c(a["x"][0].T)
    o["metaT"] = c(a["meta_tokens"].T)
    w = a["w_in"][0]
    r = np.arange
    hd = lambda base, h: base + 64 * h
    QA, KA, VA, QB, CK, KRP, QI, KI, WI, GA, GB = 0, 512, 1024, 1536, 2048, 2176, 2192, 2704, 2768, 2776, 3800
    def nope(base):
        return np.concatenate([np.concatenate([hd(base, h) + 16 + r(48), hd(base, h) + r(16)]) for h in range(8)])
    sw = np.concatenate([8 + r(8), r(8)])
    def rope(base, step):
        return (np.concatenate([base + step * h + r(16) for h in range(8)]),
                np.concatenate([base + step * h + sw for h in range(8)]))
    rba, rbb = rope(QB, 64)
    kra, krb = rope(KRP, 0)
    ria, rib = rope(QI, 64)
    kin = np.concatenate([KI + 16 + r(48), KI + r(16)] * 2)
    main = np.concatenate([KA + r(512), QA + r(512), VA + r(512), nope(QB), rba, rbb, kra, krb, CK + r(128), kin,
                           ria, rib, nope(QI), GA + r(1024), GB + r(1024)])
    small = np.concatenate([KI + r(16), KI + sw, WI + r(8)])
    def tiles(m, n):
        k, nn = m.shape
        return c(m.reshape(k // 128, 128, nn // n, n).transpose(2, 1, 0, 3).reshape(nn // n, 128, -1))
    o["wp1"] = tiles(w[:, main], 512)
    o["wp1s"] = tiles(w[:, small], 40)[0]
    wk = np.zeros((128, 4, 128), f)
    uk = a["w_uk"][0].transpose(0, 2, 1)
    wk[0:48] = uk[0::2].transpose(1, 0, 2)
    wk[64:112] = uk[1::2].transpose(1, 0, 2)
    o["wukT"] = wk
    o["wuv"] = c(a["w_uv"][0].transpose(1, 0, 2))
    o["wupa"] = c(a["w_up_a"][0].reshape(4, 128, 1024).transpose(1, 0, 2))
    o["wupb"] = c(a["w_up_b"][0].reshape(4, 128, 1024).transpose(1, 0, 2))
    o["wo"] = tiles(a["w_o"][0], 512)
    inv = (f(500000.0) ** (-r(8).astype(f) / f(8))).astype(f)
    ang = r(528).astype(f)[:, None] * inv[None]
    p = r(128)
    o["cos"] = c(np.cos(ang)[:, p % 8].T.astype(f))
    o["sin"] = c((np.sin(ang)[:, p % 8].T * np.where((p // 8) % 2, 1, -1)[:, None]).astype(f))
    q = r(128)
    P_, Q_ = p[:, None], q[None]
    sel = np.zeros((128, 240), f); sel[:, 112:128] = -1
    blk = (P_ // 64 == Q_ // 64) / 64
    cst = [P_ == Q_, np.ones((128, 128)), -np.ones((128, 128)), -(P_ >= Q_).astype(f), P_ < Q_,
           -((P_ // 16 == Q_ // 16) & (P_ >= Q_)).astype(f), sel, P_ // 16 == r(8)[None], blk, Q_ + 0 * P_]
    o["cst"] = c(np.concatenate([x.astype(f) for x in cst], 1))
    col = lambda v: v.reshape(-1, 128).T
    o["vec"] = c(np.concatenate([col(x) for x in (
        a["norm_mix_g"][0], a["norm_ffn_g"][0], a["norm_final_g"], a["norm1_g_2"][0], a["norm2_g_2"][0], a["b_ada_2"][0],
        a["c_2"][0], a["conv_w_2"][0].reshape(-1), a["conv_out_g_2"][0], )], 1).astype(f))
    ag = a["attn_out_g_2"][0].reshape(8, 64)
    ag = np.concatenate([np.concatenate([ag[j], ag[j + 4]])[:, None] for j in range(4)], 1)
    qg = np.tile(a["q_norm_g_2"][0], 2)[:, None]; kg = np.tile(a["k_norm_g_2"][0], 2)[:, None]
    o["vec"] = c(np.concatenate([o["vec"], ag, qg, kg], 1))
    def rep(x): return c(np.broadcast_to(x[None], (128,) + x.shape).astype(f))
    gr = np.concatenate([a["w_group"][0], a["w_router"][0]], 1)
    o["wgr"] = tiles(gr, 36)[0]
    o["bgr"] = rep(np.concatenate([a["b_group"][0], a["b_router"][0]]))
    o["snk"] = rep(a["sinks_2"][0])
    o["wada"] = tiles(a["w_ada_2"][0], 512)
    w2i = a["w_in_2"][0]
    qp = np.concatenate([np.concatenate([1536 + 64 * j + r(64), 1536 + 64 * (j + 4) + r(64)]) for j in range(4)])
    o["win2"] = tiles(w2i[:, np.concatenate([512 + r(512), 1024 + r(512), r(512), qp])], 512)
    o["win2s"] = tiles(w2i[:, 2048:2304], 256)[0]
    rows = np.concatenate([r(512)] + [np.concatenate([512 + 64 * j + r(64), 512 + 64 * (j + 4) + r(64)]) for j in range(4)])
    o["wout2"] = tiles(a["w_out_2"][0][rows], 512)
    o["wq"] = tiles(a["peer_wq_2"][0], 512)
    o["keysT"] = c(a["peer_keys_2"][0].transpose(3, 1, 0, 2).reshape(128, 16, 128))
    o["relb"] = a["rel_bias_2"]
    d = np.maximum(r(128), 1).astype(f)
    big = 16 + (np.log(d / f(16)) / f(np.log(8.0)) * f(16)).astype(np.int32)
    bucket = np.where(r(128) < 16, r(128), np.minimum(big, 31))
    o["hot"] = c((r(32)[:, None] == bucket[None]).astype(f))
    u = a["peer_u_2"][0].reshape(64, 2, 128, 8, 128)
    o["uT"] = c(u.transpose(0, 4, 1, 3, 2).reshape(64, 128, 2048))
    v = a["peer_v_2"][0].reshape(16, 2, 4, 128, 2, 512)
    o["v"] = c(v.transpose(0, 4, 1, 3, 2, 5).reshape(64, 128, 2048))
    o["w1"] = a["w1"][0]; o["w3"] = a["w3"][0]; o["w2"] = a["w2"][0]
    return o


def kernel(**inputs):
    import concourse.bacc as bacc
    from concourse.bass_utils import run_bass_kernel_spmd

    arrays = layout(inputs)
    nc = bacc.Bacc("TRN2", target_bir_lowering=False, num_devices=1)
    args = {}
    for name, a in arrays.items():
        args[name] = nc.dram_tensor(name, a.shape, mybir.dt.from_np(a.dtype), kind="ExternalInput").ap()
    args["out"] = nc.dram_tensor("out", (1024, 512), F32, kind="ExternalOutput").ap()
    program(nc, args)
    r = run_bass_kernel_spmd(nc, [arrays], core_ids=[0])
    return np.ascontiguousarray(r.results[0]["out"].T)[None]
```
